# Optimizing a Trainium2 kernel written in Bass

```python
import math
import jax, jax.numpy as jnp
from jax import lax
import numpy as np

D_MODEL = 1024
BATCH = 1
SEQ = 1024
DEPTH = 2

N_MIXERS = 2
ROPE_THETA = 500000.0
LN_EPS = 1e-5
RMS_EPS = 1e-6

MLA_HEADS = 8
MLA_NOPE = 128
MLA_ROPE = 64
MLA_V = 128
MLA_Q_RANK = 384
MLA_KV_RANK = 256
MLA_QBLOCK = 128

SWA_HEADS = 16
SWA_KV_HEADS = 4
SWA_HEAD_DIM = 64
SWA_WINDOW = 128
SWA_ROT = SWA_HEAD_DIM // 4

D_FF = ((8 * D_MODEL + 3 * 256 - 1) // (3 * 256)) * 256

DEEPNORM_ALPHA = (2 * DEPTH) ** 0.25
DEEPNORM_BETA = (8 * DEPTH) ** -0.25

N_MLA = (DEPTH + 1) // 2
N_SWA = DEPTH // 2

kernel_name = "hybrid_mla_swa_sink_deepnorm_adaln"

def layer_norm(x, g, b):
    xf = x.astype(jnp.float32)
    mu = jnp.mean(xf, -1, keepdims=True)
    var = jnp.mean(jnp.square(xf - mu), -1, keepdims=True)
    return ((xf - mu) * lax.rsqrt(var + LN_EPS) * g + b).astype(x.dtype)

def rms_norm(x, g):
    xf = x.astype(jnp.float32)
    return (xf * lax.rsqrt(jnp.mean(jnp.square(xf), -1, keepdims=True) + RMS_EPS) * g).astype(x.dtype)

def rope_cos_sin(positions, rot_dim):
    inv = ROPE_THETA ** (-jnp.arange(0, rot_dim, 2, dtype=jnp.float32) / rot_dim)
    ang = positions.astype(jnp.float32)[..., None] * inv
    return jnp.cos(ang), jnp.sin(ang)

def apply_rope(x, cos, sin):
    half = x.shape[-1] // 2
    x1, x2 = x[..., :half], x[..., half:]
    c = cos[:, :, None, :]
    s = sin[:, :, None, :]
    return jnp.concatenate([x1 * c - x2 * s, x2 * c + x1 * s], -1).astype(x.dtype)

def mla_mixer(h, cos, sin, w_in, q_norm, w_q_b, kv_norm, w_kv_b, w_o):
    B, S, _ = h.shape
    H = MLA_HEADS
    lat = h @ w_in
    q_lat = lat[..., :MLA_Q_RANK]
    kv_lat = lat[..., MLA_Q_RANK:MLA_Q_RANK + MLA_KV_RANK]
    k_rope = lat[..., MLA_Q_RANK + MLA_KV_RANK:]
    q = (rms_norm(q_lat, q_norm) @ w_q_b).reshape(B, S, H, MLA_NOPE + MLA_ROPE)
    q_nope = q[..., :MLA_NOPE]
    q_rope = apply_rope(q[..., MLA_NOPE:], cos, sin)
    k_rope = apply_rope(k_rope[:, :, None, :], cos, sin)[:, :, 0, :]
    kv = (rms_norm(kv_lat, kv_norm) @ w_kv_b).reshape(B, S, H, MLA_NOPE + MLA_V)
    k_nope = kv[..., :MLA_NOPE]
    v = kv[..., MLA_NOPE:]
    scale = (MLA_NOPE + MLA_ROPE) ** -0.5
    nb = S // MLA_QBLOCK
    qn_b = q_nope.reshape(B, nb, MLA_QBLOCK, H, MLA_NOPE).transpose(1, 0, 2, 3, 4)
    qr_b = q_rope.reshape(B, nb, MLA_QBLOCK, H, MLA_ROPE).transpose(1, 0, 2, 3, 4)
    starts = jnp.arange(nb, dtype=jnp.int32) * MLA_QBLOCK
    k_idx = jnp.arange(S, dtype=jnp.int32)

    def q_block(args):
        qn, qr, start = args
        s = (jnp.einsum('bqhd,bkhd->bhqk', qn, k_nope, preferred_element_type=jnp.float32)
             + jnp.einsum('bqhr,bkr->bhqk', qr, k_rope, preferred_element_type=jnp.float32)) * scale
        q_idx = start + jnp.arange(MLA_QBLOCK, dtype=jnp.int32)
        causal = k_idx[None, :] <= q_idx[:, None]
        s = jnp.where(causal[None, None], s, -jnp.inf)
        p = jax.nn.softmax(s, axis=-1).astype(v.dtype)
        return jnp.einsum('bhqk,bkhd->bqhd', p, v)

    o = lax.map(q_block, (qn_b, qr_b, starts))
    o = o.transpose(1, 0, 2, 3, 4).reshape(B, S, H * MLA_V)
    return o @ w_o

def partial_rope(x, cos, sin):
    return jnp.concatenate([apply_rope(x[..., :SWA_ROT], cos, sin), x[..., SWA_ROT:]], -1)

def swa_mixer(h, cos, sin, w_qkv, b_qkv, sinks, w_o, b_o):
    B, S, _ = h.shape
    HQ, HKV, HD, W = SWA_HEADS, SWA_KV_HEADS, SWA_HEAD_DIM, SWA_WINDOW
    G = HQ // HKV
    qkv = h @ w_qkv + b_qkv
    q = qkv[..., :HQ * HD].reshape(B, S, HQ, HD)
    k = qkv[..., HQ * HD:(HQ + HKV) * HD].reshape(B, S, HKV, HD)
    v = qkv[..., (HQ + HKV) * HD:].reshape(B, S, HKV, HD)
    q = partial_rope(q, cos, sin)
    k = partial_rope(k, cos, sin)
    nb = S // W
    qb = q.reshape(B, nb, W, HKV, G, HD)
    kb = k.reshape(B, nb, W, HKV, HD)
    vb = v.reshape(B, nb, W, HKV, HD)
    kpad = jnp.zeros_like(kb[:, :1])
    vpad = jnp.zeros_like(vb[:, :1])
    k2 = jnp.concatenate([jnp.concatenate([kpad, kb[:, :-1]], 1), kb], axis=2)
    v2 = jnp.concatenate([jnp.concatenate([vpad, vb[:, :-1]], 1), vb], axis=2)
    s = jnp.einsum('bnqhgd,bnkhd->bnhgqk', qb, k2, preferred_element_type=jnp.float32) * (HD ** -0.5)
    q_pos = jnp.arange(W, dtype=jnp.int32)[:, None] + W
    k_pos = jnp.arange(2 * W, dtype=jnp.int32)[None, :]
    rel = q_pos - k_pos
    band = (rel >= 0) & (rel < W)
    has_prev = (jnp.arange(nb)[:, None, None] > 0) | (k_pos[None] >= W)
    mask = band[None] & has_prev
    s = jnp.where(mask[None, :, None, None], s, -jnp.inf)
    sink = jnp.broadcast_to(sinks.astype(jnp.float32).reshape(HKV, G)[None, None, :, :, None, None],
                            s.shape[:-1] + (1,))
    p = jax.nn.softmax(jnp.concatenate([s, sink], -1), axis=-1)[..., :-1]
    o = jnp.einsum('bnhgqk,bnkhd->bnqhgd', p.astype(v.dtype), v2).reshape(B, S, HQ * HD)
    return o @ w_o + b_o

def swiglu(h, w_gate, w_up, w_down):
    return (jax.nn.silu(h @ w_gate) * (h @ w_up)) @ w_down

def setup_inputs(seed: int = 0) -> dict:
    key = jax.random.key(seed)
    ks = iter(jax.random.split(key, 32))
    D, F = D_MODEL, D_FF
    nrm = lambda shape, std: jax.random.normal(next(ks), shape, jnp.float32) * std
    offs = jax.random.randint(next(ks), (BATCH, 1), 0, 4096, dtype=jnp.int32)
    positions = offs + jnp.arange(SEQ, dtype=jnp.int32)[None, :]
    mla_in_w = MLA_Q_RANK + MLA_KV_RANK + MLA_ROPE
    swa_qkv_w = (SWA_HEADS + 2 * SWA_KV_HEADS) * SWA_HEAD_DIM
    return {
        "x": nrm((BATCH, SEQ, D), 1.0),
        "c": nrm((BATCH, D), 1.0),
        "positions": positions,
        "ada_w": nrm((DEPTH, D, 6 * D), 0.5 * D ** -0.5),
        "ada_b": nrm((DEPTH, 6 * D), 0.02),
        "ln_mix_g": 1.0 + nrm((DEPTH, D), 0.02),
        "ln_mix_b": nrm((DEPTH, D), 0.02),
        "ln_ffn_g": 1.0 + nrm((DEPTH, D), 0.02),
        "ln_ffn_b": nrm((DEPTH, D), 0.02),
        "ffn_w_gate": nrm((DEPTH, D, F), D ** -0.5),
        "ffn_w_up": nrm((DEPTH, D, F), D ** -0.5),
        "ffn_w_down": nrm((DEPTH, F, D), F ** -0.5 * DEEPNORM_BETA),
        "mla_w_in": nrm((N_MLA, D, mla_in_w), D ** -0.5),
        "mla_q_norm": 1.0 + nrm((N_MLA, MLA_Q_RANK), 0.02),
        "mla_w_q_b": nrm((N_MLA, MLA_Q_RANK, MLA_HEADS * (MLA_NOPE + MLA_ROPE)), MLA_Q_RANK ** -0.5),
        "mla_kv_norm": 1.0 + nrm((N_MLA, MLA_KV_RANK), 0.02),
        "mla_w_kv_b": nrm((N_MLA, MLA_KV_RANK, MLA_HEADS * (MLA_NOPE + MLA_V)), MLA_KV_RANK ** -0.5),
        "mla_w_o": nrm((N_MLA, MLA_HEADS * MLA_V, D), (MLA_HEADS * MLA_V) ** -0.5 * DEEPNORM_BETA),
        "swa_w_qkv": nrm((N_SWA, D, swa_qkv_w), D ** -0.5),
        "swa_b_qkv": nrm((N_SWA, swa_qkv_w), 0.02),
        "swa_sinks": nrm((N_SWA, SWA_HEADS), 1.0),
        "swa_w_o": nrm((N_SWA, SWA_HEADS * SWA_HEAD_DIM, D), (SWA_HEADS * SWA_HEAD_DIM) ** -0.5 * DEEPNORM_BETA),
        "swa_b_o": nrm((N_SWA, D), 0.02),
    }

def reference(x, c, positions, ada_w, ada_b, ln_mix_g, ln_mix_b, ln_ffn_g, ln_ffn_b,
              ffn_w_gate, ffn_w_up, ffn_w_down, mla_w_in, mla_q_norm, mla_w_q_b, mla_kv_norm,
              mla_w_kv_b, mla_w_o, swa_w_qkv, swa_b_qkv, swa_sinks, swa_w_o, swa_b_o):
    cos_a, sin_a = rope_cos_sin(positions, MLA_ROPE)
    cos_b, sin_b = rope_cos_sin(positions, SWA_ROT)
    cond = jax.nn.silu(c)
    for i in range(DEPTH):
        mod = (cond @ ada_w[i] + ada_b[i])[:, None, :]
        sh_m, sc_m, g_m, sh_f, sc_f, g_f = jnp.split(mod, 6, axis=-1)
        h = x * (1.0 + sc_m) + sh_m
        j = i // N_MIXERS
        if i % N_MIXERS == 0:
            y = mla_mixer(h, cos_a, sin_a, mla_w_in[j], mla_q_norm[j], mla_w_q_b[j],
                          mla_kv_norm[j], mla_w_kv_b[j], mla_w_o[j])
        else:
            y = swa_mixer(h, cos_b, sin_b, swa_w_qkv[j], swa_b_qkv[j], swa_sinks[j],
                          swa_w_o[j], swa_b_o[j])
        x = layer_norm(DEEPNORM_ALPHA * x + g_m * y, ln_mix_g[i], ln_mix_b[i])
        h = x * (1.0 + sc_f) + sh_f
        y = swiglu(h, ffn_w_gate[i], ffn_w_up[i], ffn_w_down[i])
        x = layer_norm(DEEPNORM_ALPHA * x + g_f * y, ln_ffn_g[i], ln_ffn_b[i])
    return x


_drawn_inputs = setup_inputs


def setup_inputs(seed=0):
    import zlib

    import numpy as np

    out = dict(_drawn_inputs(seed))
    spreads = {}
    factors = {'ada_b': 5.908,
     'mla_q_norm': 8.0,
     'mla_w_q_b': 5.078,
     'mla_kv_norm': 8.0,
     'swa_b_qkv': 30.027,
     'swa_sinks': 8.0,
     'swa_b_o': 8.0}
    for name, (base, spread) in spreads.items():
        noise = np.random.default_rng([zlib.crc32(name.encode()), seed]).standard_normal(out[name].shape)
        drawn = base * np.exp(spread * noise) if base else spread * noise
        out[name] = __import__('jax').numpy.asarray(drawn.astype(out[name].dtype))
    for name, factor in factors.items():
        out[name] = (out[name] * factor).astype(out[name].dtype)
    return out
```

```python
from contextlib import ExitStack

import numpy as np

import concourse.bass as bass
from concourse import mybir

F32 = mybir.dt.float32
F32R = mybir.dt.float32r
I32 = mybir.dt.int32
ALU = mybir.AluOpType
ACT = mybir.ActivationFunctionType
AX = mybir.AxisListType.X
ds = bass.ds

P = 128
D = 1024
SEQ = 1024
KC = D // P
TH = 512
NT = SEQ // TH
HEADS, NOPE, ROT, VDIM = 8, 128, 64, 128
QRANK, KVRANK = 384, 256
QC, KVC = QRANK // P, KVRANK // P
WH, WKV, WD, WROT = 16, 4, 64, 16
GRP = WH // WKV
DFF = 2816
FC = DFF // P
ITERS = FC // 2
NB = SEQ // P
DEPTH = 2
ALPHA = (2 * DEPTH) ** 0.25
LN_EPS, RMS_EPS = 1e-5, 1e-6
THETA = 500000.0
MLA_SCALE = (NOPE + ROT) ** -0.5
SWA_SCALE = WD ** -0.5
MASKED = -1e30
RING = 3

T_LAT = 0
T_HEAD = T_LAT + NT * 6
T_WO = [T_HEAD + 3 * (HEADS // 2), 0]
T_FFN = [T_WO[0] + NT * KC, 0]
T_QKV = T_FFN[0] + 6 * ITERS
T_WO[1] = T_QKV + NT * 12
T_FFN[1] = T_WO[1] + NT * KC
T_END = T_FFN[1] + 6 * ITERS

PAIR_STEPS = 22
N_LAT = 0
N_HEAD0 = N_LAT + NT * 6
N_PAIR = N_HEAD0 + 8
N_WO = [N_HEAD0 + PAIR_STEPS * (HEADS // 2), 0]
N_FFN = [N_WO[0] + NT * KC, 0]
N_QKV = N_FFN[0] + 16 * ITERS
N_WO[1] = N_QKV + NT * (12 + 16)
N_FFN[1] = N_WO[1] + NT * KC

HEAD_STEPS = [
    ("S", 0), ("S", 1), ("N", 0), ("S", 2), ("N", 1), ("S", 3), ("T", 0, 0), ("N", 2), ("V", 0, 0), ("N", 3),
    ("S", 4), ("T", 1, 0), ("T", 1, 1), ("V", 1, 0), ("V", 1, 1), ("S", 5), ("N", 4), ("S", 6), ("N", 5),
    ("T", 2, 0), ("T", 2, 1), ("V", 2, 0), ("T", 2, 2), ("V", 2, 1), ("S", 7), ("V", 2, 2), ("N", 6),
    ("Q",), ("N", 7),
    ("T", 3, 0), ("T", 3, 1), ("V", 3, 0), ("T", 3, 2), ("V", 3, 1), ("T", 3, 3), ("V", 3, 2), ("V", 3, 3), ("W",),
]
T_GROUPS = 10
SBANK = [0, 1, 2, 3, 0, 2, 0, 2]
SPREV = [(6, 2), (6, 3), (7, 3), (7, 4), (1, 3), (3, 2), (4, 2), (5, 2)]


def t_index(g, cc):
    return g * (g + 1) // 2 + cc


def lat_steps():
    out = []
    for th in range(NT):
        out.append(("E", th, 0))
        if th:
            out.append(("C", 2 * th - 1))
        out.append(("E", th, 1))
        if th:
            out.append(("B", 2 * th - 1))
        out += [("E", th, 2), ("E", th, 3), ("C", 2 * th), ("E", th, 4), ("E", th, 5), ("B", 2 * th)]
    return out + [("C", 2 * NT - 1), ("B", 2 * NT - 1)]


class Chain:

    def __init__(self, eng, sem):
        self.eng, self.sem, self.n = eng, sem, 0

    def __call__(self, ins):
        self.tick(ins)
        self.wait()

    def tick(self, ins):
        ins.then_inc(self.sem, 1)
        self.n = self.n + 1

    def wait(self):
        self.eng.wait_ge(self.sem, self.n)


def tile_width(T):
    if T_HEAD <= T < T_WO[0]:
        return (QC * P, QC * 2 * P, KVC * 4 * P)[(T - T_HEAD) % 3]
    return D


def build(nc, A):
    with ExitStack() as ctx:
        def sb(name, shape, dt=F32):
            return ctx.enter_context(nc.sbuf_tensor(name, shape, dt))

        def sem(name):
            return ctx.enter_context(nc.semaphore(name))

        ident = sb("ident", [P, P], F32R)
        ident32 = ident[:].bitcast(F32)
        ones = sb("ones", [P, P])
        band = sb("band", [P, 2, P], F32R)
        mod = sb("mod", [P, DEPTH, 6, KC])
        ada_b = sb("ada_b", [P, DEPTH, 6, KC])
        ln_gb = sb("ln_gb", [P, 4, 2, KC])
        lat_g = sb("lat_g", [P, KVC + QC])
        qk_b = sb("qk_b", [P, 10])
        wo_b = sb("wo_b", [P, KC])
        sinks = sb("sinks", [P, WH])
        cond_in = sb("cond_in", [P, KC])
        cond = sb("cond", [P, KC])
        freq = sb("freq", [P, 8])
        vecs = sb("vecs", [P, 4, KC])
        vtmp = sb("vtmp", [P, 2, KC])
        stds = sb("stds", [P, 2, 4])
        row_max = sb("row_max", [P, 8])
        neg_max = sb("neg_max", [P, 8])
        row_sum = sb("row_sum", [P, 8])
        sink_e = sb("sink_e", [P, 8])
        row_inv = sb("row_inv", [P, 8])

        base = (nc.sbuf_base + 31) // 32 * 32
        K = 1024

        def at(name, shape, dt, kib):
            size = int(np.prod(shape[1:])) * 4
            assert base + int(kib * K) + size <= nc.sbuf_usable_end, (name, base, kib)
            return nc.alloc_sbuf_tensor_at(name, shape, dt, offset=base + int(kib * K))

        h_hi = at("h_hi", [P, KC, SEQ], F32R, 0)
        h_lo = at("h_lo", [P, KC, SEQ], F32R, 32)
        w_raw = at("w_raw", [P, RING, D], F32, 64)
        w_hi = at("w_hi", [P, RING, D], F32R, 76)
        w_lo = at("w_lo", [P, RING, D], F32R, 88)
        G = 100
        x = at("x", [P, KC, SEQ], F32, G)
        lat_hi = at("lat_hi", [P, KVC + QC, SEQ], F32R, G)
        lat_lo = at("lat_lo", [P, KVC + QC, SEQ], F32R, G + 20)
        kr_hi = at("kr_hi", [P, SEQ], F32R, G + 40)
        kr_lo = at("kr_lo", [P, SEQ], F32R, G + 44)
        q_hi = at("q_hi", [P, SEQ], F32R, G + 48)
        q_lo = at("q_lo", [P, SEQ], F32R, G + 52)
        qr = at("qr", [P, 2, SEQ], F32R, G + 56)
        k_hi = at("k_hi", [P, SEQ], F32R, G + 64)
        k_lo = at("k_lo", [P, SEQ], F32R, G + 68)
        v_hi = at("v_hi", [P, NB, VDIM], F32R, G + 72)
        v_lo = at("v_lo", [P, NB, VDIM], F32R, G + 76)
        prob = at("prob", [P, 4, SEQ], F32, G + 80)
        pt_hi = at("pt_hi", [P, 2, TH], F32R, G + 96)
        pt_lo = at("pt_lo", [P, 2, TH], F32R, G + 100)
        rt_out = at("rt_out", [P, 2, TH], F32, 24)
        rt_tmp = at("rt_tmp", [P, TH], F32, 32 + 24)
        rcos = at("rcos", [P, SEQ], F32, 28)
        rsin = at("rsin", [P, SEQ], F32, 32 + 28)
        lat32 = at("lat32", [P, KVC + QC, TH], F32, G + 80)
        lat_sq = at("lat_sq", [P, 2, TH], F32, G + 90)
        lat_ss = at("lat_ss", [P, TH], F32, G + 94)
        cos0 = at("cos0", [P, SEQ], F32, G + 96)
        sin0 = at("sin0", [P, SEQ], F32, G + 100)
        diag0 = at("diag0", [P, 4, P], F32, G + 78)
        ada_acc = at("ada_acc", [P, 2, D], F32, G + 58)
        ada_raw = at("ada_raw", [P, 3, D], F32, G + 66)
        f_hi = at("f_hi", [P, 2, SEQ], F32R, G + 32)
        f_lo = at("f_lo", [P, 2, SEQ], F32R, G + 40)
        ln_s = at("ln_s", [P, TH], F32, G + 48)
        ln_sq = at("ln_sq", [P, 2, TH], F32, G + 50)
        h32 = at("h32", [P, 2, TH], F32, G + 54)
        gate_s = at("gate_s", [P, 2, TH], F32, G + 58)
        f32 = at("f32", [P, 2, TH], F32, G + 62)
        ada1_acc = at("ada1_acc", [P, 6, D], F32, G + 66)
        ada1_raw = at("ada1_raw", [P, 2, D], F32, G + 90)
        pos_i = at("pos_i", [P, SEQ], I32, G + 80)
        tab_ang = at("tab_ang", [P, SEQ], F32, G + 84)
        tab_k = at("tab_k", [P, SEQ], F32, G + 88)
        tab_t = at("tab_t", [P, SEQ], F32, G + 92)
        sq_st = at("sq_st", [P, WH, TH], F32R, G)
        sk_hi = at("sk_hi", [P, WKV, SEQ], F32R, G + 32)
        sk_lo = at("sk_lo", [P, WKV, SEQ], F32R, G + 48)
        sv_hi = at("sv_hi", [P, NB, WKV * WD], F32R, G + 64)
        sv_lo = at("sv_lo", [P, NB, WKV * WD], F32R, G + 72)
        sprob = at("sprob", [P, 2, GRP, 2 * P], F32, G + 80)
        spt_hi = at("spt_hi", [P, 2, TH], F32R, G + 88)
        spt_lo = at("spt_lo", [P, 2, TH], F32R, G + 92)
        scos = at("scos", [P, SEQ], F32, G + 96)
        ssin = at("ssin", [P, SEQ], F32, G + 100)
        sr_out = at("sr_out", [P, 2, TH], F32, G + 80)
        sr_tmp = at("sr_tmp", [P, TH], F32, G + 84)
        sv_b = at("sv_b", [P, WKV * WD], F32, G + 86)

        spad = ctx.enter_context(nc.psum_tensor("spad", [P, 4, 512], F32))
        tpad = ctx.enter_context(nc.psum_tensor("tpad", [P, 2, 512], F32))
        dpad = ctx.enter_context(nc.psum_tensor("dpad", [P, 2, 512], F32))
        spad_flat = spad[:].rearrange("p b n -> p (b n)")

        tab_dram = nc.dram_tensor("tables", (4, P, SEQ), F32, kind="Internal").ap()
        spill = nc.dram_tensor("spill", (P, KC, SEQ), F32, kind="Internal").ap()

        const_in = sem("const_in")
        pos_in = sem("pos_in")
        x_in = [sem(f"x_in{t}") for t in range(NT)]
        w_in = [sem(f"w_in{s}") for s in range(RING)]
        ada_in = [sem(f"ada_in{s}") for s in range(3)]
        ada1_in = [sem(f"ada1_in{s}") for s in range(2)]
        tab_out = sem("tab_out")
        tab_in = sem("tab_in")
        spilled = sem("spilled")
        res_in = [sem(f"res_in{t}") for t in range(NT)]
        vbias_in = sem("vbias_in")
        stored = sem("stored")
        w_rounded = sem("w_rounded")
        w_split = sem("w_split")
        consts = sem("consts")
        ident_ok = sem("ident_ok")
        cond_ok = sem("cond_ok")
        tab_k_ok = sem("tab_k_ok")
        tab_ready = sem("tab_ready")
        tab_abs = sem("tab_abs")
        tab_trig = sem("tab_trig")
        tab_sign = sem("tab_sign")
        dense_done = sem("dense_done")
        dense_free = sem("dense_free")
        ada_used = sem("ada_used")
        ada_fold = sem("ada_fold")
        mod_ok = sem("mod_ok")
        vec_ok = sem("vec_ok")
        sq_ok = sem("sq_ok")
        ss_ok = sem("ss_ok")
        stat_col = sem("stat_col")
        stat_std = sem("stat_std")
        stat_diag = sem("stat_diag")
        stat_row = sem("stat_row")
        lat_ok = sem("lat_ok")
        lat_rounded = sem("lat_rounded")
        lat_split = sem("lat_split")
        kr_ok = sem("kr_ok")
        kr_rounded = sem("kr_rounded")
        kr_split = sem("kr_split")
        h32_in = sem("h32_in")
        h32_ok = sem("h32_ok")
        h_rounded = sem("h_rounded")
        h_split = sem("h_split")
        ln_sum = sem("ln_sum")
        ln_mean = sem("ln_mean")
        ln_cent = sem("ln_cent")
        ln_sqr = sem("ln_sqr")
        ln_part = sem("ln_part")
        ln_sqsum = sem("ln_sqsum")
        ln_z = sem("ln_z")
        ln_res = sem("ln_res")
        res_scaled = sem("res_scaled")
        head_rounded = sem("head_rounded")
        rope_ok = sem("rope_ok")
        rope_rounded = sem("rope_rounded")
        s_done = sem("s_done")
        m_ok = sem("m_ok")
        e_done = sem("e_done")
        p_ok = sem("p_ok")
        t_done = sem("t_done")
        t_rounded = sem("t_rounded")
        t_split = sem("t_split")
        v_done = sem("v_done")
        o_rounded = sem("o_rounded")
        gate_done = sem("gate_done")
        up_done = sem("up_done")
        silu_ok = sem("silu_ok")
        f32_ok = sem("f32_ok")
        f_rounded = sem("f_rounded")
        f_split = sem("f_split")
        ada1_scaled = sem("ada1_scaled")
        ada1_used = sem("ada1_used")
        rot_ok = sem("rot_ok")
        rot_rounded = sem("rot_rounded")
        rot_split = sem("rot_split")
        k_stack = sem("k_stack")
        ss_done = sem("ss_done")
        sv_split = sem("sv_split")
        sm_ok = sem("sm_ok")
        se_done = sem("se_done")
        sp_ok = sem("sp_ok")
        st_done = sem("st_done")
        st_rounded = sem("st_rounded")
        st_split = sem("st_split")
        so_rounded = sem("so_rounded")
        dve_own = sem("dve_own")
        pool_own = sem("pool_own")

        block = ctx.enter_context(nc.Block())

        def halves(th):
            return slice(th * TH, th * TH + TH)

        def res_floor(q):
            return 8 * 2 * q

        @block.sync
        def _(sp):
            ada0 = A["ada_w"][0]

            def load_ada(u):
                if u >= 3:
                    sp.wait_ge(ada_used, u - 2)
                v, kc = u // KC, u % KC
                sp.dma_start(ada_raw[:, u % 3, :], ada0[kc * P:(kc + 1) * P, v * D:(v + 1) * D])\
                    .then_inc(ada_in[u % 3], 16)

            def load_w(T, src):
                if T >= RING:
                    sp.wait_ge(w_split, T - RING + 1)
                w = src.shape[-1]
                sp.dma_start(w_raw[:, T % RING, 0:w], src).then_inc(w_in[T % RING], 16)

            smalls = [(cond_in, A["cond"]), (ada_b, A["ada_b"]), (ln_gb, A["ln_gb"]), (lat_g, A["lat_g"]),
                      (qk_b, A["qk_b"]), (wo_b, A["wo_b"]), (freq, A["freq"]),
                      (sinks, A["sinks"].partition_broadcast(P))]
            for dst, src in smalls:
                sp.dma_start(dst[:], src).then_inc(const_in, 16)
            sp.dma_start(pos_i[:], A["pos"].partition_broadcast(P)).then_inc(pos_in, 16)
            for u in range(2 * KC):
                load_ada(u)
                if u == 2 * KC - 6:
                    for th in range(NT):
                        sp.dma_start(x[:, :, halves(th)], A["x"][:, :, halves(th)]).then_inc(x_in[th], 16)
            for T in range(RING):
                load_w(T, A["w_lat"][T % 6])
            u = 2 * KC
            for T in range(RING, T_HEAD + 3):
                load_w(T, A["w_lat"][T % 6] if T < T_HEAD else
                       [A["w_qr"], A["w_qn"], A["w_kv"]][T - T_HEAD][0])
                for _ in range(3):
                    if u < 6 * KC:
                        load_ada(u)
                        u += 1
            sp.wait_ge(tab_out, 16 * 8)
            sp.wait_ge(dense_done, N_HEAD0)
            sp.dma_start(rcos[:], tab_dram[0]).then_inc(tab_in, 16)
            sp.dma_start(rsin[:], tab_dram[1]).then_inc(tab_in, 16)
            for p in range(1, HEADS // 2):
                for k, src in enumerate((A["w_qr"], A["w_qn"], A["w_kv"])):
                    load_w(T_HEAD + 3 * p + k, src[p])

            def residual_back(src):
                for th in range(NT):
                    sp.dma_start(x[:, :, halves(th)], src[:, :, halves(th)]).then_inc(res_in[th], 16)

            for layer in range(DEPTH):
                for s in range(NT * KC):
                    T = T_WO[layer] + s
                    if s == 3:
                        if layer == 0:
                            sp.wait_ge(dense_done, N_PAIR + PAIR_STEPS * 3 + 10)
                            residual_back(A["x"])
                        else:
                            sp.wait_ge(ss_done, NB * WKV)
                            residual_back(spill)
                    load_w(T, A["w_o"][layer, s % KC])

                def turn(i, ks=range(6)):
                    for k in ks:
                        T = T_FFN[layer] + 6 * i + k
                        T0 = T_FFN[layer] + k
                        f = 2 * i + (k % 4) // 2 if k < 4 else 2 * i + k - 4
                        src = A["w_dn"] if k >= 4 else (A["w_gt"], A["w_up"])[k % 2]
                        src = src[layer]
                        sp.wait_ge(w_split, T - RING + 1)
                        src = src[f] if isinstance(f, int) else src[ds(f, 1)].rearrange("a p n -> (a p) n")
                        sp.dma_start(w_raw[:, T0 % RING, :], src).then_inc(w_in[T0 % RING], 16)

                with sp.Fori(0, ITERS) as i:
                    turn(i)
                if layer == 0:
                    for T in range(T_QKV, T_QKV + RING):
                        load_w(T, A["w_qkv"][T - T_QKV])
                    for th in range(NT):
                        sp.wait_ge(ln_res, res_floor(1) + KC * (th + 1))
                        sp.dma_start(spill[:, :, halves(th)], x[:, :, halves(th)]).then_inc(spilled, 16)
                    sp.wait_ge(ada_fold, 6 * DEPTH)
                    sp.wait_ge(h_split, 16 * 2 + 16)
                    sp.dma_start(scos[:], tab_dram[2]).then_inc(tab_in, 16)
                    sp.dma_start(ssin[:], tab_dram[3]).then_inc(tab_in, 16)
                    for th in range(NT):
                        for k in range(12):
                            if k == RING:
                                if th:
                                    sp.wait_ge(st_done, NB // NT * WKV)
                                sp.dma_start(sv_b[:], A["v_b"].partition_broadcast(P)).then_inc(vbias_in, 16)
                            T = T_QKV + 12 * th + k
                            if T >= T_QKV + RING:
                                load_w(T, A["w_qkv"][k])
            sp.wait_ge(spilled, 16 * NT)
            for th in range(NT):
                for c in range(KC):
                    sp.wait_ge(ln_res, res_floor(3) + KC * th + c + 1)
                    sp.dma_start(A["out"][:, c, halves(th)], x[:, c, halves(th)]).then_inc(stored, 16)
            sp.wait_ge(stored, 16 * NT * KC)

        @block.tensor
        def _(pe):
            def three(out, w, x_, first, last, skip=False):
                pe.matmul(out, w[0], x_[0], start=first, stop=False, skip_group_check=skip)
                pe.matmul(out, w[0], x_[1], start=False, stop=False, skip_group_check=skip)
                return pe.matmul(out, w[1], x_[0], start=False, stop=last, skip_group_check=skip)

            def wt(T, lo, hi):
                return w_hi[:, T % RING, lo:hi], w_lo[:, T % RING, lo:hi]

            def bank(n_static):
                return dpad[:, n_static % 2, :]

            def claim(n):
                if not isinstance(n, int) or n >= 2:
                    pe.wait_ge(dense_free, n - 1)

            def dense(n, T, chunks, src):
                pe.wait_ge(w_split, T + 1)
                claim(n)
                for k in range(chunks):
                    mm = three(bank(n), wt(T, k * P, k * P + P), src(k), k == 0, k == chunks - 1)
                mm.then_inc(dense_done, 1)

            def h_of(th):
                return lambda k: (h_hi[:, k, halves(th)], h_lo[:, k, halves(th)])

            def stat_column(src):
                for t in range(4):
                    mm = pe.matmul(tpad[:, 0, t:t + 1], src[:, t * P:t * P + P], ones[:, 0:1],
                                   start=True, stop=True, skip_group_check=True)
                mm.then_inc(stat_col, 1)

            def stat_spread(z, diag):
                pe.wait_ge(stat_diag, z + 1)
                if 0 < z < 4:
                    pe.wait_ge(lat_ok, (0, 2, 5, 7)[z])
                for t in range(4):
                    mm = pe.matmul(tpad[:, 1, t * P:t * P + P], ones[:], diag[:, t, :],
                                   start=True, stop=True, skip_group_check=True)
                mm.then_inc(stat_row, 1)

            def fold(v, acc, psum, before):
                if before:
                    pe.wait_ge(mod_ok, before)
                for c in range(KC):
                    mm = pe.matmul(psum[:, v * KC + c:v * KC + c + 1], acc[:, c * P:c * P + P], ones[:, 0:1],
                                   start=True, stop=True, skip_group_check=True)
                mm.then_inc(ada_fold, 1)

            pe.wait_ge(consts, 3)
            pe.wait_ge(ident_ok, 2)
            for v in range(2):
                pe.wait_ge(ada_used, KC * (v + 1))
                fold(v, ada_acc[:, v % 2, :], spad[:, 3, :], v)

            next_fold = 2
            for step in lat_steps():
                if step[0] == "E":
                    _, th, m = step
                    n = N_LAT + 6 * th + m
                    if m == 0:
                        pe.wait_ge(h_split, KC * (th + 1))
                    dense(n, T_LAT + 6 * th + m, KC, h_of(th))
                    if n in (4, 7, 9):
                        pe.wait_ge(ada_used, KC * (next_fold + 1))
                        fold(next_fold, ada_acc[:, next_fold % 2, :], spad[:, 3, :], next_fold)
                        next_fold += 1
                elif step[0] == "C":
                    z = step[1]
                    pe.wait_ge(ss_ok, 5 * (z // 2) + (2, 5)[z % 2])
                    stat_column(lat_ss)
                else:
                    stat_spread(step[1], diag0)
            pe.wait_ge(ada_used, KC * 6)
            fold(5, ada_acc[:, 1, :], spad[:, 3, :], 5)

            def lat(lo, c):
                return lambda k: (lat_hi[:, lo + k, c], lat_lo[:, lo + k, c])

            def proj_q(n, n0, hp, p, rotary):
                T = T_HEAD + 3 * p
                for th in range(NT):
                    pe.wait_ge(w_split, T + 2)
                    claim(n + th)
                    for k in range(QC):
                        lo = k * 2 * P + hp * P
                        mm = three(bank(n0 + th), wt(T_HEAD + 1, lo, lo + P), lat(KVC, halves(th))(k), k == 0, k == QC - 1)
                    mm.then_inc(dense_done, 1)
                for th in range(NT):
                    pe.wait_ge(w_split, T + 3)
                    claim(n + 2 + th)
                    for k in range(KVC):
                        lo = (k * 4 + 2 * hp) * P
                        mm = three(bank(n0 + th), wt(T_HEAD + 2, lo, lo + P), lat(0, halves(th))(k), k == 0, k == KVC - 1)
                    mm.then_inc(dense_done, 1)
                if rotary:
                    for th in range(NT):
                        pe.wait_ge(w_split, T + 1)
                        claim(n + 4 + th)
                        for k in range(QC):
                            mm = three(bank(n0 + th), wt(T_HEAD, k * P, k * P + P), lat(KVC, halves(th))(k),
                                       k == 0, k == QC - 1)
                        mm.then_inc(dense_done, 1)

            def proj_v(n, n0, hp):
                for part in range(2):
                    claim(n + part)
                    for t in range(4):
                        tok = slice((4 * part + t) * P, (4 * part + t) * P + P)
                        for k in range(KVC):
                            lo = (k * 4 + 2 * hp + 1) * P
                            mm = three(bank(n0 + part)[:, t * P:t * P + P], lat(0, tok)(k), wt(T_HEAD + 2, lo, lo + P),
                                       k == 0, k == KVC - 1)
                    mm.then_inc(dense_done, 1)

            def head(p, hp, first, more):
                e0 = 16 * p + 8 * hp
                u0 = 2 * T_GROUPS * p + T_GROUPS * hp
                v0 = 12 * p + 6 * hp
                n = N_PAIR + PAIR_STEPS * p + 10 * hp
                nn = N_PAIR + 10 * hp
                kk = 0
                vs = 0
                pe.wait_ge(dense_free, n)
                pe.wait_ge(rope_ok, 4 * (p + 1))
                if first:
                    pe.wait_ge(kr_split, NT)
                for st in HEAD_STEPS:
                    if st[0] == "S":
                        i = st[1]
                        if not (first and i < 4):
                            pe.wait_ge(e_done, e0 + i - SPREV[i][1] + 1)
                        for c0 in range(0, i + 1, 4):
                            c1 = min(c0 + 4, i + 1)
                            out = spad[:, SBANK[i] + c0 // 4, 0:(c1 - c0) * P]
                            q = slice(i * P, i * P + P)
                            keys = slice(c0 * P, c1 * P)
                            three(out, (q_hi[:, q], q_lo[:, q]), (k_hi[:, keys], k_lo[:, keys]), True, False)
                            pe.matmul(out, qr[:, hp, q], kr_hi[:, keys], start=False, stop=False)
                            mm = pe.matmul(out, qr[:, hp, q], kr_lo[:, keys], start=False, stop=c1 <= i)
                            if c1 > i:
                                mm = pe.matmul(out[:, (i - c0) * P:(i - c0) * P + P], ident[:], band[:, 1, :],
                                               start=False, stop=True)
                        mm.then_inc(s_done, 1)
                    elif st[0] == "T":
                        _, g, cc = st
                        u = t_index(g, cc)
                        pe.wait_ge(p_ok, e0 + 2 * g + 2)
                        if not (first and u < 2):
                            pe.wait_ge(t_split, u0 + u - 1)
                        for c in (2 * cc, 2 * cc + 1):
                            for i in (2 * g, 2 * g + 1):
                                if c <= i:
                                    col = 256 if c == 2 * g + 1 else (c % 2) * 256 + (i % 2) * P
                                    mm = pe.transpose(tpad[:, u % 2, col:col + P],
                                                      prob[:, i % 4, c * P:c * P + P], ident32)
                        mm.then_inc(t_done, 1)
                    elif st[0] == "V":
                        _, g, cc = st
                        u = t_index(g, cc)
                        pe.wait_ge(t_split, u0 + u + 1)
                        if cc == 0:
                            claim(n + kk)
                        out = bank(nn + kk)
                        for c in (2 * cc, 2 * cc + 1):
                            part = slice(P, 2 * P) if c == 2 * g + 1 else slice(0, 2 * P)
                            src = slice(256, 256 + P) if c == 2 * g + 1 else slice((c % 2) * 256, (c % 2) * 256 + 2 * P)
                            mm = three(out[:, part], (v_hi[:, c, :], v_lo[:, c, :]),
                                       (pt_hi[:, u % 2, src], pt_lo[:, u % 2, src]), c == 0, c == 2 * g + 1)
                        if cc == g:
                            mm.then_inc(dense_done, 1)
                            kk += 1
                        else:
                            mm.then_inc(v_done, 1)
                    elif st[0] == "Q":
                        if hp == 0:
                            proj_q(n + kk, nn + kk, 1, p, False)
                            kk += 4
                        elif more:
                            proj_q(n + kk, nn + kk, 0, p + 1, True)
                            kk += 6
                    elif st[0] == "W":
                        if hp == 0 or more:
                            proj_v(n + kk, nn + kk, 1 - hp)
                            kk += 2

            pe.wait_ge(lat_split, 10)
            proj_q(N_HEAD0, N_HEAD0, 0, 0, True)
            proj_v(N_HEAD0 + 6, N_HEAD0 + 6, 0)
            for p in range(HEADS // 2):
                head(p, 0, p == 0, True)
                head(p, 1, False, p < HEADS // 2 - 1)

            def ln_mean_mm(L):
                pe.wait_ge(ln_sum, L + 1)
                if L:
                    pe.wait_ge(ln_z, KC * L)
                pe.matmul(tpad[:, 1, :], ones[:], ln_s[:], start=True, stop=True).then_inc(ln_mean, 1)

            def ln_var_mm(L):
                pe.wait_ge(ln_sqsum, L + 1)
                stat_column(ln_s)

            def ln_spread(L):
                stat_spread(4 + L, ln_sq[:, 0, :].rearrange("p (t c) -> p t c", t=4))

            def out_proj(layer):
                for th in range(NT):
                    for c in range(KC):
                        s = KC * th + c
                        if layer == 0 and s == 0:
                            pe.wait_ge(o_rounded, 4 * HEADS)
                        if layer == 1 and s == 0:
                            pe.wait_ge(so_rounded, 2 * NB * WKV)
                        dense(N_WO[layer] + s, T_WO[layer] + s, KC, h_of(th))
                        if th == 1:
                            L = 4 * layer
                            if c == 0:
                                ln_mean_mm(L)
                            elif c == 3:
                                ln_var_mm(L)
                            elif c == 4:
                                ln_spread(L)

            def feed_forward(layer):
                jb = 44 * layer

                def turn(i, first, last):
                    T = T_FFN[layer] + 6 * i
                    T0 = T_FFN[layer]
                    for f in range(2):
                        for th in range(NT):
                            j = jb + 4 * i + 2 * f + th
                            for which, s in ((0, gate_done), (1, up_done)):
                                k = 2 * f + which
                                if first and f == 0 and which == 0:
                                    pe.wait_ge(h_split, 16 * (2 * layer + 1) + KC * (th + 1))
                                pe.wait_ge(w_split, T + k + 1)
                                if not (first and f == 0):
                                    pe.wait_ge((silu_ok, f32_ok)[which], j - 1)
                                for c in range(KC):
                                    mm = three(spad[:, 2 * which + th, :], wt(T0 + k, c * P, c * P + P), h_of(th)(c),
                                               c == 0, c == KC - 1)
                                mm.then_inc(s, 1)
                    for th in range(NT):
                        pe.wait_ge(f_split, jb + 4 * i + 3 + th)
                        pe.wait_ge(w_split, T + 6)
                        for c in range(KC):
                            n = N_FFN[layer] + 16 * i + KC * th + c
                            claim(n)
                            for f in range(2):
                                mm = three(bank(N_FFN[layer] + c), wt(T0 + 4 + f, c * P, c * P + P),
                                           (f_hi[:, f, halves(th)], f_lo[:, f, halves(th)]), f == 0, f == 1)
                            mm.then_inc(dense_done, 1)
                            if last and th == 1 and c == 1:
                                ln_mean_mm(4 * layer + 2)

                turn(0, True, False)
                with pe.Fori(1, ITERS - 1) as i:
                    turn(i, False, False)
                if layer == 0:
                    for v in range(6):
                        pe.wait_ge(ada1_used, KC * (v + 1))
                        fold(v, ada1_acc[:, v, :], tpad[:, 0, :], 6 + v)
                turn(ITERS - 1, False, True)
                L = 4 * layer + 2
                ln_var_mm(L)
                ln_spread(L)

            def norm_second(L):
                ln_mean_mm(L)
                ln_var_mm(L)
                ln_spread(L)

            out_proj(0)
            norm_second(1)
            feed_forward(0)
            norm_second(3)

            def qkv(th):
                for k in range(12):
                    T = T_QKV + 12 * th + k
                    n = N_QKV + 28 * th + k
                    if k == 0:
                        pe.wait_ge(h_split, 16 * 2 + KC * (th + 1))
                    if k in (2, 3):
                        pe.wait_ge(w_split, T + 1)
                        claim(n)
                        for t in range(4):
                            tok = slice(th * TH + t * P, th * TH + t * P + P)
                            for c in range(KC):
                                mm = three(bank(n)[:, t * P:t * P + P], (h_hi[:, c, tok], h_lo[:, c, tok]),
                                           wt(T, c * P, c * P + P), c == 0, c == KC - 1)
                        mm.then_inc(dense_done, 1)
                    else:
                        dense(n, T, KC, h_of(th))

            def s_scores(r):
                b, j = divmod(r, WKV)
                lo = 0 if b else P
                sl = 2 * (r % 2)
                if r >= 2:
                    pe.wait_ge(se_done, r - 1)
                q = slice((b % 4) * P, (b % 4) * P + P)
                keys = slice((b - 1) * P + lo, b * P + P)
                for half in range(2):
                    out2 = spad[:, sl + half, :].rearrange("p (g k) -> p g k", g=2)[:, :, lo:2 * P]
                    mask = band[:].rearrange("p a k -> p (a k)")[:, lo:2 * P].unsqueeze(1).to_broadcast([P, 2, 2 * P - lo])
                    pe.matmul(out2, ident[:], mask, start=True, stop=False, skip_group_check=True)
                    for g in range(2):
                        qs = sq_st[:, GRP * j + 2 * half + g, q]
                        pe.matmul(out2[:, g, :], qs, sk_hi[:, j, keys], start=False, stop=False, skip_group_check=True)
                        mm = pe.matmul(out2[:, g, :], qs, sk_lo[:, j, keys], start=False, stop=True,
                                       skip_group_check=True)
                mm.then_inc(ss_done, 1)

            def s_values(r):
                b, j = divmod(r, WKV)
                parts = (0, 1) if b else (1,)
                pe.wait_ge(sp_ok, r + 1)
                if r:
                    pe.wait_ge(st_split, r)
                for a in parts:
                    for g in range(GRP):
                        mm = pe.transpose(tpad[:, a, g * P:g * P + P], sprob[:, r % 2, g, a * P:a * P + P], ident32)
                mm.then_inc(st_done, 1)

            def s_product(r):
                b, j = divmod(r, WKV)
                parts = (0, 1) if b else (1,)
                n = N_QKV + 12 + 28 * (b // 4) + r % 16
                pe.wait_ge(st_split, r + 1)
                claim(n)
                for a in parts:
                    blk = b - 1 + a
                    mm = three(bank(n)[0:WD, :], (sv_hi[:, blk, j * WD:j * WD + WD], sv_lo[:, blk, j * WD:j * WD + WD]),
                               (spt_hi[:, a, :], spt_lo[:, a, :]), a == parts[0], a == 1)
                mm.then_inc(dense_done, 1)

            for th in range(NT):
                qkv(th)
                pe.wait_ge(k_stack, 8 * (th + 1))
                pe.wait_ge(rot_split, 16 * (th + 1))
                pe.wait_ge(rot_rounded, 26 * (th + 1))
                pe.wait_ge(sv_split, 2 * (th + 1))
                for r in range(16 * th, 16 * th + 16):
                    if r == 16 * th:
                        s_scores(r)
                    if r + 1 < 16 * th + 16:
                        s_scores(r + 1)
                    s_values(r)
                    s_product(r)

            out_proj(1)
            norm_second(5)
            feed_forward(1)
            norm_second(7)

        @block.scalar
        def _(act):
            def split(T, width=D, turn=0):
                sl = T % RING
                act.wait_ge(w_in[sl], 16 * (T // RING + 1) + 32 * turn)
                act.activation(w_hi[:, sl, 0:width], w_raw[:, sl, 0:width], ACT.Copy).then_inc(w_rounded, 1)

            def split_after(T, done, value):
                if T < T_END:
                    act.wait_ge(done, value)
                    split(T, tile_width(T))

            act.wait_ge(const_in, 16 * 8)
            act.activation(cond[:], cond_in[:], ACT.Silu).then_inc(cond_ok, 1)
            act.wait_ge(consts, 5)
            act.activation(ident[:], tab_t[:, 0:P], ACT.Copy).then_inc(ident_ok, 1)
            act.activation(band[:].rearrange("p a k -> p (a k)"), tab_t[:, P:3 * P], ACT.Copy).then_inc(ident_ok, 1)

            for T in range(RING):
                split(T)

            for th in range(NT):
                for c in range(KC):
                    act.wait_ge(h32_in, KC * th + c + 1)
                    act.activation(h_hi[:, c, halves(th)], h32[:, c % 2, :], ACT.Copy).then_inc(h_rounded, 1)

            for t in range(2):
                act.wait_ge(tab_ready, t + 1)
                if t:
                    act.wait_ge(tab_out, 16 * 4)
                act.activation(sin0[:], tab_ang[:], ACT.Sin).then_inc(tab_trig, 1)
                act.wait_ge(tab_trig, 2 * t + 1)
                act.activation(tab_ang[:], tab_ang[:], ACT.Abs).then_inc(tab_abs, 1)
                act.wait_ge(tab_abs, t + 1)
                act.wait_ge(tab_trig, 2 * t + 1)
                act.activation(cos0[:], tab_ang[:], ACT.Sin, scale=-1.0, bias=freq[:, 2:3]).then_inc(tab_trig, 1)
                act.wait_ge(tab_trig, 2 * t + 2)
                act.wait_ge(tab_sign, t + 1)
                for half in range(NT):
                    act.dma_start(tab_dram[2 - 2 * t, :, halves(half)], cos0[:, halves(half)]).then_inc(tab_out, 16)
                    act.dma_start(tab_dram[3 - 2 * t, :, halves(half)], sin0[:, halves(half)]).then_inc(tab_out, 16)
            def lat_chunk(m):
                return m - 1

            rounded = 0
            for step in lat_steps():
                if step[0] == "E":
                    _, th, m = step
                    n = N_LAT + 6 * th + m
                    if m:
                        j = 5 * th + m - 1
                        act.wait_ge(dense_done, n + 1)
                        if j >= 2:
                            act.wait_ge(ss_ok, j - 1)
                        act.activation(lat_sq[:, j % 2, :], dpad[:, n % 2, :], ACT.Square).then_inc(sq_ok, 1)
                    else:
                        act.wait_ge(kr_ok, th + 1)
                        act.activation(kr_hi[:, halves(th)], ln_sq[:, 0, :], ACT.Copy).then_inc(kr_rounded, 1)
                    split_after(T_LAT + n + RING, dense_done, n + 1)
                elif step[0] == "C":
                    z = step[1]
                    act.wait_ge(stat_col, z + 1)
                    rank = (KVRANK, QRANK)[z % 2]
                    act.activation(stds[:, 0, :], tpad[:, 0, 0:4], ACT.Sqrt, scale=1.0 / rank, bias=freq[:, 4:5])\
                        .then_inc(stat_std, 1)
                else:
                    z = step[1]
                    th = z // 2
                    for m in ((0, 1), (2, 3, 4))[z % 2]:
                        rounded += 1
                        act.wait_ge(lat_ok, rounded)
                        act.activation(lat_hi[:, m, halves(th)], lat32[:, m, :], ACT.Copy).then_inc(lat_rounded, 1)

            def proj_q(n, n0, hp, p, rotary):
                hr = 12 * p + 6 * hp
                for th in range(NT):
                    act.wait_ge(dense_done, n + th + 1)
                    act.activation(q_hi[:, halves(th)], dpad[:, (n0 + th) % 2, :], ACT.Copy).then_inc(head_rounded, 1)
                for th in range(NT):
                    act.wait_ge(dense_done, n + th + 3)
                    act.activation(k_hi[:, halves(th)], dpad[:, (n0 + th) % 2, :], ACT.Copy).then_inc(head_rounded, 1)
                if rotary:
                    for th in range(NT):
                        act.wait_ge(rope_ok, 4 * p + 2 * th + 1)
                        act.activation(qr[0:64, 0, halves(th)], rt_out[0:64, th, :], ACT.Copy).then_inc(rope_rounded, 1)
                        act.activation(qr[64:P, 1, halves(th)], rt_out[64:P, th, :], ACT.Copy).then_inc(rope_rounded, 1)

            def proj_v(n, n0):
                for part in range(2):
                    act.wait_ge(dense_done, n + part + 1)
                    act.activation(v_hi[:, 4 * part:4 * part + 4, :].rearrange("p t v -> p (t v)"),
                                   dpad[:, (n0 + part) % 2, :], ACT.Copy).then_inc(head_rounded, 1)

            def head(p, hp, first, more):
                e0 = 16 * p + 8 * hp
                u0 = 2 * T_GROUPS * p + T_GROUPS * hp
                n = N_PAIR + PAIR_STEPS * p + 10 * hp
                nn = N_PAIR + 10 * hp
                v0 = 12 * p + 6 * hp
                kk = 0
                freed = {}
                for st in HEAD_STEPS:
                    if st[0] == "V":
                        _, g, cc = st
                        u = t_index(g, cc)
                        if cc == g:
                            freed[u] = (dense_done, n + kk + 1)
                            act.wait_ge(dense_done, n + kk + 1)
                            act.activation(h_hi[:, 2 * p + hp, g * 256:g * 256 + 256], dpad[:, (nn + kk) % 2, 0:256],
                                           ACT.Copy).then_inc(o_rounded, 1)
                            kk += 1
                        else:
                            freed[u] = (v_done, v0 + g * (g - 1) // 2 + cc + 1)
                    elif st[0] == "S":
                        i = st[1]
                        act.wait_ge(m_ok, e0 + i + 1)
                        if i >= 4:
                            act.wait_ge(t_done, u0 + t_index(i // 2 - 2, i // 2 - 2) + 1)
                        elif not first:
                            act.wait_ge(t_done, u0 - T_GROUPS + t_index(i // 2 + 2, i // 2 + 2) + 1)
                        act.activation(prob[:, i % 4, 0:(i + 1) * P],
                                       spad_flat[:, SBANK[i] * 512:SBANK[i] * 512 + (i + 1) * P], ACT.Exp,
                                       bias=neg_max[:, i:i + 1], scale=MLA_SCALE, accum_out=row_sum[:, i:i + 1])\
                            .then_inc(e_done, 1)
                    elif st[0] == "T":
                        _, g, cc = st
                        u = t_index(g, cc)
                        w = 384 if cc == g else 512
                        act.wait_ge(t_done, u0 + u + 1)
                        if u >= 2:
                            act.wait_ge(*freed[u - 2])
                        elif not first:
                            act.wait_ge(v_done, v0)
                            act.wait_ge(dense_done, n - 2)
                        act.activation(pt_hi[:, u % 2, 0:w], tpad[:, u % 2, 0:w], ACT.Copy).then_inc(t_rounded, 1)
                    elif st[0] == "Q":
                        if hp == 0:
                            proj_q(n + kk, nn + kk, 1, p, False)
                            kk += 4
                            split_after(T_HEAD + 3 * p + 3, dense_done, n + kk)
                            split_after(T_HEAD + 3 * p + 4, dense_done, n + kk)
                        elif more:
                            proj_q(n + kk, nn + kk, 0, p + 1, True)
                            kk += 6
                    elif st[0] == "W":
                        if hp == 0 or more:
                            proj_v(n + kk, nn + kk)
                            kk += 2
                        if hp == 0:
                            split_after(T_HEAD + 3 * p + 5, dense_done, n + kk)

            act.wait_ge(ada_used, 6 * KC)
            proj_q(N_HEAD0, N_HEAD0, 0, 0, True)
            proj_v(N_HEAD0 + 6, N_HEAD0 + 6)
            for p in range(HEADS // 2):
                head(p, 0, p == 0, True)
                head(p, 1, False, p < HEADS // 2 - 1)

            def ln_squares(L):
                th = L % 2
                for c in range(KC):
                    act.wait_ge(ln_cent, KC * L + c + 1)
                    if c >= 2:
                        act.wait_ge(ln_part, 7 * L + c - 1)
                    act.activation(ln_sq[:, c % 2, :], x[:, c, halves(th)], ACT.Square).then_inc(ln_sqr, 1)

            def ln_root(L):
                act.wait_ge(stat_col, 4 + L + 1)
                act.activation(stds[:, 0, :], tpad[:, 0, 0:4], ACT.Sqrt, scale=1.0 / D, bias=freq[:, 3:4])\
                    .then_inc(stat_std, 1)

            def ln_outputs(L, last):
                th = L % 2
                for c in range(KC):
                    xc = x[:, c, halves(th)]
                    if not last:
                        act.wait_ge(h32_ok, KC * L + c + 1)
                        act.activation(h_hi[:, c, halves(th)], h32[:, c % 2, :], ACT.Copy).then_inc(h_rounded, 1)
                    else:
                        act.wait_ge(ln_z, KC * L + c + 1)
                    act.activation(xc, xc, ACT.Identity, scale=vecs[:, 2, c:c + 1], bias=vecs[:, 3, c:c + 1])\
                        .then_inc(ln_res, 1)

            def ln(L, last=False):
                ln_squares(L)
                ln_root(L)
                ln_outputs(L, last)

            ln_eps = freq[:, 3:4]

            def out_proj(layer):
                for th in range(NT):
                    for c in range(KC):
                        s = KC * th + c
                        split_after(T_WO[layer] + s + RING, dense_done, N_WO[layer] + s + 1)
                        if th == 1:
                            L = 4 * layer
                            if c == 1:
                                ln_squares(L)
                            elif c == 3:
                                ln_root(L)
                            elif c == 5:
                                ln_outputs(L, False)
                ln(4 * layer + 1)

            def feed_forward(layer):
                jb = 44 * layer

                def turn(i, first, last):
                    T = T_FFN[layer] + 6 * i
                    T0 = T_FFN[layer]
                    j0 = jb + 4 * i

                    def next_split(k, done, value):
                        if last and layer == DEPTH - 1 and k >= 6:
                            return
                        act.wait_ge(done, value)
                        split(T0 + k, D, i)

                    def silu(s):
                        act.wait_ge(gate_done, j0 + s + 1)
                        if not (first and s < 2):
                            act.wait_ge(f32_ok, j0 + s - 1)
                        act.activation(gate_s[:, s % 2, :], spad[:, s % 2, :], ACT.Silu).then_inc(silu_ok, 1)

                    def hi(s):
                        act.wait_ge(f32_ok, j0 + s + 1)
                        act.activation(f_hi[:, s // 2, halves(s % 2)], f32[:, s % 2, :], ACT.Copy)\
                            .then_inc(f_rounded, 1)

                    silu(0)
                    hi(0)
                    silu(1)
                    next_split(3, gate_done, j0 + 2)
                    hi(1)
                    next_split(4, up_done, j0 + 2)
                    silu(2)
                    hi(2)
                    silu(3)
                    next_split(5, gate_done, j0 + 4)
                    hi(3)
                    next_split(6, up_done, j0 + 4)
                    next_split(7, dense_done, N_FFN[layer] + 16 * i + 16)
                    next_split(8, dense_done, N_FFN[layer] + 16 * i + 16)

                turn(0, True, False)
                with act.Fori(1, ITERS - 1) as i:
                    turn(i, False, False)
                turn(ITERS - 1, False, True)
                ln(4 * layer + 2, layer == DEPTH - 1)
                ln(4 * layer + 3, layer == DEPTH - 1)

            out_proj(0)
            feed_forward(0)

            def qkv(th):
                for k in range(12):
                    n = N_QKV + 28 * th + k
                    m = 12 * th + k
                    if k in (2, 3):
                        act.wait_ge(dense_free, n + 1)
                    else:
                        act.wait_ge(rot_ok, 10 * th + (k if k < 2 else k - 2) + 1)
                    if k < 2:
                        for part in range(2):
                            rows = slice(64 * part, 64 * part + 64)
                            for dst in range(2):
                                act.activation(sk_hi[64 * dst:64 * dst + 64, 2 * k + part, halves(th)],
                                               sr_out[rows, m % 2, :], ACT.Copy).then_inc(rot_rounded, 1)
                    elif k < 4:
                        act.activation(sv_hi[:, 4 * th:4 * th + 4, (k - 2) * P:(k - 1) * P],
                                       sr_out[:, m % 2, :].rearrange("p (t v) -> p t v", t=4), ACT.Copy)\
                            .then_inc(rot_rounded, 1)
                    else:
                        c = k - 4
                        if k == 4 and th == 0:
                            act.wait_ge(spilled, 16 * NT)
                        act.activation(sq_st[0:64, 2 * c, :], sr_out[0:64, m % 2, :], ACT.Copy).then_inc(rot_rounded, 1)
                        act.activation(sq_st[64:P, 2 * c + 1, :], sr_out[64:P, m % 2, :], ACT.Copy)\
                            .then_inc(rot_rounded, 1)
                    split_after(T_QKV + 12 * th + k + RING, dense_done, n + 1)

            def s_exp(r):
                b = r // WKV
                lo = 0 if b else P
                act.wait_ge(sm_ok, r + 1)
                if r >= 2:
                    act.wait_ge(st_done, r - 1)
                sl = 4 * (r % 2)
                act.activation(sink_e[:, sl:sl + GRP], sink_e[:, sl:sl + GRP], ACT.Exp)
                for g in range(GRP):
                    mm = act.activation(sprob[:, r % 2, g, lo:2 * P],
                                        spad[:, 2 * (r % 2) + g // 2, (g % 2) * 256 + lo:(g % 2) * 256 + 256], ACT.Exp,
                                        bias=neg_max[:, sl + g:sl + g + 1], scale=SWA_SCALE,
                                        accum_out=row_sum[:, sl + g:sl + g + 1])
                mm.then_inc(se_done, 1)

            def s_out(r):
                b, j = divmod(r, WKV)
                n = N_QKV + 12 + 28 * (b // 4) + r % 16
                act.wait_ge(dense_done, n + 1)
                src = dpad[0:WD, n % 2, :].rearrange("p (c e q) -> p c e q", c=2, e=2)
                for e in range(2):
                    act.activation(h_hi[64 * e:64 * e + 64, 2 * j:2 * j + 2, b * P:b * P + P], src[:, :, e, :], ACT.Copy)\
                        .then_inc(so_rounded, 1)

            for th in range(NT):
                qkv(th)
                for r in range(16 * th, 16 * th + 16):
                    if r == 16 * th:
                        s_exp(r)
                    if r + 1 < 16 * th + 16:
                        s_exp(r + 1)
                    act.wait_ge(st_done, r + 1)
                    if r:
                        n_prev = N_QKV + 12 + 28 * ((r - 1) // 16) + (r - 1) % 16
                        act.wait_ge(dense_done, n_prev + 1)
                    lo = 0 if r // WKV else 1
                    act.activation(spt_hi[:, lo:2, :], tpad[:, lo:2, :], ACT.Copy).then_inc(st_rounded, 1)
                    s_out(r)

            out_proj(1)
            feed_forward(1)

        @block.vector
        def _(dve):
            own = Chain(dve, dve_own)

            def split(T, width=D, turn=0):
                sl = T % RING
                dve.wait_ge(w_rounded, T + 1 + 6 * turn)
                dve.tensor_tensor(w_lo[:, sl, 0:width], w_raw[:, sl, 0:width], w_hi[:, sl, 0:width].bitcast(F32),
                                  ALU.subtract).then_inc(w_split, 1)

            def split_if(T):
                if T < T_END:
                    split(T, tile_width(T))

            def add_ada(u):
                v, kc = u // KC, u % KC
                dve.wait_ge(ada_in[u % 3], 16 * (u // 3 + 1))
                acc = ada_acc[:, v % 2, :]
                if kc == 0:
                    if v >= 2:
                        dve.wait_ge(ada_fold, v - 1)
                    dve.tensor_scalar(acc, ada_raw[:, u % 3, :], cond[:, 0:1], None, ALU.mult).then_inc(ada_used, 1)
                else:
                    dve.wait_ge(ada_used, u)
                    dve.scalar_tensor_tensor(acc, ada_raw[:, u % 3, :], cond[:, kc:kc + 1], acc, ALU.mult, ALU.add)\
                        .then_inc(ada_used, 1)

            def finish_mod(layer, v, psum):
                dve.wait_ge(ada_fold, 6 * layer + v + 1)
                dve.tensor_tensor(mod[:, layer, v, :], psum[:, v * KC:v * KC + KC], ada_b[:, layer, v, :], ALU.add)\
                    .then_inc(mod_ok, 1)

            def split_h(idx, c, src, th):
                dve.wait_ge(h_rounded, idx + 1)
                dve.tensor_tensor(h_lo[:, c, halves(th)], src, h_hi[:, c, halves(th)].bitcast(F32), ALU.subtract)\
                    .then_inc(h_split, 1)

            dve.wait_ge(cond_ok, 1)
            for u in range(2 * KC):
                add_ada(u)
            finish_mod(0, 0, spad[:, 3, :])
            finish_mod(0, 1, spad[:, 3, :])
            dve.wait_ge(mod_ok, 2)
            own(dve.tensor_scalar(vecs[:, 0, :], mod[:, 0, 1, :], 1.0, None, ALU.add))
            for th in range(NT):
                dve.wait_ge(x_in[th], 16)
                for c in range(KC + 1):
                    if c < KC:
                        if KC * th + c >= 2:
                            dve.wait_ge(h_split, KC * th + c - 1)
                        dve.tensor_scalar(h32[:, c % 2, :], x[:, c, halves(th)], vecs[:, 0, c:c + 1],
                                          mod[:, 0, 0, c:c + 1], ALU.mult, ALU.add).then_inc(h32_in, 1)
                    if c:
                        split_h(KC * th + c - 1, c - 1, h32[:, (c - 1) % 2, :], th)
                if th == 0:
                    for T in range(RING):
                        split(T)

            def inverse_diag(z, diag):
                dve.wait_ge(stat_std, z + 1)
                own(dve.reciprocal(stds[:, 1, :], stds[:, 0, :]))
                for t in range(4):
                    ins = dve.tensor_scalar(diag[:, t, :], ident32, stds[:, 1, t:t + 1], None, ALU.mult)
                ins.then_inc(stat_diag, 1)

            def rotate(n, n0, cos, sin, out, tmp, bias=None):
                ps = dpad[:, n0 % 2, :]
                dve.wait_ge(dense_done, n + 1)
                for qd in range(4):
                    a = slice(32 * qd, 32 * qd + 32)
                    b = slice(32 * (qd ^ 1), 32 * (qd ^ 1) + 32)
                    if bias is None:
                        own.tick(dve.tensor_tensor(tmp[a, :], ps[b, :], sin[b, :], ALU.mult))
                    else:
                        own.tick(dve.scalar_tensor_tensor(tmp[a, :], ps[b, :], bias[b, :], sin[b, :], ALU.add, ALU.mult))
                if bias is None:
                    dve.tensor_tensor(out, ps, cos, ALU.mult).then_inc(dense_free, 1)
                else:
                    dve.scalar_tensor_tensor(out, ps, bias, cos, ALU.add, ALU.mult).then_inc(dense_free, 1)
                own.wait()
                dve.wait_ge(dense_free, n + 1)
                return dve.tensor_tensor(out, out, tmp, ALU.add)

            u = 2 * KC
            normed = 0
            folded = 2
            for step in lat_steps():
                if step[0] == "E":
                    _, th, m = step
                    n = N_LAT + 6 * th + m
                    if m:
                        j = 5 * th + m - 1
                        dve.wait_ge(sq_ok, j + 1)
                        if th:
                            dve.wait_ge(lat_split, 2 if m <= KVC else 5)
                        dve.tensor_copy(lat32[:, m - 1, :], dpad[:, n % 2, :]).then_inc(dense_free, 1)
                        if m in (1, 3):
                            if j:
                                dve.wait_ge(stat_col, 2 * th + (m == 3))
                            dve.tensor_copy(lat_ss[:], lat_sq[:, j % 2, :]).then_inc(ss_ok, 1)
                        else:
                            dve.wait_ge(ss_ok, j)
                            dve.tensor_tensor(lat_ss[:], lat_ss[:], lat_sq[:, j % 2, :], ALU.add).then_inc(ss_ok, 1)
                    else:
                        if th == 0:
                            dve.wait_ge(tab_out, 16 * 8)
                        rotate(n, n, cos0[:, halves(th)], sin0[:, halves(th)], ln_sq[:, 0, :], ln_sq[:, 1, :])\
                            .then_inc(kr_ok, 1)
                        dve.wait_ge(kr_rounded, th + 1)
                        dve.tensor_tensor(kr_lo[:, halves(th)], ln_sq[:, 0, :], kr_hi[:, halves(th)].bitcast(F32),
                                          ALU.subtract).then_inc(kr_split, 1)
                    split_if(T_LAT + n + RING)
                    for _ in range(3):
                        if u < 6 * KC:
                            add_ada(u)
                            u += 1
                    if n in (6, 8, 10):
                        finish_mod(0, (2, 3, 4)[(n - 6) // 2], spad[:, 3, :])
                elif step[0] == "C":
                    inverse_diag(step[1], diag0)
                else:
                    z = step[1]
                    dve.wait_ge(stat_row, z + 1)
                    ms = ((0, 1), (2, 3, 4))[z % 2]
                    dve.wait_ge(dense_free, N_LAT + 6 * (z // 2) + (3, 6)[z % 2])
                    for m in ms:
                        dve.scalar_tensor_tensor(lat32[:, m, :], lat32[:, m, :], lat_g[:, m:m + 1], tpad[:, 1, :],
                                                 ALU.mult, ALU.mult).then_inc(lat_ok, 1)
                    for m in ms:
                        normed += 1
                        dve.wait_ge(lat_rounded, normed)
                        dve.tensor_tensor(lat_lo[:, m, halves(z // 2)], lat32[:, m, :],
                                          lat_hi[:, m, halves(z // 2)].bitcast(F32), ALU.subtract).then_inc(lat_split, 1)
            finish_mod(0, 5, spad[:, 3, :])

            def proj_q(n, n0, hp, p, rotary):
                hr = 12 * p + 6 * hp
                for th in range(NT):
                    dve.wait_ge(head_rounded, hr + th + 1)
                    dve.tensor_tensor(q_lo[:, halves(th)], dpad[:, (n0 + th) % 2, :], q_hi[:, halves(th)].bitcast(F32),
                                      ALU.subtract).then_inc(dense_free, 1)
                for th in range(NT):
                    dve.wait_ge(head_rounded, hr + th + 3)
                    dve.tensor_tensor(k_lo[:, halves(th)], dpad[:, (n0 + th) % 2, :], k_hi[:, halves(th)].bitcast(F32),
                                      ALU.subtract).then_inc(dense_free, 1)
                if rotary:
                    for th in range(NT):
                        rotate(n + 4 + th, n0 + th, rcos[:, halves(th)], rsin[:, halves(th)], rt_out[:, th, :],
                               rt_tmp[:]).then_inc(rope_ok, 1)
                        dve.wait_ge(rope_rounded, 4 * p + 2 * th + 2)
                        own.tick(dve.tensor_tensor(qr[64:P, 0, halves(th)], rt_out[0:64, th, :],
                                                   qr[0:64, 0, halves(th)].bitcast(F32), ALU.subtract))
                        dve.tensor_tensor(qr[0:64, 1, halves(th)], rt_out[64:P, th, :],
                                          qr[64:P, 1, halves(th)].bitcast(F32), ALU.subtract).then_inc(rope_ok, 1)
                        dve.wait_ge(rope_ok, 4 * p + 2 * th + 2)

            def proj_v(hr, n0):
                for part in range(2):
                    dve.wait_ge(head_rounded, hr + part + 1)
                    tiles = slice(4 * part, 4 * part + 4)
                    dve.tensor_tensor(v_lo[:, tiles, :].rearrange("p t v -> p (t v)"), dpad[:, (n0 + part) % 2, :],
                                      v_hi[:, tiles, :].rearrange("p t v -> p (t v)").bitcast(F32), ALU.subtract)\
                        .then_inc(dense_free, 1)

            def head(p, hp, first, more):
                e0 = 16 * p + 8 * hp
                u0 = 2 * T_GROUPS * p + T_GROUPS * hp
                n = N_PAIR + PAIR_STEPS * p + 10 * hp
                nn = N_PAIR + 10 * hp
                hr = 12 * p + 6 * hp
                kk = 0
                for st in HEAD_STEPS:
                    if st[0] == "S":
                        i = st[1]
                        dve.wait_ge(s_done, e0 + i + 1)
                        own(dve.tensor_reduce(row_max[:, i:i + 1],
                                              spad_flat[:, SBANK[i] * 512:SBANK[i] * 512 + (i + 1) * P], AX, ALU.max))
                        dve.tensor_scalar(neg_max[:, i:i + 1], row_max[:, i:i + 1], -MLA_SCALE, None, ALU.mult)\
                            .then_inc(m_ok, 1)
                    elif st[0] == "N":
                        i = st[1]
                        dve.wait_ge(e_done, e0 + i + 1)
                        own(dve.reciprocal(row_inv[:, i:i + 1], row_sum[:, i:i + 1]))
                        dve.tensor_scalar(prob[:, i % 4, 0:(i + 1) * P], prob[:, i % 4, 0:(i + 1) * P],
                                          row_inv[:, i:i + 1], None, ALU.mult).then_inc(p_ok, 1)
                    elif st[0] == "T":
                        _, g, cc = st
                        uu = t_index(g, cc)
                        w = 384 if cc == g else 512
                        dve.wait_ge(t_rounded, u0 + uu + 1)
                        dve.tensor_tensor(pt_lo[:, uu % 2, 0:w], tpad[:, uu % 2, 0:w], pt_hi[:, uu % 2, 0:w].bitcast(F32),
                                          ALU.subtract).then_inc(t_split, 1)
                    elif st[0] == "V":
                        _, g, cc = st
                        if cc == g:
                            dve.wait_ge(o_rounded, 8 * p + 4 * hp + g + 1)
                            cols = slice(g * 256, g * 256 + 256)
                            dve.tensor_tensor(h_lo[:, 2 * p + hp, cols], dpad[:, (nn + kk) % 2, 0:256],
                                              h_hi[:, 2 * p + hp, cols].bitcast(F32), ALU.subtract)\
                                .then_inc(dense_free, 1)
                            kk += 1
                    elif st[0] == "Q":
                        if hp == 0:
                            proj_q(n + kk, nn + kk, 1, p, False)
                            kk += 4
                            split_if(T_HEAD + 3 * p + 3)
                            split_if(T_HEAD + 3 * p + 4)
                        elif more:
                            proj_q(n + kk, nn + kk, 0, p + 1, True)
                            kk += 6
                    elif st[0] == "W":
                        if hp == 0 or more:
                            proj_v(hr + 6 + 4, nn + kk)
                            kk += 2
                        if hp == 0:
                            split_if(T_HEAD + 3 * p + 5)

            dve.wait_ge(tab_in, 32)
            proj_q(N_HEAD0, N_HEAD0, 0, 0, True)
            proj_v(4, N_HEAD0 + 6)
            for p in range(HEADS // 2):
                head(p, 0, p == 0, True)
                head(p, 1, False, p < HEADS // 2 - 1)

            def norm_vectors(q):
                g, b = ln_gb[:, q, 0, :], ln_gb[:, q, 1, :]
                if q:
                    dve.wait_ge(ln_res, res_floor(q))
                    dve.wait_ge(vec_ok, q)
                if q == 3:
                    own(dve.tensor_copy(vecs[:, 2, :], g))
                    dve.tensor_copy(vecs[:, 3, :], b).then_inc(vec_ok, 1)
                    return
                layer, sh = ((0, 3), (1, 0), (1, 3))[q]
                dve.wait_ge(mod_ok, 6 * (layer + 1))
                own(dve.tensor_scalar(vtmp[:, 0, :], mod[:, layer, sh + 1, :], 1.0, None, ALU.add))
                own(dve.tensor_tensor(vecs[:, 0, :], g, vtmp[:, 0, :], ALU.mult))
                own(dve.tensor_tensor(vtmp[:, 1, :], b, vtmp[:, 0, :], ALU.mult))
                own(dve.tensor_tensor(vecs[:, 1, :], vtmp[:, 1, :], mod[:, layer, sh, :], ALU.add))
                own(dve.tensor_scalar(vecs[:, 2, :], g, ALPHA, None, ALU.mult))
                if q == 1:
                    own(dve.tensor_tensor(vtmp[:, 0, :], wo_b[:], mod[:, 1, 2, :], ALU.mult))
                    dve.scalar_tensor_tensor(vecs[:, 3, :], b, ALPHA, vtmp[:, 0, :], ALU.mult, ALU.add)\
                        .then_inc(vec_ok, 1)
                else:
                    dve.tensor_scalar(vecs[:, 3, :], b, ALPHA, None, ALU.mult).then_inc(vec_ok, 1)

            def ln_total(L):
                c0 = halves(L % 2)
                if L % 2 == 0:
                    norm_vectors(L // 2)
                if L:
                    dve.wait_ge(stat_col, 4 + L)
                own(dve.tensor_tensor(ln_s[:], x[:, 0, c0], x[:, 1, c0], ALU.add))
                for c in range(2, KC):
                    ins = dve.tensor_tensor(ln_s[:], ln_s[:], x[:, c, c0], ALU.add)
                    if c < KC - 1:
                        own(ins)
                    else:
                        ins.then_inc(ln_sum, 1)

            def ln_center(L):
                c0 = halves(L % 2)
                dve.wait_ge(ln_mean, L + 1)

                def add_square(c):
                    dve.wait_ge(ln_sqr, KC * L + c + 1)
                    if c == 0:
                        dve.tensor_copy(ln_s[:], ln_sq[:, 0, :]).then_inc(ln_part, 1)
                    else:
                        dve.wait_ge(ln_part, 7 * L + c)
                        dve.tensor_tensor(ln_s[:], ln_s[:], ln_sq[:, c % 2, :], ALU.add)\
                            .then_inc(ln_part if c < KC - 1 else ln_sqsum, 1)

                for c in range(KC + 1):
                    if c < KC:
                        dve.scalar_tensor_tensor(x[:, c, c0], tpad[:, 1, :], -1.0 / D, x[:, c, c0], ALU.mult, ALU.add)\
                            .then_inc(ln_cent, 1)
                    if c:
                        add_square(c - 1)

            def ln_inverse(L):
                inverse_diag(4 + L, ln_sq[:, 0, :].rearrange("p (t c) -> p t c", t=4))

            def ln_scale(L, last):
                c0 = halves(L % 2)
                dve.wait_ge(stat_row, 4 + L + 1)
                dve.wait_ge(ln_cent, KC * (L + 1))
                for c in range(KC + 2):
                    if c < KC:
                        dve.tensor_tensor(x[:, c, c0], x[:, c, c0], tpad[:, 1, :], ALU.mult).then_inc(ln_z, 1)
                    if c >= 2 and not last:
                        split_h(16 + KC * L + c - 2, c - 2, h32[:, c % 2, :], L % 2)

            def add_out(layer, n, n0, c, th, which):
                dve.wait_ge(dense_done, n + 1)
                dve.scalar_tensor_tensor(x[:, c, halves(th)], dpad[:, n0 % 2, :], mod[:, layer, which, c:c + 1],
                                         x[:, c, halves(th)], ALU.mult, ALU.add).then_inc(dense_free, 1)

            def out_proj(layer):
                for th in range(NT):
                    for c in range(KC):
                        s = KC * th + c
                        n = N_WO[layer] + s
                        if layer == 0:
                            dve.wait_ge(res_scaled, s + 1)
                        else:
                            dve.wait_ge(res_in[th], 32)
                        add_out(layer, n, n, c, th, 2)
                        split_if(T_WO[layer] + s + RING)
                        if s == KC - 1:
                            dve.wait_ge(dense_free, n + 1)
                            ln_total(4 * layer)
                        if th == 1:
                            L = 4 * layer
                            if c == 1:
                                ln_center(L)
                            elif c == 3:
                                ln_inverse(L)
                            elif c == 5:
                                ln_scale(L, False)
                dve.wait_ge(dense_free, N_WO[layer] + NT * KC)
                L = 4 * layer + 1
                ln_total(L)
                ln_center(L)
                ln_inverse(L)
                ln_scale(L, False)

            def feed_forward(layer):
                jb = 44 * layer

                def turn(i, first, last):
                    T = T_FFN[layer] + 6 * i
                    T0 = T_FFN[layer]
                    j0 = jb + 4 * i

                    def next_split(k):
                        if last and layer == DEPTH - 1 and k >= 6:
                            return
                        split(T0 + k, D, i)

                    def product(s):
                        dve.wait_ge(up_done, j0 + s + 1)
                        dve.wait_ge(silu_ok, j0 + s + 1)
                        if not (first and s < 2):
                            dve.wait_ge(f_split, j0 + s - 1)
                        dve.tensor_tensor(f32[:, s % 2, :], spad[:, 2 + s % 2, :], gate_s[:, s % 2, :], ALU.mult)\
                            .then_inc(f32_ok, 1)

                    def lo(s):
                        dve.wait_ge(f_rounded, j0 + s + 1)
                        part = halves(s % 2)
                        dve.tensor_tensor(f_lo[:, s // 2, part], f32[:, s % 2, :], f_hi[:, s // 2, part].bitcast(F32),
                                          ALU.subtract).then_inc(f_split, 1)

                    product(0)
                    lo(0)
                    next_split(3)
                    product(1)
                    lo(1)
                    next_split(4)
                    product(2)
                    lo(2)
                    next_split(5)
                    product(3)
                    lo(3)
                    next_split(6)
                    for th in range(NT):
                        for c in range(KC):
                            k = KC * th + c
                            n = N_FFN[layer] + 16 * i + k
                            if first:
                                dve.wait_ge(ln_res, 16 * (2 * layer) + k + 1)
                            else:
                                dve.wait_ge(dense_free, n - 15)
                            add_out(layer, n, N_FFN[layer] + k, c, th, 5)
                        if last and th == 0:
                            dve.wait_ge(dense_free, N_FFN[layer] + 16 * i + KC)
                            ln_total(4 * layer + 2)
                    next_split(7)
                    next_split(8)

                turn(0, True, False)
                with dve.Fori(1, ITERS - 1) as i:
                    turn(i, False, False)
                if layer == 0:
                    for v in range(6):
                        finish_mod(1, v, tpad[:, 0, :])
                turn(ITERS - 1, False, True)
                L = 4 * layer + 2
                last = layer == DEPTH - 1
                ln_center(L)
                ln_inverse(L)
                ln_scale(L, last)
                dve.wait_ge(dense_free, N_FFN[layer] + 16 * ITERS)
                ln_total(L + 1)
                ln_center(L + 1)
                ln_inverse(L + 1)
                ln_scale(L + 1, last)

            out_proj(0)
            feed_forward(0)

            def qkv(th):
                for k in range(12):
                    n = N_QKV + 28 * th + k
                    m = 12 * th + k
                    out = sr_out[:, m % 2, :]
                    if m >= 2 and k >= 6:
                        dve.wait_ge(rot_split, 16 * th + 2 * (k - 5))
                    if k < 2 or k >= 4:
                        if k == 0:
                            dve.wait_ge(tab_in, 64)
                            if th == 0:
                                dve.wait_ge(h_split, 48)
                            else:
                                dve.wait_ge(st_done, 16 * th)
                        bcol = k if k < 2 else k - 2
                        if k in (4, 5):
                            dve.wait_ge(sv_split, 2 * th + k - 3)
                        rotate(n, n, scos[:, halves(th)], ssin[:, halves(th)], out, sr_tmp[:], qk_b[:, bcol:bcol + 1])\
                            .then_inc(rot_ok, 1)
                        dve.wait_ge(rot_ok, 10 * th + bcol + 1)
                        if k < 2:
                            dve.wait_ge(rot_rounded, 26 * th + 4 * k + 4)
                            for part in range(2):
                                rows = slice(64 * part, 64 * part + 64)
                                other = slice(64 - 64 * part, P - 64 * part)
                                kv = 2 * k + part
                                dve.tensor_tensor(sk_lo[rows, kv, halves(th)], sr_out[rows, m % 2, :],
                                                  sk_hi[rows, kv, halves(th)].bitcast(F32), ALU.subtract)\
                                    .then_inc(k_stack, 1)
                                dve.tensor_tensor(sk_lo[other, kv, halves(th)], sr_out[rows, m % 2, :],
                                                  sk_hi[rows, kv, halves(th)].bitcast(F32), ALU.subtract)\
                                    .then_inc(k_stack, 1)
                    else:
                        dve.wait_ge(vbias_in, 16 * (th + 1))
                        dve.wait_ge(k_stack, 8 * (th + 1))
                        dve.wait_ge(dense_done, n + 1)
                        bias = sv_b[:, (k - 2) * P:(k - 1) * P].unsqueeze(1).to_broadcast([P, 4, P])
                        dve.tensor_tensor(out.rearrange("p (t v) -> p t v", t=4),
                                          dpad[:, n % 2, :].rearrange("p (t v) -> p t v", t=4), bias, ALU.add)\
                            .then_inc(dense_free, 1)
                        dve.wait_ge(rot_rounded, 26 * th + 8 + (k - 1))
                        dve.tensor_tensor(sv_lo[:, 4 * th:4 * th + 4, (k - 2) * P:(k - 1) * P],
                                          out.rearrange("p (t v) -> p t v", t=4),
                                          sv_hi[:, 4 * th:4 * th + 4, (k - 2) * P:(k - 1) * P].bitcast(F32),
                                          ALU.subtract).then_inc(sv_split, 1)
                    split_if(T_QKV + 12 * th + k + RING)

            def s_max(r):
                b, j = divmod(r, WKV)
                lo = 0 if b else P
                sl = 4 * (r % 2)
                cols = slice(sl, sl + GRP)
                dve.wait_ge(ss_done, r + 1)
                src = spad[:, 2 * (r % 2):2 * (r % 2) + 2, :].rearrange("p b (g k) -> p (b g) k", g=2)[:, :, lo:2 * P]
                own(dve.tensor_reduce(row_max[:, cols], src, AX, ALU.max))
                own(dve.scalar_tensor_tensor(row_max[:, cols], row_max[:, cols], SWA_SCALE, sinks[:, GRP * j:GRP * j + GRP],
                                             ALU.mult, ALU.max))
                own(dve.tensor_scalar(neg_max[:, cols], row_max[:, cols], -1.0, None, ALU.mult))
                dve.tensor_tensor(sink_e[:, cols], sinks[:, GRP * j:GRP * j + GRP], neg_max[:, cols], ALU.add)\
                    .then_inc(sm_ok, 1)

            def s_norm(r):
                lo = 0 if r // WKV else P
                sl = 4 * (r % 2)
                cols = slice(sl, sl + GRP)
                dve.wait_ge(se_done, r + 1)
                own(dve.tensor_tensor(row_sum[:, cols], row_sum[:, cols], sink_e[:, cols], ALU.add))
                own(dve.reciprocal(row_inv[:, cols], row_sum[:, cols]))
                for g in range(GRP):
                    pr = sprob[:, r % 2, g, lo:2 * P]
                    ins = dve.tensor_scalar(pr, pr, row_inv[:, sl + g:sl + g + 1], None, ALU.mult)
                ins.then_inc(sp_ok, 1)

            def s_out(r):
                b, j = divmod(r, WKV)
                n = N_QKV + 12 + 28 * (b // 4) + r % 16
                src = dpad[0:WD, n % 2, :].rearrange("p (c e q) -> p c e q", c=2, e=2)
                dve.wait_ge(so_rounded, 2 * r + 2)
                for e in range(2):
                    rows, cs, cols = slice(64 * e, 64 * e + 64), slice(2 * j, 2 * j + 2), slice(b * P, b * P + P)
                    ins = dve.tensor_tensor(h_lo[rows, cs, cols], src[:, :, e, :], h_hi[rows, cs, cols].bitcast(F32),
                                            ALU.subtract)
                ins.then_inc(dense_free, 1)

            for th in range(NT):
                qkv(th)
                for r in range(16 * th, 16 * th + 16):
                    if r == 16 * th:
                        s_max(r)
                    if r + 1 < 16 * th + 16:
                        s_max(r + 1)
                    s_norm(r)
                    dve.wait_ge(st_rounded, r + 1)
                    lo = 0 if r // WKV else 1
                    dve.tensor_tensor(spt_lo[:, lo:2, :], tpad[:, lo:2, :], spt_hi[:, lo:2, :].bitcast(F32), ALU.subtract)\
                        .then_inc(st_split, 1)
                    s_out(r)

            out_proj(1)
            feed_forward(1)

        @block.gpsimd
        def _(pool):
            own = Chain(pool, pool_own)
            pool.memset(ones[:], 1.0).then_inc(consts, 1)
            pool.memset(tab_t[:, 0:3 * P], 0.0).then_inc(consts, 1)
            pool.wait_ge(consts, 2)
            pool.affine_select(out=tab_t[:, 0:P], in_=tab_t[:, 0:P], compare_op=ALU.not_equal, fill=1.0, base=0,
                               pattern=[[-1, P]], channel_multiplier=1).then_inc(consts, 1)
            pool.affine_select(out=tab_t[:, P:2 * P], in_=tab_t[:, P:2 * P], compare_op=ALU.is_gt, fill=MASKED, base=0,
                               pattern=[[1, P]], channel_multiplier=-1).then_inc(consts, 1)
            pool.affine_select(out=tab_t[:, 2 * P:3 * P], in_=tab_t[:, 2 * P:3 * P], compare_op=ALU.is_ge, fill=MASKED,
                               base=0, pattern=[[-1, P]], channel_multiplier=1).then_inc(consts, 1)
            pool.wait_ge(ident_ok, 2)
            pool.wait_ge(pos_in, 16)
            TWO_PI_PARTS = (6.28125, 0.0019350051879882812, 3.0199159819591595e-07)
            NEAREST = 1.5 * 2.0 ** 23
            PI_BELOW = 3.1415925
            for t in range(2):
                if t:
                    pool.wait_ge(tab_trig, 2)
                own(pool.tensor_copy(tab_t[:], pos_i[:]))
                own(pool.tensor_scalar(tab_ang[:], tab_t[:], freq[:, t:t + 1], 1.0, ALU.mult, ALU.mult))
                own(pool.tensor_scalar(tab_k[:], tab_ang[:], 1.0 / (2.0 * np.pi), NEAREST, ALU.mult, ALU.add))
                own(pool.tensor_scalar(tab_k[:], tab_k[:], -NEAREST, -1.0, ALU.add, ALU.mult))
                for part in TWO_PI_PARTS:
                    own(pool.tensor_scalar(tab_t[:], tab_k[:], part, 1.0, ALU.mult, ALU.mult))
                    own(pool.tensor_tensor(tab_ang[:], tab_ang[:], tab_t[:], ALU.add))
                pool.tensor_scalar(tab_ang[:], tab_ang[:], PI_BELOW, -PI_BELOW, ALU.min, ALU.max)\
                    .then_inc(tab_ready, 1)
                pool.wait_ge(tab_trig, 2 * t + 1)
                pool.tensor_scalar(sin0[:], sin0[:], freq[:, 5:6], 1.0, ALU.mult, ALU.mult).then_inc(tab_sign, 1)

            for th in range(NT):
                pool.wait_ge(res_in[th], 16)
                for c in range(KC):
                    xc = x[:, c, halves(th)]
                    pool.tensor_scalar(xc, xc, ALPHA, 1.0, ALU.mult, ALU.mult).then_inc(res_scaled, 1)

            def modulate(L):
                pool.wait_ge(vec_ok, L // 2 + 1)
                for c in range(KC):
                    pool.wait_ge(ln_z, KC * L + c + 1)
                    pool.wait_ge(h_split, 16 + KC * L + c - 1)
                    pool.tensor_scalar(h32[:, c % 2, :], x[:, c, halves(L % 2)], vecs[:, 0, c:c + 1], vecs[:, 1, c:c + 1],
                                       ALU.mult, ALU.add).then_inc(h32_ok, 1)

            modulate(0)
            modulate(1)

            ada1 = A["ada_w"][1]

            def load_ada1(v, kc):
                pool.dma_start(ada1_raw[:, kc % 2, :], ada1[kc * P:(kc + 1) * P, v * D:(v + 1) * D])\
                    .then_inc(ada1_in[kc % 2], 16)

            pool.wait_ge(f_split, 1)
            for kc in range(2):
                load_ada1(0, kc)
            for v in range(6):
                for kc in range(KC):
                    u = v * KC + kc
                    pool.wait_ge(ada1_in[kc % 2], 16 * (u // 2 + 1))
                    raw = ada1_raw[:, kc % 2, :]
                    dst = ada1_acc[:, v, :] if kc == 0 else raw
                    pool.tensor_scalar(dst, raw, cond[:, kc:kc + 1], 1.0, ALU.mult, ALU.mult)\
                        .then_inc(ada1_scaled if kc else ada1_used, 1)
                    if kc:
                        pool.wait_ge(ada1_scaled, v * (KC - 1) + kc)
                        pool.wait_ge(ada1_used, u)
                        pool.tensor_tensor(ada1_acc[:, v, :], ada1_acc[:, v, :], raw, ALU.add).then_inc(ada1_used, 1)
                    if u + 2 < 6 * KC:
                        pool.wait_ge(ada1_used, u + 1)
                        load_ada1((u + 2) // KC, (u + 2) % KC)
            modulate(2)
            modulate(3)

            for th in range(NT):
                for c in range(8):
                    m = 12 * th + 4 + c
                    pool.wait_ge(rot_rounded, 26 * th + 10 + 2 * c + 2)
                    pool.tensor_tensor(sq_st[64:P, 2 * c, :], sr_out[0:64, m % 2, :], sq_st[0:64, 2 * c, :].bitcast(F32),
                                       ALU.subtract).then_inc(rot_split, 1)
                    pool.tensor_tensor(sq_st[0:64, 2 * c + 1, :], sr_out[64:P, m % 2, :],
                                       sq_st[64:P, 2 * c + 1, :].bitcast(F32), ALU.subtract).then_inc(rot_split, 1)
            modulate(4)
            modulate(5)



def _tiles(w):
    k, n = w.shape
    return np.ascontiguousarray(w.reshape(k // P, P, n // P, P).transpose(2, 1, 0, 3)).reshape(n // P, P, k)


def _rotary_order(w):
    w = w.reshape(w.shape[0], -1, WD)
    half = WROT // 2
    return np.concatenate([w[:, :, 0:half], w[:, :, WROT:WROT + 24], w[:, :, half:WROT], w[:, :, WROT + 24:]],
                          axis=2).reshape(w.shape[0], -1)


def _columns(v):
    v = v.reshape(v.shape[:-1] + (-1, P))
    return np.ascontiguousarray(np.moveaxis(v, -1, 0))


def kernel(**inputs):
    import concourse.bacc as bacc
    from concourse.bass_utils import run_bass_kernel_spmd

    i = {k: np.asarray(v) for k, v in inputs.items()}
    q_cols = WH * WD
    w_in = i["mla_w_in"][0]
    rope_in = w_in[:, QRANK + KVRANK:]
    w_q = i["mla_w_q_b"][0].reshape(QC, P, HEADS // 2, 2, NOPE + ROT)
    w_kv = i["mla_w_kv_b"][0].reshape(KVC, P, HEADS // 2, 2 * (NOPE + VDIM))
    w_qkv, b_qkv = i["swa_w_qkv"][0], i["swa_b_qkv"]
    k_end = q_cols + WKV * WD
    inv = np.zeros((P, 8), np.float32)
    for p in range(P):
        r = p % 32
        if r < WROT // 2:
            inv[p, 0] = np.float32(THETA) ** np.float32(-2 * r / WROT)
        inv[p, 1] = np.float32(THETA) ** np.float32(-2 * r / ROT)
        inv[p, 5] = 1.0 if (p // 32) % 2 == 0 else -1.0
    inv[:, 2], inv[:, 3], inv[:, 4] = np.pi / 2, LN_EPS, RMS_EPS
    arrays = {
        "x": np.ascontiguousarray(i["x"][0].T.reshape(KC, P, SEQ).transpose(1, 0, 2)),
        "cond": _columns(i["c"][0]),
        "pos": np.ascontiguousarray(i["positions"][0]),
        "ada_w": i["ada_w"],
        "ada_b": _columns(i["ada_b"].reshape(DEPTH, 6, D)),
        "ln_gb": _columns(np.stack([np.stack([i["ln_mix_g"], i["ln_ffn_g"]], 1), np.stack([i["ln_mix_b"], i["ln_ffn_b"]], 1)],
                                   2).reshape(4, 2, D)),
        "lat_g": np.concatenate([_columns(i["mla_kv_norm"][0]), _columns(i["mla_q_norm"][0])], 1),
        "qk_b": np.concatenate([_columns(_rotary_order(b_qkv[:, q_cols:k_end])[0]),
                                _columns(_rotary_order(b_qkv[:, :q_cols])[0])], 1),
        "v_b": np.ascontiguousarray(b_qkv[0, k_end:]),
        "wo_b": _columns(i["swa_b_o"][0]),
        "sinks": np.ascontiguousarray(i["swa_sinks"][0]),
        "freq": inv,
        "w_lat": _tiles(np.concatenate([rope_in, rope_in, w_in[:, QRANK:QRANK + KVRANK], w_in[:, :QRANK]], 1)),
        "w_qr": np.ascontiguousarray(w_q[..., NOPE:].transpose(2, 1, 0, 3, 4)).reshape(HEADS // 2, P, -1),
        "w_qn": np.ascontiguousarray(w_q[..., :NOPE].transpose(2, 1, 0, 3, 4)).reshape(HEADS // 2, P, -1),
        "w_kv": np.ascontiguousarray(w_kv.transpose(2, 1, 0, 3)).reshape(HEADS // 2, P, -1),
        "w_qkv": np.concatenate([_tiles(_rotary_order(w_qkv[:, q_cols:k_end])), _tiles(w_qkv[:, k_end:]),
                                 _tiles(_rotary_order(w_qkv[:, :q_cols]))], 0),
        "w_o": np.stack([_tiles(i["mla_w_o"][0]), _tiles(i["swa_w_o"][0])]),
        "w_gt": np.stack([_tiles(w) for w in i["ffn_w_gate"]]),
        "w_up": np.stack([_tiles(w) for w in i["ffn_w_up"]]),
        "w_dn": i["ffn_w_down"].reshape(DEPTH, FC, P, D),
    }
    nc = bacc.Bacc("TRN2", target_bir_lowering=False, num_devices=1)
    A = {k: nc.dram_tensor("in_" + k, a.shape, I32 if k == "pos" else F32, kind="ExternalInput").ap() for k, a in arrays.items()}
    A["out"] = nc.dram_tensor("out", (P, KC, SEQ), F32, kind="ExternalOutput").ap()
    build(nc, A)
    got = run_bass_kernel_spmd(nc, [{"in_" + k: a for k, a in arrays.items()}], core_ids=[0]).results[0]["out"]
    return np.ascontiguousarray(got.transpose(2, 1, 0)).reshape(1, SEQ, D)
```

```python
from contextlib import ExitStack

import numpy as np

import concourse.bass as bass
from concourse import mybir

F32 = mybir.dt.float32
F32R = mybir.dt.float32r
I32 = mybir.dt.int32
ALU = mybir.AluOpType
ACT = mybir.ActivationFunctionType
AX = mybir.AxisListType.X
ds = bass.ds

P = 128
D = 1024
SEQ = 1024
KC = D // P
TH = 512
NT = SEQ // TH
HEADS, NOPE, ROT, VDIM = 8, 128, 64, 128
QRANK, KVRANK = 384, 256
QC, KVC = QRANK // P, KVRANK // P
WH, WKV, WD, WROT = 16, 4, 64, 16
GRP = WH // WKV
DFF = 2816
FC = DFF // P
ITERS = FC // 2
NB = SEQ // P
DEPTH = 2
ALPHA = (2 * DEPTH) ** 0.25
LN_EPS, RMS_EPS = 1e-5, 1e-6
THETA = 500000.0
MLA_SCALE = (NOPE + ROT) ** -0.5
SWA_SCALE = WD ** -0.5
MASKED = -1e30
RING = 3

T_LAT = 0
T_HEAD = T_LAT + NT * 6
T_WO = [T_HEAD + 3 * (HEADS // 2), 0]
T_FFN = [T_WO[0] + NT * KC, 0]
T_QKV = T_FFN[0] + 6 * ITERS
T_WO[1] = T_QKV + NT * 12
T_FFN[1] = T_WO[1] + NT * KC
T_END = T_FFN[1] + 6 * ITERS

PAIR_STEPS = 22
N_LAT = 0
N_HEAD0 = N_LAT + NT * 6
N_WO = [N_HEAD0 + PAIR_STEPS * (HEADS // 2), 0]
N_FFN = [N_WO[0] + NT * KC, 0]
N_QKV = N_FFN[0] + 16 * ITERS
N_WO[1] = N_QKV + NT * (12 + 16)
N_FFN[1] = N_WO[1] + NT * KC

PE_ORDER = ("T00 S4 S5 T10 T11 V00 S6 V10 T20 V11 Q0+ T21 V20 T22 S7 V21 V22 Q1+ K0+ T30 T31 K1+ R0+ T32 R1+ "
            "W0+ V30 V31 T33 S0+ S1+ S2+ V32 V33 S3+ W1+")
ACT_ORDER = ("S4 T10 S5 T11 V00 T20 V11 S6 Q0+ T21 T22 V22 S7 Q1+ K0+ T30 T31 K1+ X0 X1 R0+ R1+ T32 W0+ T33 "
             "S0+ S1+ V33 S2+ S3+ W1+ X2 T00+")
DVE_ORDER = ("S4 S5 N4 T10 N5 T11 V00 S6 T20 V11 N6 Q0+ T21 T22 S7 V22 N7 Q1+ K0+ T30 T31 K1+ X0 X1 R0+ R1+ L0+ L1+ "
             "T32 W0+ T33 S0+ S1+ S2+ N0+ N1+ V33 N2+ S3+ N3+ W1+ X2 T00+")
T_GROUPS = 10
SBANK = [0, 1, 2, 3, 0, 2, 0, 2]
SPREV = [(6, 2), (6, 3), (7, 3), (7, 4), (1, 3), (3, 2), (4, 2), (5, 2)]


def t_index(g, cc):
    return g * (g + 1) // 2 + cc


def head_work(order):
    for body in range(-1, HEADS + 1):
        for item in order.split():
            kind, digits, h = item[0], item[1:].rstrip("+"), body + item.endswith("+")
            if 0 <= h < HEADS and not (kind in "RL" and h % 2) and not (kind == "X" and h % 2):
                yield kind, int(digits[0]), int(digits[-1]), h


def dense_numbers():
    steps = [w for w in head_work(PE_ORDER) if w[0] in "QKRW" or (w[0] == "V" and w[1] == w[2])]
    return {w: N_HEAD0 + k for k, w in enumerate(steps)}


def parts_before(r):
    return r if r < WKV else 2 * r - WKV


def part_number(r, a):
    return parts_before(r) + (1 if a else 2)


def swa_number(r):
    return N_QKV + 12 + 28 * (r // 16) + r % 16


def lat_steps():
    out = []
    for th in range(NT):
        out.append(("E", th, 0))
        if th:
            out.append(("C", 2 * th - 1))
        out.append(("E", th, 1))
        if th:
            out.append(("B", 2 * th - 1))
        out += [("E", th, 2), ("E", th, 3), ("C", 2 * th), ("E", th, 4), ("E", th, 5), ("B", 2 * th)]
    return out + [("C", 2 * NT - 1), ("B", 2 * NT - 1)]


class Chain:

    def __init__(self, eng, sem):
        self.eng, self.sem, self.n = eng, sem, 0

    def __call__(self, ins):
        self.tick(ins)
        self.wait()

    def tick(self, ins):
        ins.then_inc(self.sem, 1)
        self.n = self.n + 1

    def wait(self):
        self.eng.wait_ge(self.sem, self.n)


def tile_width(T):
    if T_HEAD <= T < T_WO[0]:
        return (QC * P, QC * 2 * P, KVC * 4 * P)[(T - T_HEAD) % 3]
    return D


def build(nc, A):
    with ExitStack() as ctx:
        def sb(name, shape, dt=F32):
            return ctx.enter_context(nc.sbuf_tensor(name, shape, dt))

        def sem(name):
            return ctx.enter_context(nc.semaphore(name))

        ident = sb("ident", [P, P], F32R)
        ident32 = ident[:].bitcast(F32)
        ones = sb("ones", [P, P])
        band = sb("band", [P, 2, P], F32R)
        mod = sb("mod", [P, DEPTH, 6, KC])
        ada_b = sb("ada_b", [P, DEPTH, 6, KC])
        ln_gb = sb("ln_gb", [P, 4, 2, KC])
        lat_g = sb("lat_g", [P, KVC + QC])
        qk_b = sb("qk_b", [P, 10])
        wo_b = sb("wo_b", [P, KC])
        sinks = sb("sinks", [P, WH])
        neg_sinks = sb("neg_sinks", [P, WH])
        cond_in = sb("cond_in", [P, KC])
        cond = sb("cond", [P, KC])
        freq = sb("freq", [P, 8])
        vecs = sb("vecs", [P, 4, KC])
        vtmp = sb("vtmp", [P, 2, KC])
        stds = sb("stds", [P, 2, 4])
        row_max = sb("row_max", [P, 8])
        neg_max = sb("neg_max", [P, 8])
        row_sum = sb("row_sum", [P, 8])
        sink_e = sb("sink_e", [P, 8])
        row_inv = sb("row_inv", [P, 8])

        base = (nc.sbuf_base + 31) // 32 * 32
        K = 1024

        def at(name, shape, dt, kib):
            size = int(np.prod(shape[1:])) * 4
            assert base + int(kib * K) + size <= nc.sbuf_usable_end, (name, base, kib)
            return nc.alloc_sbuf_tensor_at(name, shape, dt, offset=base + int(kib * K))

        h_hi = at("h_hi", [P, KC, SEQ], F32R, 0)
        h_lo = at("h_lo", [P, KC, SEQ], F32R, 32)
        w_raw = at("w_raw", [P, RING, D], F32, 64)
        w_hi = at("w_hi", [P, RING, D], F32R, 76)
        w_lo = at("w_lo", [P, RING, D], F32R, 88)
        G = 100
        x = at("x", [P, KC, SEQ], F32, G)
        lat_hi = at("lat_hi", [P, KVC + QC, SEQ], F32R, G)
        lat_lo = at("lat_lo", [P, KVC + QC, SEQ], F32R, G + 20)
        kr_hi = at("kr_hi", [P, SEQ], F32R, G + 40)
        kr_lo = at("kr_lo", [P, SEQ], F32R, G + 44)
        q_hi = at("q_hi", [P, SEQ], F32R, G + 48)
        q_lo = at("q_lo", [P, SEQ], F32R, G + 52)
        qr = at("qr", [P, 2, SEQ], F32R, G + 56)
        k_hi = at("k_hi", [P, SEQ], F32R, G + 64)
        k_lo = at("k_lo", [P, SEQ], F32R, G + 68)
        v_hi = at("v_hi", [P, NB, VDIM], F32R, G + 72)
        v_lo = at("v_lo", [P, NB, VDIM], F32R, G + 76)
        prob = at("prob", [P, 4, SEQ], F32, G + 80)
        pt_hi = at("pt_hi", [P, 2, TH], F32R, G + 96)
        pt_lo = at("pt_lo", [P, 2, TH], F32R, G + 100)
        rt_out = at("rt_out", [P, 2, TH], F32, 24)
        rt_tmp = at("rt_tmp", [P, TH], F32, 32 + 24)
        rcos = at("rcos", [P, SEQ], F32, 28)
        rsin = at("rsin", [P, SEQ], F32, 32 + 28)
        lat32 = at("lat32", [P, KVC + QC, TH], F32, G + 80)
        lat_sq = at("lat_sq", [P, 2, TH], F32, G + 90)
        lat_ss = at("lat_ss", [P, TH], F32, G + 94)
        cos0 = at("cos0", [P, SEQ], F32, G + 96)
        sin0 = at("sin0", [P, SEQ], F32, G + 100)
        diag0 = at("diag0", [P, 4, P], F32, G + 78)
        ada_acc = at("ada_acc", [P, 2, D], F32, G + 58)
        ada_raw = at("ada_raw", [P, 3, D], F32, G + 66)
        f_hi = at("f_hi", [P, 2, SEQ], F32R, G + 32)
        f_lo = at("f_lo", [P, 2, SEQ], F32R, G + 40)
        ln_s = at("ln_s", [P, TH], F32, G + 48)
        ln_sq = at("ln_sq", [P, 2, TH], F32, G + 50)
        h32 = at("h32", [P, 2, TH], F32, G + 54)
        gate_s = at("gate_s", [P, 2, TH], F32, G + 58)
        f32 = at("f32", [P, 2, TH], F32, G + 62)
        ada1_acc = at("ada1_acc", [P, 6, D], F32, G + 66)
        ada1_raw = at("ada1_raw", [P, 2, D], F32, G + 90)
        pos_i = at("pos_i", [P, SEQ], I32, G + 80)
        tab_ang = at("tab_ang", [P, SEQ], F32, G + 84)
        tab_k = at("tab_k", [P, SEQ], F32, G + 88)
        tab_t = at("tab_t", [P, SEQ], F32, G + 92)
        sq_st = at("sq_st", [P, WH, TH], F32R, G)
        sk_hi = at("sk_hi", [P, WKV, SEQ], F32R, G + 32)
        sk_lo = at("sk_lo", [P, WKV, SEQ], F32R, G + 48)
        sv_hi = at("sv_hi", [P, NB, WKV * WD], F32R, G + 64)
        sv_lo = at("sv_lo", [P, NB, WKV * WD], F32R, G + 72)
        sprob = at("sprob", [P, 2, GRP, 2 * P], F32, G + 80)
        spt_hi = at("spt_hi", [P, 2, TH], F32R, G + 88)
        spt_lo = at("spt_lo", [P, 2, TH], F32R, G + 92)
        scos = at("scos", [P, SEQ], F32, G + 96)
        ssin = at("ssin", [P, SEQ], F32, G + 100)
        sr_out = at("sr_out", [P, 2, TH], F32, G + 80)
        sr_tmp = at("sr_tmp", [P, TH], F32, G + 84)
        sv_b = at("sv_b", [P, WKV * WD], F32, G + 86)

        spad = ctx.enter_context(nc.psum_tensor("spad", [P, 4, 512], F32))
        tpad = ctx.enter_context(nc.psum_tensor("tpad", [P, 2, 512], F32))
        dpad = ctx.enter_context(nc.psum_tensor("dpad", [P, 2, 512], F32))
        spad_flat = spad[:].rearrange("p b n -> p (b n)")

        tab_dram = nc.dram_tensor("tables", (4, P, SEQ), F32, kind="Internal").ap()
        spill = nc.dram_tensor("spill", (P, KC, SEQ), F32, kind="Internal").ap()

        const_in = sem("const_in")
        pos_in = sem("pos_in")
        x_in = [sem(f"x_in{t}") for t in range(NT)]
        w_in = [sem(f"w_in{s}") for s in range(RING)]
        ada_in = [sem(f"ada_in{s}") for s in range(3)]
        ada1_in = [sem(f"ada1_in{s}") for s in range(2)]
        tab_out = sem("tab_out")
        tab_in = sem("tab_in")
        spilled = sem("spilled")
        res_in = [sem(f"res_in{t}") for t in range(NT)]
        vbias_in = sem("vbias_in")
        stored = sem("stored")
        w_rounded = sem("w_rounded")
        w_split = sem("w_split")
        consts = sem("consts")
        ident_ok = sem("ident_ok")
        cond_ok = sem("cond_ok")
        tab_k_ok = sem("tab_k_ok")
        tab_ready = sem("tab_ready")
        tab_abs = sem("tab_abs")
        tab_trig = sem("tab_trig")
        tab_sign = sem("tab_sign")
        dense_done = sem("dense_done")
        dense_free = sem("dense_free")
        ada_used = sem("ada_used")
        ada_fold = sem("ada_fold")
        mod_ok = sem("mod_ok")
        vec_ok = sem("vec_ok")
        sq_ok = sem("sq_ok")
        ss_ok = sem("ss_ok")
        stat_col = sem("stat_col")
        stat_std = sem("stat_std")
        stat_diag = sem("stat_diag")
        stat_row = sem("stat_row")
        lat_ok = sem("lat_ok")
        lat_rounded = sem("lat_rounded")
        lat_split = sem("lat_split")
        kr_ok = sem("kr_ok")
        kr_rounded = sem("kr_rounded")
        kr_split = sem("kr_split")
        h32_in = sem("h32_in")
        h32_ok = sem("h32_ok")
        h_rounded = sem("h_rounded")
        h_split = sem("h_split")
        ln_sum = sem("ln_sum")
        ln_mean = sem("ln_mean")
        ln_cent = sem("ln_cent")
        ln_sqr = sem("ln_sqr")
        ln_part = sem("ln_part")
        ln_sqsum = sem("ln_sqsum")
        ln_z = sem("ln_z")
        ln_res = sem("ln_res")
        res_scaled = sem("res_scaled")
        head_rounded = sem("head_rounded")
        rope_ok = sem("rope_ok")
        rope_rounded = sem("rope_rounded")
        s_done = sem("s_done")
        m_ok = sem("m_ok")
        e_done = sem("e_done")
        p_ok = sem("p_ok")
        t_done = sem("t_done")
        t_rounded = sem("t_rounded")
        t_split = sem("t_split")
        v_done = sem("v_done")
        o_rounded = sem("o_rounded")
        gate_done = sem("gate_done")
        up_done = sem("up_done")
        silu_ok = sem("silu_ok")
        f32_ok = sem("f32_ok")
        f_rounded = sem("f_rounded")
        f_split = sem("f_split")
        ada1_scaled = sem("ada1_scaled")
        ada1_used = sem("ada1_used")
        rot_ok = sem("rot_ok")
        rot_rounded = sem("rot_rounded")
        rot_split = sem("rot_split")
        k_stack = sem("k_stack")
        ss_done = sem("ss_done")
        sv_split = sem("sv_split")
        sm_ok = sem("sm_ok")
        se_done = sem("se_done")
        sp_ok = sem("sp_ok")
        sr_ok = sem("sr_ok")
        st_done = sem("st_done")
        sv_done = sem("sv_done")
        st_rounded = sem("st_rounded")
        st_split = sem("st_split")
        so_rounded = sem("so_rounded")
        dve_own = sem("dve_own")
        pool_own = sem("pool_own")

        DN = dense_numbers()
        block = ctx.enter_context(nc.Block())

        def halves(th):
            return slice(th * TH, th * TH + TH)

        def res_floor(q):
            return 8 * 2 * q

        @block.sync
        def _(sp):
            ada0 = A["ada_w"][0]

            def load_ada(u):
                if u >= 3:
                    sp.wait_ge(ada_used, u - 2)
                v, kc = u // KC, u % KC
                sp.dma_start(ada_raw[:, u % 3, :], ada0[kc * P:(kc + 1) * P, v * D:(v + 1) * D])\
                    .then_inc(ada_in[u % 3], 16)

            def load_w(T, src):
                if T >= RING:
                    sp.wait_ge(w_split, T - RING + 1)
                w = src.shape[-1]
                sp.dma_start(w_raw[:, T % RING, 0:w], src).then_inc(w_in[T % RING], 16)

            smalls = [(cond_in, A["cond"]), (ada_b, A["ada_b"]), (ln_gb, A["ln_gb"]), (lat_g, A["lat_g"]),
                      (qk_b, A["qk_b"]), (wo_b, A["wo_b"]), (freq, A["freq"]),
                      (sinks, A["sinks"].partition_broadcast(P))]
            for dst, src in smalls:
                sp.dma_start(dst[:], src).then_inc(const_in, 16)
            sp.dma_start(pos_i[:], A["pos"].partition_broadcast(P)).then_inc(pos_in, 16)
            for u in range(2 * KC):
                load_ada(u)
                if u == 2 * KC - 6:
                    for th in range(NT):
                        sp.dma_start(x[:, :, halves(th)], A["x"][:, :, halves(th)]).then_inc(x_in[th], 16)
            for T in range(RING):
                load_w(T, A["w_lat"][T % 6])
            u = 2 * KC
            for T in range(RING, T_HEAD + 3):
                load_w(T, A["w_lat"][T % 6] if T < T_HEAD else
                       [A["w_qr"], A["w_qn"], A["w_kv"]][T - T_HEAD][0])
                for _ in range(3):
                    if u < 6 * KC:
                        load_ada(u)
                        u += 1
            sp.wait_ge(tab_out, 16 * 8)
            sp.wait_ge(dense_done, N_HEAD0)
            sp.dma_start(rcos[:], tab_dram[0]).then_inc(tab_in, 16)
            sp.dma_start(rsin[:], tab_dram[1]).then_inc(tab_in, 16)
            for p in range(1, HEADS // 2):
                for k, src in enumerate((A["w_qr"], A["w_qn"], A["w_kv"])):
                    load_w(T_HEAD + 3 * p + k, src[p])

            def residual_back(src):
                for th in range(NT):
                    sp.dma_start(x[:, :, halves(th)], src[:, :, halves(th)]).then_inc(res_in[th], 16)

            for layer in range(DEPTH):
                for s in range(NT * KC):
                    T = T_WO[layer] + s
                    if s == 3:
                        if layer == 0:
                            sp.wait_ge(dense_done, DN["W", 1, 1, HEADS - 1] + 1)
                            residual_back(A["x"])
                        else:
                            sp.wait_ge(ss_done, NB * WKV)
                            residual_back(spill)
                    load_w(T, A["w_o"][layer, s % KC])

                def turn(i, ks=range(6)):
                    for k in ks:
                        T = T_FFN[layer] + 6 * i + k
                        T0 = T_FFN[layer] + k
                        f = 2 * i + (k % 4) // 2 if k < 4 else 2 * i + k - 4
                        src = A["w_dn"] if k >= 4 else (A["w_gt"], A["w_up"])[k % 2]
                        src = src[layer]
                        sp.wait_ge(w_split, T - RING + 1)
                        src = src[f] if isinstance(f, int) else src[ds(f, 1)].rearrange("a p n -> (a p) n")
                        sp.dma_start(w_raw[:, T0 % RING, :], src).then_inc(w_in[T0 % RING], 16)

                with sp.Fori(0, ITERS) as i:
                    turn(i)
                if layer == 0:
                    for T in range(T_QKV, T_QKV + RING):
                        load_w(T, A["w_qkv"][T - T_QKV])
                    for th in range(NT):
                        sp.wait_ge(ln_res, res_floor(1) + KC * (th + 1))
                        sp.dma_start(spill[:, :, halves(th)], x[:, :, halves(th)]).then_inc(spilled, 16)
                    sp.wait_ge(ada_fold, 6 * DEPTH)
                    sp.wait_ge(h_split, 16 * 2 + 16)
                    sp.dma_start(scos[:], tab_dram[2]).then_inc(tab_in, 16)
                    sp.dma_start(ssin[:], tab_dram[3]).then_inc(tab_in, 16)
                    for th in range(NT):
                        for k in range(12):
                            if k == RING:
                                if th:
                                    sp.wait_ge(st_done, parts_before(NB // NT * WKV))
                                sp.dma_start(sv_b[:], A["v_b"].partition_broadcast(P)).then_inc(vbias_in, 16)
                            T = T_QKV + 12 * th + k
                            if T >= T_QKV + RING:
                                load_w(T, A["w_qkv"][k])
            sp.wait_ge(spilled, 16 * NT)
            for th in range(NT):
                for c in range(KC):
                    sp.wait_ge(ln_res, res_floor(3) + KC * th + c + 1)
                    sp.dma_start(A["out"][:, c, halves(th)], x[:, c, halves(th)]).then_inc(stored, 16)
            sp.wait_ge(stored, 16 * NT * KC)

        @block.tensor
        def _(pe):
            def three(out, w, x_, first, last, skip=False):
                pe.matmul(out, w[0], x_[0], start=first, stop=False, skip_group_check=skip)
                pe.matmul(out, w[0], x_[1], start=False, stop=False, skip_group_check=skip)
                return pe.matmul(out, w[1], x_[0], start=False, stop=last, skip_group_check=skip)

            def wt(T, lo, hi):
                return w_hi[:, T % RING, lo:hi], w_lo[:, T % RING, lo:hi]

            def bank(n_static):
                return dpad[:, n_static % 2, :]

            def claim(n):
                if not isinstance(n, int) or n >= 2:
                    pe.wait_ge(dense_free, n - 1)

            def dense(n, T, chunks, src):
                pe.wait_ge(w_split, T + 1)
                claim(n)
                for k in range(chunks):
                    mm = three(bank(n), wt(T, k * P, k * P + P), src(k), k == 0, k == chunks - 1)
                mm.then_inc(dense_done, 1)

            def h_of(th):
                return lambda k: (h_hi[:, k, halves(th)], h_lo[:, k, halves(th)])

            def stat_column(src):
                for t in range(4):
                    mm = pe.matmul(tpad[:, 0, t:t + 1], src[:, t * P:t * P + P], ones[:, 0:1],
                                   start=True, stop=True, skip_group_check=True)
                mm.then_inc(stat_col, 1)

            def stat_spread(z, diag):
                pe.wait_ge(stat_diag, z + 1)
                if 0 < z < 4:
                    pe.wait_ge(lat_ok, (0, 2, 5, 7)[z])
                for t in range(4):
                    mm = pe.matmul(tpad[:, 1, t * P:t * P + P], ones[:], diag[:, t, :],
                                   start=True, stop=True, skip_group_check=True)
                mm.then_inc(stat_row, 1)

            def fold(v, acc, psum, before):
                if before:
                    pe.wait_ge(mod_ok, before)
                for c in range(KC):
                    mm = pe.matmul(psum[:, v * KC + c:v * KC + c + 1], acc[:, c * P:c * P + P], ones[:, 0:1],
                                   start=True, stop=True, skip_group_check=True)
                mm.then_inc(ada_fold, 1)

            pe.wait_ge(consts, 3)
            pe.wait_ge(ident_ok, 2)
            for v in range(2):
                pe.wait_ge(ada_used, KC * (v + 1))
                fold(v, ada_acc[:, v % 2, :], spad[:, 3, :], v)

            next_fold = 2
            for step in lat_steps():
                if step[0] == "E":
                    _, th, m = step
                    n = N_LAT + 6 * th + m
                    if m == 0:
                        pe.wait_ge(h_split, KC * (th + 1))
                    dense(n, T_LAT + 6 * th + m, KC, h_of(th))
                    if n in (4, 7, 9):
                        pe.wait_ge(ada_used, KC * (next_fold + 1))
                        fold(next_fold, ada_acc[:, next_fold % 2, :], spad[:, 3, :], next_fold)
                        next_fold += 1
                elif step[0] == "C":
                    z = step[1]
                    pe.wait_ge(ss_ok, 5 * (z // 2) + (2, 5)[z % 2])
                    stat_column(lat_ss)
                else:
                    stat_spread(step[1], diag0)
            pe.wait_ge(ada_used, KC * 6)
            fold(5, ada_acc[:, 1, :], spad[:, 3, :], 5)

            def lat(lo, c):
                return lambda k: (lat_hi[:, lo + k, c], lat_lo[:, lo + k, c])

            pe.wait_ge(lat_split, 10)
            for kind, a, b, h in head_work(PE_ORDER):
                p, hp = divmod(h, 2)
                T = T_HEAD + 3 * p
                e0 = 8 * h
                u0 = T_GROUPS * h
                if kind == "S":
                    i = a
                    if not (h == 0 and i < 4):
                        pe.wait_ge(e_done, e0 + i - SPREV[i][1] + 1)
                    th = i // 4
                    pe.wait_ge(dense_free, DN["K", th, th, h] + 1)
                    pe.wait_ge(rope_ok, 4 * p + 3 + th)
                    if h == 0:
                        pe.wait_ge(kr_split, NT)
                    for c0 in range(0, i + 1, 4):
                        c1 = min(c0 + 4, i + 1)
                        out = spad[:, SBANK[i] + c0 // 4, 0:(c1 - c0) * P]
                        q = slice(i * P, i * P + P)
                        keys = slice(c0 * P, c1 * P)
                        three(out, (q_hi[:, q], q_lo[:, q]), (k_hi[:, keys], k_lo[:, keys]), True, False)
                        pe.matmul(out, qr[:, hp, q], kr_hi[:, keys], start=False, stop=False)
                        mm = pe.matmul(out, qr[:, hp, q], kr_lo[:, keys], start=False, stop=c1 <= i)
                        if c1 > i:
                            mm = pe.matmul(out[:, (i - c0) * P:(i - c0) * P + P], ident[:], band[:, 1, :],
                                           start=False, stop=True)
                    mm.then_inc(s_done, 1)
                elif kind == "T":
                    g, cc = a, b
                    u = t_index(g, cc)
                    pe.wait_ge(p_ok, e0 + 2 * g + 2)
                    if u0 + u >= 2:
                        pe.wait_ge(t_split, u0 + u - 1)
                    for c in (2 * cc, 2 * cc + 1):
                        for i in (2 * g, 2 * g + 1):
                            if c <= i:
                                col = 256 if c == 2 * g + 1 else (c % 2) * 256 + (i % 2) * P
                                mm = pe.transpose(tpad[:, u % 2, col:col + P], prob[:, i % 4, c * P:c * P + P], ident32)
                    mm.then_inc(t_done, 1)
                elif kind == "V":
                    g, cc = a, b
                    u = t_index(g, cc)
                    n = DN["V", g, g, h]
                    pe.wait_ge(t_split, u0 + u + 1)
                    if cc == 0:
                        pe.wait_ge(dense_free, DN["W", g // 2, g // 2, h] + 1)
                        claim(n)
                    for c in (2 * cc, 2 * cc + 1):
                        part = slice(P, 2 * P) if c == 2 * g + 1 else slice(0, 2 * P)
                        src = slice(256, 256 + P) if c == 2 * g + 1 else slice((c % 2) * 256, (c % 2) * 256 + 2 * P)
                        mm = three(bank(n)[:, part], (v_hi[:, c, :], v_lo[:, c, :]),
                                   (pt_hi[:, u % 2, src], pt_lo[:, u % 2, src]), c == 0, c == 2 * g + 1)
                    mm.then_inc(dense_done if cc == g else v_done, 1)
                elif kind == "W":
                    n = DN[kind, a, b, h]
                    pe.wait_ge(w_split, T + 3)
                    claim(n)
                    for t in range(4):
                        tok = slice((4 * a + t) * P, (4 * a + t) * P + P)
                        for k in range(KVC):
                            lo = (k * 4 + 2 * hp + 1) * P
                            mm = three(bank(n)[:, t * P:t * P + P], lat(0, tok)(k), wt(T_HEAD + 2, lo, lo + P),
                                       k == 0, k == KVC - 1)
                    mm.then_inc(dense_done, 1)
                else:
                    n = DN[kind, a, b, h]
                    tile, chunks, src, step, first = {"R": (0, QC, KVC, P, 0), "Q": (1, QC, KVC, 2 * P, hp * P),
                                                      "K": (2, KVC, 0, 4 * P, 2 * hp * P)}[kind]
                    pe.wait_ge(w_split, T + tile + 1)
                    claim(n)
                    for k in range(chunks):
                        lo = k * step + first
                        mm = three(bank(n), wt(T_HEAD + tile, lo, lo + P), lat(src, halves(a))(k),
                                   k == 0, k == chunks - 1)
                    mm.then_inc(dense_done, 1)

            def ln_mean_mm(L):
                pe.wait_ge(ln_sum, L + 1)
                if L:
                    pe.wait_ge(ln_z, KC * L)
                pe.matmul(tpad[:, 1, :], ones[:], ln_s[:], start=True, stop=True).then_inc(ln_mean, 1)

            def ln_var_mm(L):
                pe.wait_ge(ln_sqsum, L + 1)
                stat_column(ln_s)

            def ln_spread(L):
                stat_spread(4 + L, ln_sq[:, 0, :].rearrange("p (t c) -> p t c", t=4))

            def out_proj(layer):
                for th in range(NT):
                    for c in range(KC):
                        s = KC * th + c
                        if layer == 0 and s == 0:
                            pe.wait_ge(o_rounded, 4 * HEADS)
                        if layer == 1 and s == 0:
                            pe.wait_ge(so_rounded, 2 * NB * WKV)
                        dense(N_WO[layer] + s, T_WO[layer] + s, KC, h_of(th))
                        if th == 1:
                            L = 4 * layer
                            if c == 0:
                                ln_mean_mm(L)
                            elif c == 3:
                                ln_var_mm(L)
                            elif c == 4:
                                ln_spread(L)

            def feed_forward(layer):
                jb = 44 * layer

                def turn(i, first, last):
                    T = T_FFN[layer] + 6 * i
                    T0 = T_FFN[layer]
                    for f in range(2):
                        for th in range(NT):
                            j = jb + 4 * i + 2 * f + th
                            for which, s in ((0, gate_done), (1, up_done)):
                                k = 2 * f + which
                                if first and f == 0 and which == 0:
                                    pe.wait_ge(h_split, 16 * (2 * layer + 1) + KC * (th + 1))
                                pe.wait_ge(w_split, T + k + 1)
                                if not (first and f == 0):
                                    pe.wait_ge((silu_ok, f32_ok)[which], j - 1)
                                for c in range(KC):
                                    mm = three(spad[:, 2 * which + th, :], wt(T0 + k, c * P, c * P + P), h_of(th)(c),
                                               c == 0, c == KC - 1)
                                mm.then_inc(s, 1)
                    for th in range(NT):
                        pe.wait_ge(f_split, jb + 4 * i + 3 + th)
                        pe.wait_ge(w_split, T + 6)
                        for c in range(KC):
                            n = N_FFN[layer] + 16 * i + KC * th + c
                            claim(n)
                            for f in range(2):
                                mm = three(bank(N_FFN[layer] + c), wt(T0 + 4 + f, c * P, c * P + P),
                                           (f_hi[:, f, halves(th)], f_lo[:, f, halves(th)]), f == 0, f == 1)
                            mm.then_inc(dense_done, 1)
                            if last and th == 1 and c == 1:
                                ln_mean_mm(4 * layer + 2)

                turn(0, True, False)
                with pe.Fori(1, ITERS - 1) as i:
                    turn(i, False, False)
                if layer == 0:
                    for v in range(6):
                        pe.wait_ge(ada1_used, KC * (v + 1))
                        fold(v, ada1_acc[:, v, :], tpad[:, 0, :], 6 + v)
                turn(ITERS - 1, False, True)
                L = 4 * layer + 2
                ln_var_mm(L)
                ln_spread(L)

            def norm_second(L):
                ln_mean_mm(L)
                ln_var_mm(L)
                ln_spread(L)

            out_proj(0)
            norm_second(1)
            feed_forward(0)
            norm_second(3)

            def qkv(th):
                for k in range(12):
                    T = T_QKV + 12 * th + k
                    n = N_QKV + 28 * th + k
                    if k == 0:
                        pe.wait_ge(h_split, 16 * 2 + KC * (th + 1))
                    if k in (2, 3):
                        pe.wait_ge(w_split, T + 1)
                        claim(n)
                        for t in range(4):
                            tok = slice(th * TH + t * P, th * TH + t * P + P)
                            for c in range(KC):
                                mm = three(bank(n)[:, t * P:t * P + P], (h_hi[:, c, tok], h_lo[:, c, tok]),
                                           wt(T, c * P, c * P + P), c == 0, c == KC - 1)
                        mm.then_inc(dense_done, 1)
                    else:
                        dense(n, T, KC, h_of(th))

            def s_scores(r):
                b, j = divmod(r, WKV)
                lo = 0 if b else P
                sl = 2 * (r % 2)
                if r >= 2:
                    pe.wait_ge(se_done, r - 1)
                q = slice((b % 4) * P, (b % 4) * P + P)
                keys = slice((b - 1) * P + lo, b * P + P)
                for half in range(2):
                    out2 = spad[:, sl + half, :].rearrange("p (g k) -> p g k", g=2)[:, :, lo:2 * P]
                    mask = band[:].rearrange("p a k -> p (a k)")[:, lo:2 * P].unsqueeze(1).to_broadcast([P, 2, 2 * P - lo])
                    pe.matmul(out2, ident[:], mask, start=True, stop=False, skip_group_check=True)
                    for g in range(2):
                        qs = sq_st[:, GRP * j + 2 * half + g, q]
                        pe.matmul(out2[:, g, :], qs, sk_hi[:, j, keys], start=False, stop=False, skip_group_check=True)
                        mm = pe.matmul(out2[:, g, :], qs, sk_lo[:, j, keys], start=False, stop=True,
                                       skip_group_check=True)
                mm.then_inc(ss_done, 1)

            def s_transpose(r, a):
                if r // WKV or a:
                    pe.wait_ge(sp_ok, r + 1)
                    if r > (0 if a else WKV):
                        pe.wait_ge(st_split, part_number(r - 1, a))
                    for g in range(GRP):
                        mm = pe.transpose(tpad[:, a, g * P:g * P + P], sprob[:, r % 2, g, a * P:a * P + P], ident32)
                    mm.then_inc(st_done, 1)

            def s_product(r, a):
                b, j = divmod(r, WKV)
                if b or a:
                    n = swa_number(r)
                    pe.wait_ge(st_split, part_number(r, a))
                    if a:
                        claim(n)
                    last = a == 0 or b == 0
                    blk = b - 1 + a
                    mm = three(bank(n)[0:WD, :], (sv_hi[:, blk, j * WD:j * WD + WD], sv_lo[:, blk, j * WD:j * WD + WD]),
                               (spt_hi[:, a, :], spt_lo[:, a, :]), a == 1, last)
                    mm.then_inc(dense_done if last else sv_done, 1)

            for th in range(NT):
                qkv(th)
                pe.wait_ge(k_stack, 8 * (th + 1))
                pe.wait_ge(rot_split, 16 * (th + 1))
                pe.wait_ge(rot_rounded, 26 * (th + 1))
                pe.wait_ge(sv_split, 2 * (th + 1))
                units = range(16 * th, 16 * th + 16)
                for r in range(16 * th - 2, 16 * th + 17):
                    if r + 2 in units:
                        s_scores(r + 2)
                    if r - 1 in units:
                        s_product(r - 1, 1)
                    if r in units:
                        s_transpose(r, 1)
                        s_transpose(r, 0)
                    if r - 1 in units:
                        s_product(r - 1, 0)

            out_proj(1)
            norm_second(5)
            feed_forward(1)
            norm_second(7)

        @block.scalar
        def _(act):
            def split(T, width=D, turn=0):
                sl = T % RING
                act.wait_ge(w_in[sl], 16 * (T // RING + 1) + 32 * turn)
                act.activation(w_hi[:, sl, 0:width], w_raw[:, sl, 0:width], ACT.Copy).then_inc(w_rounded, 1)

            def split_after(T, done, value):
                if T < T_END:
                    act.wait_ge(done, value)
                    split(T, tile_width(T))

            act.wait_ge(const_in, 16 * 8)
            act.activation(cond[:], cond_in[:], ACT.Silu).then_inc(cond_ok, 1)
            act.wait_ge(consts, 5)
            act.activation(ident[:], tab_t[:, 0:P], ACT.Copy).then_inc(ident_ok, 1)
            act.activation(band[:].rearrange("p a k -> p (a k)"), tab_t[:, P:3 * P], ACT.Copy).then_inc(ident_ok, 1)

            for T in range(RING):
                split(T)

            for th in range(NT):
                for c in range(KC):
                    act.wait_ge(h32_in, KC * th + c + 1)
                    act.activation(h_hi[:, c, halves(th)], h32[:, c % 2, :], ACT.Copy).then_inc(h_rounded, 1)

            for t in range(2):
                act.wait_ge(tab_ready, t + 1)
                if t:
                    act.wait_ge(tab_out, 16 * 4)
                act.activation(sin0[:], tab_ang[:], ACT.Sin).then_inc(tab_trig, 1)
                act.wait_ge(tab_trig, 2 * t + 1)
                act.activation(tab_ang[:], tab_ang[:], ACT.Abs).then_inc(tab_abs, 1)
                act.wait_ge(tab_abs, t + 1)
                act.wait_ge(tab_trig, 2 * t + 1)
                act.activation(cos0[:], tab_ang[:], ACT.Sin, scale=-1.0, bias=freq[:, 2:3]).then_inc(tab_trig, 1)
                act.wait_ge(tab_trig, 2 * t + 2)
                act.wait_ge(tab_sign, t + 1)
                for half in range(NT):
                    act.dma_start(tab_dram[2 - 2 * t, :, halves(half)], cos0[:, halves(half)]).then_inc(tab_out, 16)
                    act.dma_start(tab_dram[3 - 2 * t, :, halves(half)], sin0[:, halves(half)]).then_inc(tab_out, 16)
            def lat_chunk(m):
                return m - 1

            rounded = 0
            for step in lat_steps():
                if step[0] == "E":
                    _, th, m = step
                    n = N_LAT + 6 * th + m
                    if m:
                        j = 5 * th + m - 1
                        act.wait_ge(dense_done, n + 1)
                        if j >= 2:
                            act.wait_ge(ss_ok, j - 1)
                        act.activation(lat_sq[:, j % 2, :], dpad[:, n % 2, :], ACT.Square).then_inc(sq_ok, 1)
                    else:
                        act.wait_ge(kr_ok, th + 1)
                        act.activation(kr_hi[:, halves(th)], ln_sq[:, 0, :], ACT.Copy).then_inc(kr_rounded, 1)
                    split_after(T_LAT + n + RING, dense_done, n + 1)
                elif step[0] == "C":
                    z = step[1]
                    act.wait_ge(stat_col, z + 1)
                    rank = (KVRANK, QRANK)[z % 2]
                    act.activation(stds[:, 0, :], tpad[:, 0, 0:4], ACT.Sqrt, scale=1.0 / rank, bias=freq[:, 4:5])\
                        .then_inc(stat_std, 1)
                else:
                    z = step[1]
                    th = z // 2
                    for m in ((0, 1), (2, 3, 4))[z % 2]:
                        rounded += 1
                        act.wait_ge(lat_ok, rounded)
                        act.activation(lat_hi[:, m, halves(th)], lat32[:, m, :], ACT.Copy).then_inc(lat_rounded, 1)

            def product_done(h, g, cc):
                if g == cc:
                    act.wait_ge(dense_done, DN["V", g, g, h] + 1)
                else:
                    act.wait_ge(v_done, 6 * h + g * (g - 1) // 2 + cc + 1)

            act.wait_ge(ada_used, 6 * KC)
            for kind, a, b, h in head_work(ACT_ORDER):
                p = h // 2
                u0 = T_GROUPS * h
                if kind == "S":
                    i = a
                    act.wait_ge(m_ok, 8 * h + i + 1)
                    if i >= 4:
                        act.wait_ge(t_done, u0 + t_index(i // 2 - 2, i // 2 - 2) + 1)
                    elif h:
                        act.wait_ge(t_done, u0 - T_GROUPS + t_index(i // 2 + 2, i // 2 + 2) + 1)
                    act.activation(prob[:, i % 4, 0:(i + 1) * P],
                                   spad_flat[:, SBANK[i] * 512:SBANK[i] * 512 + (i + 1) * P], ACT.Exp,
                                   bias=neg_max[:, i:i + 1], scale=MLA_SCALE, accum_out=row_sum[:, i:i + 1])\
                        .then_inc(e_done, 1)
                elif kind == "T":
                    g, cc = a, b
                    u = t_index(g, cc)
                    w = 384 if cc == g else 512
                    act.wait_ge(t_done, u0 + u + 1)
                    if u >= 2:
                        product_done(h, *((0, 0), (1, 0), (1, 1), (2, 0), (2, 1), (2, 2), (3, 0), (3, 1))[u - 2])
                    elif h:
                        product_done(h - 1, 3, 2 + u)
                    act.activation(pt_hi[:, u % 2, 0:w], tpad[:, u % 2, 0:w], ACT.Copy).then_inc(t_rounded, 1)
                elif kind == "R":
                    act.wait_ge(rope_ok, 4 * p + a + 1)
                    act.activation(qr[0:64, 0, halves(a)], rt_out[0:64, a, :], ACT.Copy).then_inc(rope_rounded, 1)
                    act.activation(qr[64:P, 1, halves(a)], rt_out[64:P, a, :], ACT.Copy).then_inc(rope_rounded, 1)
                elif kind == "X":
                    last = ("Q", "Q", "W")[a]
                    split_after(T_HEAD + 3 * p + 3 + a, dense_done, DN[last, 1, 1, h + 1] + 1)
                else:
                    n = DN[kind, a, b, h]
                    act.wait_ge(dense_done, n + 1)
                    if kind == "V":
                        act.activation(h_hi[:, h, a * 256:a * 256 + 256], dpad[:, n % 2, 0:256], ACT.Copy)\
                            .then_inc(o_rounded, 1)
                        continue
                    if kind == "W":
                        if h:
                            product_done(h - 1, 3, 2 * a + 1)
                        dst = v_hi[:, 4 * a:4 * a + 4, :].rearrange("p t v -> p (t v)")
                    else:
                        dst = (q_hi if kind == "Q" else k_hi)[:, halves(a)]
                    act.activation(dst, dpad[:, n % 2, :], ACT.Copy).then_inc(head_rounded, 1)

            def ln_squares(L):
                th = L % 2
                for c in range(KC):
                    act.wait_ge(ln_cent, KC * L + c + 1)
                    if c >= 2:
                        act.wait_ge(ln_part, 7 * L + c - 1)
                    act.activation(ln_sq[:, c % 2, :], x[:, c, halves(th)], ACT.Square).then_inc(ln_sqr, 1)

            def ln_root(L):
                act.wait_ge(stat_col, 4 + L + 1)
                act.activation(stds[:, 0, :], tpad[:, 0, 0:4], ACT.Sqrt, scale=1.0 / D, bias=freq[:, 3:4])\
                    .then_inc(stat_std, 1)

            def ln_outputs(L, last):
                th = L % 2
                for c in range(KC):
                    xc = x[:, c, halves(th)]
                    if not last:
                        act.wait_ge(h32_ok, KC * L + c + 1)
                        act.activation(h_hi[:, c, halves(th)], h32[:, c % 2, :], ACT.Copy).then_inc(h_rounded, 1)
                    else:
                        act.wait_ge(ln_z, KC * L + c + 1)
                    act.activation(xc, xc, ACT.Identity, scale=vecs[:, 2, c:c + 1], bias=vecs[:, 3, c:c + 1])\
                        .then_inc(ln_res, 1)

            def ln(L, last=False):
                ln_squares(L)
                ln_root(L)
                ln_outputs(L, last)

            ln_eps = freq[:, 3:4]

            def out_proj(layer):
                for th in range(NT):
                    for c in range(KC):
                        s = KC * th + c
                        split_after(T_WO[layer] + s + RING, dense_done, N_WO[layer] + s + 1)
                        if th == 1:
                            L = 4 * layer
                            if c == 1:
                                ln_squares(L)
                            elif c == 3:
                                ln_root(L)
                            elif c == 5:
                                ln_outputs(L, False)
                ln(4 * layer + 1)

            def feed_forward(layer):
                jb = 44 * layer

                def turn(i, first, last):
                    T = T_FFN[layer] + 6 * i
                    T0 = T_FFN[layer]
                    j0 = jb + 4 * i

                    def next_split(k, done, value):
                        if last and layer == DEPTH - 1 and k >= 6:
                            return
                        act.wait_ge(done, value)
                        split(T0 + k, D, i)

                    def silu(s):
                        act.wait_ge(gate_done, j0 + s + 1)
                        if not (first and s < 2):
                            act.wait_ge(f32_ok, j0 + s - 1)
                        act.activation(gate_s[:, s % 2, :], spad[:, s % 2, :], ACT.Silu).then_inc(silu_ok, 1)

                    def hi(s):
                        act.wait_ge(f32_ok, j0 + s + 1)
                        act.activation(f_hi[:, s // 2, halves(s % 2)], f32[:, s % 2, :], ACT.Copy)\
                            .then_inc(f_rounded, 1)

                    silu(0)
                    hi(0)
                    silu(1)
                    next_split(3, gate_done, j0 + 2)
                    hi(1)
                    next_split(4, up_done, j0 + 2)
                    silu(2)
                    hi(2)
                    silu(3)
                    next_split(5, gate_done, j0 + 4)
                    hi(3)
                    next_split(6, up_done, j0 + 4)
                    next_split(7, dense_done, N_FFN[layer] + 16 * i + 16)
                    next_split(8, dense_done, N_FFN[layer] + 16 * i + 16)

                turn(0, True, False)
                with act.Fori(1, ITERS - 1) as i:
                    turn(i, False, False)
                turn(ITERS - 1, False, True)
                ln(4 * layer + 2, layer == DEPTH - 1)
                ln(4 * layer + 3, layer == DEPTH - 1)

            out_proj(0)
            feed_forward(0)

            def qkv(th):
                for k in range(12):
                    n = N_QKV + 28 * th + k
                    m = 12 * th + k
                    if k in (2, 3):
                        act.wait_ge(dense_free, n + 1)
                    else:
                        act.wait_ge(rot_ok, 10 * th + (k if k < 2 else k - 2) + 1)
                    if k < 2:
                        for part in range(2):
                            rows = slice(64 * part, 64 * part + 64)
                            for dst in range(2):
                                act.activation(sk_hi[64 * dst:64 * dst + 64, 2 * k + part, halves(th)],
                                               sr_out[rows, m % 2, :], ACT.Copy).then_inc(rot_rounded, 1)
                    elif k < 4:
                        act.activation(sv_hi[:, 4 * th:4 * th + 4, (k - 2) * P:(k - 1) * P],
                                       sr_out[:, m % 2, :].rearrange("p (t v) -> p t v", t=4), ACT.Copy)\
                            .then_inc(rot_rounded, 1)
                    else:
                        c = k - 4
                        if k == 4 and th == 0:
                            act.wait_ge(spilled, 16 * NT)
                        act.activation(sq_st[0:64, 2 * c, :], sr_out[0:64, m % 2, :], ACT.Copy).then_inc(rot_rounded, 1)
                        act.activation(sq_st[64:P, 2 * c + 1, :], sr_out[64:P, m % 2, :], ACT.Copy)\
                            .then_inc(rot_rounded, 1)
                    split_after(T_QKV + 12 * th + k + RING, dense_done, n + 1)

            def s_exp(r):
                b = r // WKV
                lo = 0 if b else P
                act.wait_ge(sm_ok, r + 1)
                if r >= 2:
                    act.wait_ge(st_done, parts_before(r - 1))
                sl = 4 * (r % 2)
                act.activation(sink_e[:, sl:sl + GRP], sink_e[:, sl:sl + GRP], ACT.Exp)
                for g in range(GRP):
                    mm = act.activation(sprob[:, r % 2, g, lo:2 * P],
                                        spad[:, 2 * (r % 2) + g // 2, (g % 2) * 256 + lo:(g % 2) * 256 + 256], ACT.Exp,
                                        bias=neg_max[:, sl + g:sl + g + 1], scale=SWA_SCALE,
                                        accum_out=row_sum[:, sl + g:sl + g + 1])
                mm.then_inc(se_done, 1)

            def s_round(r, a):
                if r // WKV or a:
                    act.wait_ge(st_done, part_number(r, a))
                    if r > WKV and a:
                        act.wait_ge(sv_done, r - WKV)
                    elif r:
                        act.wait_ge(dense_done, swa_number(r - 1) + 1)
                    act.activation(spt_hi[:, a, :], tpad[:, a, :], ACT.Copy).then_inc(st_rounded, 1)

            def s_out(r):
                b, j = divmod(r, WKV)
                n = swa_number(r)
                act.wait_ge(dense_done, n + 1)
                src = dpad[0:WD, n % 2, :].rearrange("p (c e q) -> p c e q", c=2, e=2)
                for e in range(2):
                    act.activation(h_hi[64 * e:64 * e + 64, 2 * j:2 * j + 2, b * P:b * P + P], src[:, :, e, :], ACT.Copy)\
                        .then_inc(so_rounded, 1)

            for th in range(NT):
                qkv(th)
                units = range(16 * th, 16 * th + 16)
                for r in range(16 * th - 2, 16 * th + 17):
                    if r in units:
                        s_round(r, 1)
                        s_round(r, 0)
                    if r + 2 in units:
                        s_exp(r + 2)
                    if r - 1 in units:
                        s_out(r - 1)

            out_proj(1)
            feed_forward(1)

        @block.vector
        def _(dve):
            own = Chain(dve, dve_own)

            def split(T, width=D, turn=0):
                sl = T % RING
                dve.wait_ge(w_rounded, T + 1 + 6 * turn)
                dve.tensor_tensor(w_lo[:, sl, 0:width], w_raw[:, sl, 0:width], w_hi[:, sl, 0:width].bitcast(F32),
                                  ALU.subtract).then_inc(w_split, 1)

            def split_if(T):
                if T < T_END:
                    split(T, tile_width(T))

            def add_ada(u):
                v, kc = u // KC, u % KC
                dve.wait_ge(ada_in[u % 3], 16 * (u // 3 + 1))
                acc = ada_acc[:, v % 2, :]
                if kc == 0:
                    if v >= 2:
                        dve.wait_ge(ada_fold, v - 1)
                    dve.tensor_scalar(acc, ada_raw[:, u % 3, :], cond[:, 0:1], None, ALU.mult).then_inc(ada_used, 1)
                else:
                    dve.wait_ge(ada_used, u)
                    dve.scalar_tensor_tensor(acc, ada_raw[:, u % 3, :], cond[:, kc:kc + 1], acc, ALU.mult, ALU.add)\
                        .then_inc(ada_used, 1)

            def finish_mod(layer, v, psum):
                dve.wait_ge(ada_fold, 6 * layer + v + 1)
                dve.tensor_tensor(mod[:, layer, v, :], psum[:, v * KC:v * KC + KC], ada_b[:, layer, v, :], ALU.add)\
                    .then_inc(mod_ok, 1)

            def split_h(idx, c, src, th):
                dve.wait_ge(h_rounded, idx + 1)
                dve.tensor_tensor(h_lo[:, c, halves(th)], src, h_hi[:, c, halves(th)].bitcast(F32), ALU.subtract)\
                    .then_inc(h_split, 1)

            dve.wait_ge(cond_ok, 1)
            for u in range(2 * KC):
                add_ada(u)
            finish_mod(0, 0, spad[:, 3, :])
            finish_mod(0, 1, spad[:, 3, :])
            dve.wait_ge(mod_ok, 2)
            own(dve.tensor_scalar(vecs[:, 0, :], mod[:, 0, 1, :], 1.0, None, ALU.add))
            for th in range(NT):
                dve.wait_ge(x_in[th], 16)
                for c in range(KC + 1):
                    if c < KC:
                        if KC * th + c >= 2:
                            dve.wait_ge(h_split, KC * th + c - 1)
                        dve.tensor_scalar(h32[:, c % 2, :], x[:, c, halves(th)], vecs[:, 0, c:c + 1],
                                          mod[:, 0, 0, c:c + 1], ALU.mult, ALU.add).then_inc(h32_in, 1)
                    if c:
                        split_h(KC * th + c - 1, c - 1, h32[:, (c - 1) % 2, :], th)
                if th == 0:
                    for T in range(RING):
                        split(T)

            def inverse_diag(z, diag):
                dve.wait_ge(stat_std, z + 1)
                own(dve.reciprocal(stds[:, 1, :], stds[:, 0, :]))
                for t in range(4):
                    ins = dve.tensor_scalar(diag[:, t, :], ident32, stds[:, 1, t:t + 1], None, ALU.mult)
                ins.then_inc(stat_diag, 1)

            def rotate(n, n0, cos, sin, out, tmp, bias=None):
                ps = dpad[:, n0 % 2, :]
                dve.wait_ge(dense_done, n + 1)
                for qd in range(4):
                    a = slice(32 * qd, 32 * qd + 32)
                    b = slice(32 * (qd ^ 1), 32 * (qd ^ 1) + 32)
                    if bias is None:
                        own.tick(dve.tensor_tensor(tmp[a, :], ps[b, :], sin[b, :], ALU.mult))
                    else:
                        own.tick(dve.scalar_tensor_tensor(tmp[a, :], ps[b, :], bias[b, :], sin[b, :], ALU.add, ALU.mult))
                if bias is None:
                    dve.tensor_tensor(out, ps, cos, ALU.mult).then_inc(dense_free, 1)
                else:
                    dve.scalar_tensor_tensor(out, ps, bias, cos, ALU.add, ALU.mult).then_inc(dense_free, 1)
                own.wait()
                dve.wait_ge(dense_free, n + 1)
                return dve.tensor_tensor(out, out, tmp, ALU.add)

            u = 2 * KC
            normed = 0
            folded = 2
            for step in lat_steps():
                if step[0] == "E":
                    _, th, m = step
                    n = N_LAT + 6 * th + m
                    if m:
                        j = 5 * th + m - 1
                        dve.wait_ge(sq_ok, j + 1)
                        if th:
                            dve.wait_ge(lat_split, 2 if m <= KVC else 5)
                        dve.tensor_copy(lat32[:, m - 1, :], dpad[:, n % 2, :]).then_inc(dense_free, 1)
                        if m in (1, 3):
                            if j:
                                dve.wait_ge(stat_col, 2 * th + (m == 3))
                            dve.tensor_copy(lat_ss[:], lat_sq[:, j % 2, :]).then_inc(ss_ok, 1)
                        else:
                            dve.wait_ge(ss_ok, j)
                            dve.tensor_tensor(lat_ss[:], lat_ss[:], lat_sq[:, j % 2, :], ALU.add).then_inc(ss_ok, 1)
                    else:
                        if th == 0:
                            dve.wait_ge(tab_out, 16 * 8)
                        rotate(n, n, cos0[:, halves(th)], sin0[:, halves(th)], ln_sq[:, 0, :], ln_sq[:, 1, :])\
                            .then_inc(kr_ok, 1)
                        dve.wait_ge(kr_rounded, th + 1)
                        dve.tensor_tensor(kr_lo[:, halves(th)], ln_sq[:, 0, :], kr_hi[:, halves(th)].bitcast(F32),
                                          ALU.subtract).then_inc(kr_split, 1)
                    split_if(T_LAT + n + RING)
                    for _ in range(3):
                        if u < 6 * KC:
                            add_ada(u)
                            u += 1
                    if n in (6, 8, 10):
                        finish_mod(0, (2, 3, 4)[(n - 6) // 2], spad[:, 3, :])
                elif step[0] == "C":
                    inverse_diag(step[1], diag0)
                else:
                    z = step[1]
                    dve.wait_ge(stat_row, z + 1)
                    ms = ((0, 1), (2, 3, 4))[z % 2]
                    dve.wait_ge(dense_free, N_LAT + 6 * (z // 2) + (3, 6)[z % 2])
                    for m in ms:
                        dve.scalar_tensor_tensor(lat32[:, m, :], lat32[:, m, :], lat_g[:, m:m + 1], tpad[:, 1, :],
                                                 ALU.mult, ALU.mult).then_inc(lat_ok, 1)
                    for m in ms:
                        normed += 1
                        dve.wait_ge(lat_rounded, normed)
                        dve.tensor_tensor(lat_lo[:, m, halves(z // 2)], lat32[:, m, :],
                                          lat_hi[:, m, halves(z // 2)].bitcast(F32), ALU.subtract).then_inc(lat_split, 1)
            finish_mod(0, 5, spad[:, 3, :])

            dve.wait_ge(tab_in, 32)
            for kind, a, b, h in head_work(DVE_ORDER):
                p = h // 2
                if kind == "S":
                    i = a
                    dve.wait_ge(s_done, 8 * h + i + 1)
                    own(dve.tensor_reduce(row_max[:, i:i + 1], spad_flat[:, SBANK[i] * 512:SBANK[i] * 512 + (i + 1) * P],
                                          AX, ALU.max))
                    dve.tensor_scalar(neg_max[:, i:i + 1], row_max[:, i:i + 1], -MLA_SCALE, None, ALU.mult)\
                        .then_inc(m_ok, 1)
                elif kind == "N":
                    i = a
                    dve.wait_ge(e_done, 8 * h + i + 1)
                    own(dve.reciprocal(row_inv[:, i:i + 1], row_sum[:, i:i + 1]))
                    dve.tensor_scalar(prob[:, i % 4, 0:(i + 1) * P], prob[:, i % 4, 0:(i + 1) * P],
                                      row_inv[:, i:i + 1], None, ALU.mult).then_inc(p_ok, 1)
                elif kind == "T":
                    u = t_index(a, b)
                    w = 384 if a == b else 512
                    dve.wait_ge(t_rounded, T_GROUPS * h + u + 1)
                    dve.tensor_tensor(pt_lo[:, u % 2, 0:w], tpad[:, u % 2, 0:w], pt_hi[:, u % 2, 0:w].bitcast(F32),
                                      ALU.subtract).then_inc(t_split, 1)
                elif kind == "R":
                    if a:
                        dve.wait_ge(rope_ok, 4 * p + 1)
                    n = DN[kind, a, b, h]
                    rotate(n, n, rcos[:, halves(a)], rsin[:, halves(a)], rt_out[:, a, :], rt_tmp[:]).then_inc(rope_ok, 1)
                elif kind == "L":
                    dve.wait_ge(rope_rounded, 4 * p + 2 * a + 2)
                    dve.tensor_tensor(qr[64:P, 0, halves(a)], rt_out[0:64, a, :],
                                      qr[0:64, 0, halves(a)].bitcast(F32), ALU.subtract)
                    dve.tensor_tensor(qr[0:64, 1, halves(a)], rt_out[64:P, a, :],
                                      qr[64:P, 1, halves(a)].bitcast(F32), ALU.subtract).then_inc(rope_ok, 1)
                elif kind == "X":
                    split_if(T_HEAD + 3 * p + 3 + a)
                else:
                    n = DN[kind, a, b, h]
                    if kind == "V":
                        dve.wait_ge(o_rounded, 4 * h + a + 1)
                        cols = slice(a * 256, a * 256 + 256)
                        lo, hi, ps = h_lo[:, h, cols], h_hi[:, h, cols], dpad[:, n % 2, 0:256]
                    else:
                        dve.wait_ge(head_rounded, 6 * h + 2 * "QKW".index(kind) + a + 1)
                        ps = dpad[:, n % 2, :]
                        if kind == "W":
                            lo, hi = (v[:, 4 * a:4 * a + 4, :].rearrange("p t v -> p (t v)") for v in (v_lo, v_hi))
                        else:
                            lo, hi = (v[:, halves(a)] for v in ((q_lo, q_hi) if kind == "Q" else (k_lo, k_hi)))
                    dve.tensor_tensor(lo, ps, hi.bitcast(F32), ALU.subtract).then_inc(dense_free, 1)

            def norm_vectors(q):
                g, b = ln_gb[:, q, 0, :], ln_gb[:, q, 1, :]
                if q:
                    dve.wait_ge(ln_res, res_floor(q))
                    dve.wait_ge(vec_ok, q)
                if q == 3:
                    own(dve.tensor_copy(vecs[:, 2, :], g))
                    dve.tensor_copy(vecs[:, 3, :], b).then_inc(vec_ok, 1)
                    return
                layer, sh = ((0, 3), (1, 0), (1, 3))[q]
                dve.wait_ge(mod_ok, 6 * (layer + 1))
                own(dve.tensor_scalar(vtmp[:, 0, :], mod[:, layer, sh + 1, :], 1.0, None, ALU.add))
                own(dve.tensor_tensor(vecs[:, 0, :], g, vtmp[:, 0, :], ALU.mult))
                own(dve.tensor_tensor(vtmp[:, 1, :], b, vtmp[:, 0, :], ALU.mult))
                own(dve.tensor_tensor(vecs[:, 1, :], vtmp[:, 1, :], mod[:, layer, sh, :], ALU.add))
                own(dve.tensor_scalar(vecs[:, 2, :], g, ALPHA, None, ALU.mult))
                if q == 1:
                    own(dve.tensor_tensor(vtmp[:, 0, :], wo_b[:], mod[:, 1, 2, :], ALU.mult))
                    dve.scalar_tensor_tensor(vecs[:, 3, :], b, ALPHA, vtmp[:, 0, :], ALU.mult, ALU.add)\
                        .then_inc(vec_ok, 1)
                else:
                    dve.tensor_scalar(vecs[:, 3, :], b, ALPHA, None, ALU.mult).then_inc(vec_ok, 1)

            def ln_total(L):
                c0 = halves(L % 2)
                if L % 2 == 0:
                    norm_vectors(L // 2)
                if L:
                    dve.wait_ge(stat_col, 4 + L)
                own(dve.tensor_tensor(ln_s[:], x[:, 0, c0], x[:, 1, c0], ALU.add))
                for c in range(2, KC):
                    ins = dve.tensor_tensor(ln_s[:], ln_s[:], x[:, c, c0], ALU.add)
                    if c < KC - 1:
                        own(ins)
                    else:
                        ins.then_inc(ln_sum, 1)

            def ln_center(L):
                c0 = halves(L % 2)
                dve.wait_ge(ln_mean, L + 1)

                def add_square(c):
                    dve.wait_ge(ln_sqr, KC * L + c + 1)
                    if c == 0:
                        dve.tensor_copy(ln_s[:], ln_sq[:, 0, :]).then_inc(ln_part, 1)
                    else:
                        dve.wait_ge(ln_part, 7 * L + c)
                        dve.tensor_tensor(ln_s[:], ln_s[:], ln_sq[:, c % 2, :], ALU.add)\
                            .then_inc(ln_part if c < KC - 1 else ln_sqsum, 1)

                for c in range(KC + 1):
                    if c < KC:
                        dve.scalar_tensor_tensor(x[:, c, c0], tpad[:, 1, :], -1.0 / D, x[:, c, c0], ALU.mult, ALU.add)\
                            .then_inc(ln_cent, 1)
                    if c:
                        add_square(c - 1)

            def ln_inverse(L):
                inverse_diag(4 + L, ln_sq[:, 0, :].rearrange("p (t c) -> p t c", t=4))

            def ln_scale(L, last):
                c0 = halves(L % 2)
                dve.wait_ge(stat_row, 4 + L + 1)
                dve.wait_ge(ln_cent, KC * (L + 1))
                for c in range(KC + 2):
                    if c < KC:
                        dve.tensor_tensor(x[:, c, c0], x[:, c, c0], tpad[:, 1, :], ALU.mult).then_inc(ln_z, 1)
                    if c >= 2 and not last:
                        split_h(16 + KC * L + c - 2, c - 2, h32[:, c % 2, :], L % 2)

            def add_out(layer, n, n0, c, th, which):
                dve.wait_ge(dense_done, n + 1)
                dve.scalar_tensor_tensor(x[:, c, halves(th)], dpad[:, n0 % 2, :], mod[:, layer, which, c:c + 1],
                                         x[:, c, halves(th)], ALU.mult, ALU.add).then_inc(dense_free, 1)

            def out_proj(layer):
                for th in range(NT):
                    for c in range(KC):
                        s = KC * th + c
                        n = N_WO[layer] + s
                        if layer == 0:
                            dve.wait_ge(res_scaled, s + 1)
                        else:
                            dve.wait_ge(res_in[th], 32)
                        add_out(layer, n, n, c, th, 2)
                        split_if(T_WO[layer] + s + RING)
                        if s == KC - 1:
                            dve.wait_ge(dense_free, n + 1)
                            ln_total(4 * layer)
                        if th == 1:
                            L = 4 * layer
                            if c == 1:
                                ln_center(L)
                            elif c == 3:
                                ln_inverse(L)
                            elif c == 5:
                                ln_scale(L, False)
                dve.wait_ge(dense_free, N_WO[layer] + NT * KC)
                L = 4 * layer + 1
                ln_total(L)
                ln_center(L)
                ln_inverse(L)
                ln_scale(L, False)

            def feed_forward(layer):
                jb = 44 * layer

                def turn(i, first, last):
                    T = T_FFN[layer] + 6 * i
                    T0 = T_FFN[layer]
                    j0 = jb + 4 * i

                    def next_split(k):
                        if last and layer == DEPTH - 1 and k >= 6:
                            return
                        split(T0 + k, D, i)

                    def product(s):
                        dve.wait_ge(up_done, j0 + s + 1)
                        dve.wait_ge(silu_ok, j0 + s + 1)
                        if not (first and s < 2):
                            dve.wait_ge(f_split, j0 + s - 1)
                        dve.tensor_tensor(f32[:, s % 2, :], spad[:, 2 + s % 2, :], gate_s[:, s % 2, :], ALU.mult)\
                            .then_inc(f32_ok, 1)

                    def lo(s):
                        dve.wait_ge(f_rounded, j0 + s + 1)
                        part = halves(s % 2)
                        dve.tensor_tensor(f_lo[:, s // 2, part], f32[:, s % 2, :], f_hi[:, s // 2, part].bitcast(F32),
                                          ALU.subtract).then_inc(f_split, 1)

                    product(0)
                    lo(0)
                    next_split(3)
                    product(1)
                    lo(1)
                    next_split(4)
                    product(2)
                    lo(2)
                    next_split(5)
                    product(3)
                    lo(3)
                    next_split(6)
                    for th in range(NT):
                        for c in range(KC):
                            k = KC * th + c
                            n = N_FFN[layer] + 16 * i + k
                            if first:
                                dve.wait_ge(ln_res, 16 * (2 * layer) + k + 1)
                            else:
                                dve.wait_ge(dense_free, n - 15)
                            add_out(layer, n, N_FFN[layer] + k, c, th, 5)
                        if last and th == 0:
                            dve.wait_ge(dense_free, N_FFN[layer] + 16 * i + KC)
                            ln_total(4 * layer + 2)
                    next_split(7)
                    next_split(8)

                turn(0, True, False)
                with dve.Fori(1, ITERS - 1) as i:
                    turn(i, False, False)
                if layer == 0:
                    for v in range(6):
                        finish_mod(1, v, tpad[:, 0, :])
                turn(ITERS - 1, False, True)
                L = 4 * layer + 2
                last = layer == DEPTH - 1
                ln_center(L)
                ln_inverse(L)
                ln_scale(L, last)
                dve.wait_ge(dense_free, N_FFN[layer] + 16 * ITERS)
                ln_total(L + 1)
                ln_center(L + 1)
                ln_inverse(L + 1)
                ln_scale(L + 1, last)

            out_proj(0)
            feed_forward(0)

            def qkv(th):
                for k in range(12):
                    n = N_QKV + 28 * th + k
                    m = 12 * th + k
                    out = sr_out[:, m % 2, :]
                    if m >= 2 and k >= 6:
                        dve.wait_ge(rot_split, 16 * th + 2 * (k - 5))
                    if k < 2 or k >= 4:
                        if k == 0:
                            dve.wait_ge(tab_in, 64)
                            if th == 0:
                                dve.wait_ge(h_split, 48)
                            else:
                                dve.wait_ge(st_done, parts_before(16 * th))
                        bcol = k if k < 2 else k - 2
                        if k in (4, 5):
                            dve.wait_ge(sv_split, 2 * th + k - 3)
                        rotate(n, n, scos[:, halves(th)], ssin[:, halves(th)], out, sr_tmp[:], qk_b[:, bcol:bcol + 1])\
                            .then_inc(rot_ok, 1)
                        dve.wait_ge(rot_ok, 10 * th + bcol + 1)
                        if k < 2:
                            dve.wait_ge(rot_rounded, 26 * th + 4 * k + 4)
                            for part in range(2):
                                rows = slice(64 * part, 64 * part + 64)
                                other = slice(64 - 64 * part, P - 64 * part)
                                kv = 2 * k + part
                                dve.tensor_tensor(sk_lo[rows, kv, halves(th)], sr_out[rows, m % 2, :],
                                                  sk_hi[rows, kv, halves(th)].bitcast(F32), ALU.subtract)\
                                    .then_inc(k_stack, 1)
                                dve.tensor_tensor(sk_lo[other, kv, halves(th)], sr_out[rows, m % 2, :],
                                                  sk_hi[rows, kv, halves(th)].bitcast(F32), ALU.subtract)\
                                    .then_inc(k_stack, 1)
                    else:
                        dve.wait_ge(vbias_in, 16 * (th + 1))
                        dve.wait_ge(k_stack, 8 * (th + 1))
                        dve.wait_ge(dense_done, n + 1)
                        bias = sv_b[:, (k - 2) * P:(k - 1) * P].unsqueeze(1).to_broadcast([P, 4, P])
                        dve.tensor_tensor(out.rearrange("p (t v) -> p t v", t=4),
                                          dpad[:, n % 2, :].rearrange("p (t v) -> p t v", t=4), bias, ALU.add)\
                            .then_inc(dense_free, 1)
                        dve.wait_ge(rot_rounded, 26 * th + 8 + (k - 1))
                        dve.tensor_tensor(sv_lo[:, 4 * th:4 * th + 4, (k - 2) * P:(k - 1) * P],
                                          out.rearrange("p (t v) -> p t v", t=4),
                                          sv_hi[:, 4 * th:4 * th + 4, (k - 2) * P:(k - 1) * P].bitcast(F32),
                                          ALU.subtract).then_inc(sv_split, 1)
                    split_if(T_QKV + 12 * th + k + RING)

            def s_max(r):
                b, j = divmod(r, WKV)
                lo = 0 if b else P
                sl = 4 * (r % 2)
                cols = slice(sl, sl + GRP)
                dve.wait_ge(ss_done, r + 1)
                src = spad[:, 2 * (r % 2):2 * (r % 2) + 2, :].rearrange("p b (g k) -> p (b g) k", g=2)[:, :, lo:2 * P]
                own(dve.tensor_reduce(row_max[:, cols], src, AX, ALU.max))
                own(dve.scalar_tensor_tensor(neg_max[:, cols], row_max[:, cols], -SWA_SCALE,
                                             neg_sinks[:, GRP * j:GRP * j + GRP], ALU.mult, ALU.min))
                dve.tensor_tensor(sink_e[:, cols], sinks[:, GRP * j:GRP * j + GRP], neg_max[:, cols], ALU.add)\
                    .then_inc(sm_ok, 1)

            def s_inverse(r):
                cols = slice(4 * (r % 2), 4 * (r % 2) + GRP)
                dve.wait_ge(se_done, r + 1)
                own(dve.tensor_tensor(row_sum[:, cols], row_sum[:, cols], sink_e[:, cols], ALU.add))
                dve.reciprocal(row_inv[:, cols], row_sum[:, cols]).then_inc(sr_ok, 1)

            def s_low(r, a):
                if r // WKV or a:
                    dve.wait_ge(st_rounded, part_number(r, a))
                    dve.tensor_tensor(spt_lo[:, a, :], tpad[:, a, :], spt_hi[:, a, :].bitcast(F32), ALU.subtract)\
                        .then_inc(st_split, 1)

            def s_out(r):
                b, j = divmod(r, WKV)
                n = swa_number(r)
                src = dpad[0:WD, n % 2, :].rearrange("p (c e q) -> p c e q", c=2, e=2)
                dve.wait_ge(so_rounded, 2 * r + 2)
                for e in range(2):
                    rows, cs, cols = slice(64 * e, 64 * e + 64), slice(2 * j, 2 * j + 2), slice(b * P, b * P + P)
                    ins = dve.tensor_tensor(h_lo[rows, cs, cols], src[:, :, e, :], h_hi[rows, cs, cols].bitcast(F32),
                                            ALU.subtract)
                ins.then_inc(dense_free, 1)

            own(dve.tensor_scalar(neg_sinks[:], sinks[:], -1.0, None, ALU.mult))
            for th in range(NT):
                qkv(th)
                units = range(16 * th, 16 * th + 16)
                for r in range(16 * th - 2, 16 * th + 18):
                    if r + 2 in units:
                        s_max(r + 2)
                    if r + 1 in units:
                        s_inverse(r + 1)
                    if r - 2 in units:
                        s_out(r - 2)
                    if r in units:
                        s_low(r, 1)
                        s_low(r, 0)

            out_proj(1)
            feed_forward(1)

        @block.gpsimd
        def _(pool):
            own = Chain(pool, pool_own)
            pool.memset(ones[:], 1.0).then_inc(consts, 1)
            pool.memset(tab_t[:, 0:3 * P], 0.0).then_inc(consts, 1)
            pool.wait_ge(consts, 2)
            pool.affine_select(out=tab_t[:, 0:P], in_=tab_t[:, 0:P], compare_op=ALU.not_equal, fill=1.0, base=0,
                               pattern=[[-1, P]], channel_multiplier=1).then_inc(consts, 1)
            pool.affine_select(out=tab_t[:, P:2 * P], in_=tab_t[:, P:2 * P], compare_op=ALU.is_gt, fill=MASKED, base=0,
                               pattern=[[1, P]], channel_multiplier=-1).then_inc(consts, 1)
            pool.affine_select(out=tab_t[:, 2 * P:3 * P], in_=tab_t[:, 2 * P:3 * P], compare_op=ALU.is_ge, fill=MASKED,
                               base=0, pattern=[[-1, P]], channel_multiplier=1).then_inc(consts, 1)
            pool.wait_ge(ident_ok, 2)
            pool.wait_ge(pos_in, 16)
            TWO_PI_PARTS = (6.28125, 0.0019350051879882812, 3.0199159819591595e-07)
            NEAREST = 1.5 * 2.0 ** 23
            PI_BELOW = 3.1415925
            for t in range(2):
                if t:
                    pool.wait_ge(tab_trig, 2)
                own(pool.tensor_copy(tab_t[:], pos_i[:]))
                own(pool.tensor_scalar(tab_ang[:], tab_t[:], freq[:, t:t + 1], 1.0, ALU.mult, ALU.mult))
                own(pool.tensor_scalar(tab_k[:], tab_ang[:], 1.0 / (2.0 * np.pi), NEAREST, ALU.mult, ALU.add))
                own(pool.tensor_scalar(tab_k[:], tab_k[:], -NEAREST, -1.0, ALU.add, ALU.mult))
                for part in TWO_PI_PARTS:
                    own(pool.tensor_scalar(tab_t[:], tab_k[:], part, 1.0, ALU.mult, ALU.mult))
                    own(pool.tensor_tensor(tab_ang[:], tab_ang[:], tab_t[:], ALU.add))
                pool.tensor_scalar(tab_ang[:], tab_ang[:], PI_BELOW, -PI_BELOW, ALU.min, ALU.max)\
                    .then_inc(tab_ready, 1)
                pool.wait_ge(tab_trig, 2 * t + 1)
                pool.tensor_scalar(sin0[:], sin0[:], freq[:, 5:6], 1.0, ALU.mult, ALU.mult).then_inc(tab_sign, 1)

            for th in range(NT):
                pool.wait_ge(res_in[th], 16)
                for c in range(KC):
                    xc = x[:, c, halves(th)]
                    pool.tensor_scalar(xc, xc, ALPHA, 1.0, ALU.mult, ALU.mult).then_inc(res_scaled, 1)

            def modulate(L):
                pool.wait_ge(vec_ok, L // 2 + 1)
                for c in range(KC):
                    pool.wait_ge(ln_z, KC * L + c + 1)
                    pool.wait_ge(h_split, 16 + KC * L + c - 1)
                    pool.tensor_scalar(h32[:, c % 2, :], x[:, c, halves(L % 2)], vecs[:, 0, c:c + 1], vecs[:, 1, c:c + 1],
                                       ALU.mult, ALU.add).then_inc(h32_ok, 1)

            modulate(0)
            modulate(1)

            ada1 = A["ada_w"][1]

            def load_ada1(v, kc):
                pool.dma_start(ada1_raw[:, kc % 2, :], ada1[kc * P:(kc + 1) * P, v * D:(v + 1) * D])\
                    .then_inc(ada1_in[kc % 2], 16)

            pool.wait_ge(f_split, 1)
            for kc in range(2):
                load_ada1(0, kc)
            for v in range(6):
                for kc in range(KC):
                    u = v * KC + kc
                    pool.wait_ge(ada1_in[kc % 2], 16 * (u // 2 + 1))
                    raw = ada1_raw[:, kc % 2, :]
                    dst = ada1_acc[:, v, :] if kc == 0 else raw
                    pool.tensor_scalar(dst, raw, cond[:, kc:kc + 1], 1.0, ALU.mult, ALU.mult)\
                        .then_inc(ada1_scaled if kc else ada1_used, 1)
                    if kc:
                        pool.wait_ge(ada1_scaled, v * (KC - 1) + kc)
                        pool.wait_ge(ada1_used, u)
                        pool.tensor_tensor(ada1_acc[:, v, :], ada1_acc[:, v, :], raw, ALU.add).then_inc(ada1_used, 1)
                    if u + 2 < 6 * KC:
                        pool.wait_ge(ada1_used, u + 1)
                        load_ada1((u + 2) // KC, (u + 2) % KC)
            modulate(2)
            modulate(3)

            for th in range(NT):
                for c in range(8):
                    m = 12 * th + 4 + c
                    pool.wait_ge(rot_rounded, 26 * th + 10 + 2 * c + 2)
                    pool.tensor_tensor(sq_st[64:P, 2 * c, :], sr_out[0:64, m % 2, :], sq_st[0:64, 2 * c, :].bitcast(F32),
                                       ALU.subtract).then_inc(rot_split, 1)
                    pool.tensor_tensor(sq_st[0:64, 2 * c + 1, :], sr_out[64:P, m % 2, :],
                                       sq_st[64:P, 2 * c + 1, :].bitcast(F32), ALU.subtract).then_inc(rot_split, 1)
                for r in range(16 * th, 16 * th + 16):
                    lo = 0 if r // WKV else P
                    pool.wait_ge(sr_ok, r + 1)
                    for g in range(GRP):
                        pr = sprob[:, r % 2, g, lo:2 * P]
                        col = 4 * (r % 2) + g
                        ins = pool.tensor_scalar(pr, pr, row_inv[:, col:col + 1], 1.0, ALU.mult, ALU.mult)
                    ins.then_inc(sp_ok, 1)
            modulate(4)
            modulate(5)



def _tiles(w):
    k, n = w.shape
    return np.ascontiguousarray(w.reshape(k // P, P, n // P, P).transpose(2, 1, 0, 3)).reshape(n // P, P, k)


def _rotary_order(w):
    w = w.reshape(w.shape[0], -1, WD)
    half = WROT // 2
    return np.concatenate([w[:, :, 0:half], w[:, :, WROT:WROT + 24], w[:, :, half:WROT], w[:, :, WROT + 24:]],
                          axis=2).reshape(w.shape[0], -1)


def _columns(v):
    v = v.reshape(v.shape[:-1] + (-1, P))
    return np.ascontiguousarray(np.moveaxis(v, -1, 0))


def kernel(**inputs):
    import concourse.bacc as bacc
    from concourse.bass_utils import run_bass_kernel_spmd

    i = {k: np.asarray(v) for k, v in inputs.items()}
    q_cols = WH * WD
    w_in = i["mla_w_in"][0]
    rope_in = w_in[:, QRANK + KVRANK:]
    w_q = i["mla_w_q_b"][0].reshape(QC, P, HEADS // 2, 2, NOPE + ROT)
    w_kv = i["mla_w_kv_b"][0].reshape(KVC, P, HEADS // 2, 2 * (NOPE + VDIM))
    w_qkv, b_qkv = i["swa_w_qkv"][0], i["swa_b_qkv"]
    k_end = q_cols + WKV * WD
    inv = np.zeros((P, 8), np.float32)
    for p in range(P):
        r = p % 32
        if r < WROT // 2:
            inv[p, 0] = np.float32(THETA) ** np.float32(-2 * r / WROT)
        inv[p, 1] = np.float32(THETA) ** np.float32(-2 * r / ROT)
        inv[p, 5] = 1.0 if (p // 32) % 2 == 0 else -1.0
    inv[:, 2], inv[:, 3], inv[:, 4] = np.pi / 2, LN_EPS, RMS_EPS
    arrays = {
        "x": np.ascontiguousarray(i["x"][0].T.reshape(KC, P, SEQ).transpose(1, 0, 2)),
        "cond": _columns(i["c"][0]),
        "pos": np.ascontiguousarray(i["positions"][0]),
        "ada_w": i["ada_w"],
        "ada_b": _columns(i["ada_b"].reshape(DEPTH, 6, D)),
        "ln_gb": _columns(np.stack([np.stack([i["ln_mix_g"], i["ln_ffn_g"]], 1), np.stack([i["ln_mix_b"], i["ln_ffn_b"]], 1)],
                                   2).reshape(4, 2, D)),
        "lat_g": np.concatenate([_columns(i["mla_kv_norm"][0]), _columns(i["mla_q_norm"][0])], 1),
        "qk_b": np.concatenate([_columns(_rotary_order(b_qkv[:, q_cols:k_end])[0]),
                                _columns(_rotary_order(b_qkv[:, :q_cols])[0])], 1),
        "v_b": np.ascontiguousarray(b_qkv[0, k_end:]),
        "wo_b": _columns(i["swa_b_o"][0]),
        "sinks": np.ascontiguousarray(i["swa_sinks"][0]),
        "freq": inv,
        "w_lat": _tiles(np.concatenate([rope_in, rope_in, w_in[:, QRANK:QRANK + KVRANK], w_in[:, :QRANK]], 1)),
        "w_qr": np.ascontiguousarray(w_q[..., NOPE:].transpose(2, 1, 0, 3, 4)).reshape(HEADS // 2, P, -1),
        "w_qn": np.ascontiguousarray(w_q[..., :NOPE].transpose(2, 1, 0, 3, 4)).reshape(HEADS // 2, P, -1),
        "w_kv": np.ascontiguousarray(w_kv.transpose(2, 1, 0, 3)).reshape(HEADS // 2, P, -1),
        "w_qkv": np.concatenate([_tiles(_rotary_order(w_qkv[:, q_cols:k_end])), _tiles(w_qkv[:, k_end:]),
                                 _tiles(_rotary_order(w_qkv[:, :q_cols]))], 0),
        "w_o": np.stack([_tiles(i["mla_w_o"][0]), _tiles(i["swa_w_o"][0])]),
        "w_gt": np.stack([_tiles(w) for w in i["ffn_w_gate"]]),
        "w_up": np.stack([_tiles(w) for w in i["ffn_w_up"]]),
        "w_dn": i["ffn_w_down"].reshape(DEPTH, FC, P, D),
    }
    nc = bacc.Bacc("TRN2", target_bir_lowering=False, num_devices=1)
    A = {k: nc.dram_tensor("in_" + k, a.shape, I32 if k == "pos" else F32, kind="ExternalInput").ap() for k, a in arrays.items()}
    A["out"] = nc.dram_tensor("out", (P, KC, SEQ), F32, kind="ExternalOutput").ap()
    build(nc, A)
    got = run_bass_kernel_spmd(nc, [{"in_" + k: a for k, a in arrays.items()}], core_ids=[0]).results[0]["out"]
    return np.ascontiguousarray(got.transpose(2, 1, 0)).reshape(1, SEQ, D)
```

```python
from contextlib import ExitStack

import numpy as np

import concourse.bass as bass
from concourse import mybir

F32 = mybir.dt.float32
F32R = mybir.dt.float32r
I32 = mybir.dt.int32
ALU = mybir.AluOpType
ACT = mybir.ActivationFunctionType
AX = mybir.AxisListType.X
ds = bass.ds

P = 128
D = 1024
SEQ = 1024
KC = D // P
TH = 512
NT = SEQ // TH
HEADS, NOPE, ROT, VDIM = 8, 128, 64, 128
QRANK, KVRANK = 384, 256
QC, KVC = QRANK // P, KVRANK // P
WH, WKV, WD, WROT = 16, 4, 64, 16
GRP = WH // WKV
DFF = 2816
FC = DFF // P
ITERS = FC // 2
NB = SEQ // P
DEPTH = 2
ALPHA = (2 * DEPTH) ** 0.25
LN_EPS, RMS_EPS = 1e-5, 1e-6
THETA = 500000.0
MLA_SCALE = (NOPE + ROT) ** -0.5
SWA_SCALE = WD ** -0.5
MASKED = -1e30
RING = 3
ADA_RING = 6
SQ_POOL = 3

T_LAT = 0
T_HEAD = T_LAT + NT * 6
T_WO = [T_HEAD + 3 * (HEADS // 2), 0]
T_FFN = [T_WO[0] + NT * KC, 0]
T_QKV = T_FFN[0] + 6 * ITERS
T_WO[1] = T_QKV + NT * 12
T_FFN[1] = T_WO[1] + NT * KC
T_END = T_FFN[1] + 6 * ITERS

PAIR_STEPS = 22
N_LAT = 0
N_HEAD0 = N_LAT + NT * 6
N_WO = [N_HEAD0 + PAIR_STEPS * (HEADS // 2) + 2, 0]
N_FFN = [N_WO[0] + NT * KC, 0]
N_QKV = N_FFN[0] + 16 * ITERS
N_WO[1] = N_QKV + NT * (12 + 16)
N_FFN[1] = N_WO[1] + NT * KC

PE_ORDER = ("T00 S4 S5 T10 T11 V00 S6 V10 T20 V11 Q0+ T21 V20 T22 S7 V21 V22 Q1+ K0+ T30 T31 K1+ R0+ T32 R1+ "
            "W00+ V30 V31 T33 S0+ S1+ S2+ V32 V33 S3+ W01+ W10+ W11+ A0")
ACT_ORDER = ("S4 T10 X0 S5 T11 X1 V00 T20 X2 V11 S6 Q0+ T21 T22 V22 S7 Q1+ T30 K0+ T31 K1+ R0+ R1+ T32 W00+ T33 "
             "S0+ S1+ V33 S2+ S3+ W01+ W10+ W11+ T00+")
DVE_ORDER = ("S4 S5 N4 T10 X0 N5 T11 X1 V00 S6 T20 X2 V11 N6 Q0+ T21 T22 S7 V22 N7 Q1+ T30 K0+ T31 K1+ R0+ R1+ L0+ L1+ "
             "T32 W00+ T33 S0+ S1+ S2+ N0+ N1+ V33 N2+ S3+ N3+ W01+ W10+ W11+ A0 T00+")
T_GROUPS = 10
SBANK = [0, 1, 2, 3, 0, 2, 0, 2]
SPREV = [(6, 2), (6, 3), (7, 3), (7, 4), (1, 3), (3, 2), (4, 2), (5, 2)]


def t_index(g, cc):
    return g * (g + 1) // 2 + cc


def head_work(order):
    for body in range(-1, HEADS + 1):
        for item in order.split():
            kind, digits, h = item[0], item[1:].rstrip("+"), body + item.endswith("+")
            if 0 <= h < HEADS and not (kind in "RL" and h % 2) and not (kind == "X" and h % 2 == 0) \
                    and not (kind == "A" and h not in (2, 3)) and not (kind == "W" and h % 2 and digits[-1] == "1"):
                yield kind, int(digits[0]), int(digits[-1]), h


def dense_numbers():
    steps = [w for w in head_work(PE_ORDER) if w[0] in "QKRA" or (w[0] == "W" and w[3] % 2 == 0)
             or (w[0] == "V" and w[1] == w[2])]
    return {w: N_HEAD0 + k for k, w in enumerate(steps)}


def parts_before(r):
    return r if r < WKV else 2 * r - WKV


def part_number(r, a):
    return parts_before(r) + (1 if a else 2)


def swa_number(r):
    return N_QKV + 12 + 28 * (r // 16) + r % 16


def lat_steps():
    out = []
    for th in range(NT):
        out.append(("E", th, 0))
        if th:
            out.append(("C", 2 * th - 1))
        out.append(("E", th, 1))
        if th:
            out.append(("B", 2 * th - 1))
        out += [("E", th, 2), ("E", th, 3), ("C", 2 * th), ("E", th, 4), ("E", th, 5), ("B", 2 * th)]
    return out + [("C", 2 * NT - 1), ("B", 2 * NT - 1)]


class Chain:

    def __init__(self, eng, sem):
        self.eng, self.sem, self.n = eng, sem, 0

    def __call__(self, ins):
        self.tick(ins)
        self.wait()

    def tick(self, ins):
        ins.then_inc(self.sem, 1)
        self.n = self.n + 1

    def wait(self):
        self.eng.wait_ge(self.sem, self.n)


def tile_width(T):
    if T_HEAD <= T < T_WO[0]:
        return (QC * P, QC * 2 * P, KVC * 4 * P)[(T - T_HEAD) % 3]
    return D


def build(nc, A):
    with ExitStack() as ctx:
        def sb(name, shape, dt=F32):
            return ctx.enter_context(nc.sbuf_tensor(name, shape, dt))

        def sem(name):
            return ctx.enter_context(nc.semaphore(name))

        ident = sb("ident", [P, P], F32R)
        ident32 = ident[:].bitcast(F32)
        ones = sb("ones", [P, P])
        band = sb("band", [P, 2, P], F32R)
        mod = sb("mod", [P, DEPTH, 6, KC])
        ada_b = sb("ada_b", [P, DEPTH, 6, KC])
        ln_gb = sb("ln_gb", [P, 4, 2, KC])
        lat_g = sb("lat_g", [P, KVC + QC])
        qk_b = sb("qk_b", [P, 10])
        wo_b = sb("wo_b", [P, KC])
        sinks = sb("sinks", [P, WH])
        neg_sinks = sb("neg_sinks", [P, WH])
        cond_in = sb("cond_in", [P, KC])
        cond = sb("cond", [P, KC])
        freq = sb("freq", [P, 8])
        vecs = sb("vecs", [P, 4, KC])
        vtmp = sb("vtmp", [P, 2, KC])
        stds = sb("stds", [P, 2, 4])
        row_max = sb("row_max", [P, 8])
        neg_max = sb("neg_max", [P, 8])
        row_sum = sb("row_sum", [P, 8])
        sink_e = sb("sink_e", [P, 8])
        row_inv = sb("row_inv", [P, 8])

        base = (nc.sbuf_base + 31) // 32 * 32
        K = 1024

        def at(name, shape, dt, kib):
            size = int(np.prod(shape[1:])) * 4
            assert base + int(kib * K) + size <= nc.sbuf_usable_end, (name, base, kib)
            return nc.alloc_sbuf_tensor_at(name, shape, dt, offset=base + int(kib * K))

        h_hi = at("h_hi", [P, KC, SEQ], F32R, 0)
        h_lo = at("h_lo", [P, KC, SEQ], F32R, 32)
        w_raw = at("w_raw", [P, RING, D], F32, 64)
        w_hi = at("w_hi", [P, RING, D], F32R, 76)
        w_lo = at("w_lo", [P, RING, D], F32R, 88)
        G = 100
        x = at("x", [P, KC, SEQ], F32, G)
        lat_hi = at("lat_hi", [P, KVC + QC, SEQ], F32R, G)
        lat_lo = at("lat_lo", [P, KVC + QC, SEQ], F32R, G + 20)
        kr_hi = at("kr_hi", [P, SEQ], F32R, G + 40)
        kr_lo = at("kr_lo", [P, SEQ], F32R, G + 44)
        q_hi = at("q_hi", [P, SEQ], F32R, G + 48)
        q_lo = at("q_lo", [P, SEQ], F32R, G + 52)
        qr = at("qr", [P, 2, SEQ], F32R, G + 56)
        k_hi = at("k_hi", [P, SEQ], F32R, G + 64)
        k_lo = at("k_lo", [P, SEQ], F32R, G + 68)
        v_hi = at("v_hi", [P, NB, VDIM], F32R, G + 72)
        v_lo = at("v_lo", [P, NB, VDIM], F32R, G + 76)
        prob = at("prob", [P, 4, SEQ], F32, G + 80)
        pt_hi = at("pt_hi", [P, 2, TH], F32R, G + 96)
        pt_lo = at("pt_lo", [P, 2, TH], F32R, G + 100)
        rt_out = at("rt_out", [P, 2, TH], F32, 24)
        rt_tmp = at("rt_tmp", [P, TH], F32, 32 + 24)
        rcos = at("rcos", [P, SEQ], F32, 28)
        rsin = at("rsin", [P, SEQ], F32, 32 + 28)
        lat32 = at("lat32", [P, KVC + QC, TH], F32, G + 80)
        lat_sq = at("lat_sq", [P, 2, TH], F32, G + 90)
        lat_ss = at("lat_ss", [P, TH], F32, G + 94)
        cos0 = at("cos0", [P, SEQ], F32, G + 96)
        sin0 = at("sin0", [P, SEQ], F32, G + 100)
        diag0 = at("diag0", [P, 4, P], F32, G + 78)
        ada_acc = at("ada_acc", [P, 2, D], F32, G + 58)
        h0 = at("h0", [P, 4, TH], F32, G + 58)
        ada_raw = at("ada_raw", [P, ADA_RING, D], F32, G + 32)
        ada0_acc = [at(f"ada0_acc{v}", [P, D], F32, 32 * (v % 2) + 12 + 4 * (v // 2)) for v in range(4)]
        ada0_raw = [at(f"ada0_raw{s}", [P, D], F32, 32 * s + 20) for s in range(2)]
        f_hi = at("f_hi", [P, 2, SEQ], F32R, G + 32)
        f_lo = at("f_lo", [P, 2, SEQ], F32R, G + 40)
        ln_sq = at("ln_sq", [P, 2, TH], F32, G + 50)
        h32 = at("h32", [P, 2, TH], F32, G + 54)
        gate_s = at("gate_s", [P, 2, TH], F32, G + 58)
        f32 = at("f32", [P, 2, TH], F32, G + 62)
        ln_tot = at("ln_tot", [P, TH], F32, G + 66)
        ln_sq8 = at("ln_sq8", [P, KC, TH], F32, G + 68)
        ada1_acc = at("ada1_acc", [P, 6, D], F32, G + 66)
        ada1_raw = at("ada1_raw", [P, 2, D], F32, G + 90)
        spos_i = at("spos_i", [P, SEQ], I32, G + 90)
        stab_k = at("stab_k", [P, TH], F32, G + 94)
        pos_i = at("pos_i", [P, SEQ], I32, G + 80)
        tab_ang = at("tab_ang", [P, SEQ], F32, G + 84)
        tab_k = at("tab_k", [P, SEQ], F32, G + 88)
        tab_t = at("tab_t", [P, SEQ], F32, G + 92)
        sq_st = at("sq_st", [P, WH, TH], F32R, G)
        sk_hi = at("sk_hi", [P, WKV, SEQ], F32R, G + 32)
        sk_lo = at("sk_lo", [P, WKV, SEQ], F32R, G + 48)
        sv_hi = at("sv_hi", [P, NB, WKV * WD], F32R, G + 64)
        sv_lo = at("sv_lo", [P, NB, WKV * WD], F32R, G + 72)
        sprob = at("sprob", [P, 2, GRP, 2 * P], F32, G + 80)
        spt_hi = at("spt_hi", [P, 2, TH], F32R, G + 88)
        spt_lo = at("spt_lo", [P, 2, TH], F32R, G + 92)
        scos = at("scos", [P, SEQ], F32, G + 96)
        ssin = at("ssin", [P, SEQ], F32, G + 100)
        sr_out = at("sr_out", [P, 2, TH], F32, G + 88)
        sr_tmp = at("sr_tmp", [P, TH], F32, G + 92)
        sv_b = at("sv_b", [P, WKV * WD], F32, G + 94)

        spad = ctx.enter_context(nc.psum_tensor("spad", [P, 4, 512], F32))
        tpad = ctx.enter_context(nc.psum_tensor("tpad", [P, 2, 512], F32))
        dpad = ctx.enter_context(nc.psum_tensor("dpad", [P, 2, 512], F32))
        spad_flat = spad[:].rearrange("p b n -> p (b n)")

        beside = ((T_HEAD % RING) * D + QC * P) * 4 / K
        v32 = [at(f"v32_{t}", [P, 4, VDIM], F32, (64, 76)[t] + beside) for t in range(2)]

        spill = nc.dram_tensor("spill", (P, KC, SEQ), F32, kind="Internal").ap()

        const_in = sem("const_in")
        c_in = sem("c_in")
        pos_in = sem("pos_in")
        spos_in = sem("spos_in")
        x_in = [sem(f"x_in{t}") for t in range(2 * NT)]
        w_in = [sem(f"w_in{s}") for s in range(RING)]
        ada_in = [sem(f"ada_in{s}") for s in range(ADA_RING)]
        ada1_in = [sem(f"ada1_in{s}") for s in range(2)]
        tab_in = sem("tab_in")
        spilled = sem("spilled")
        res_in = [sem(f"res_in{t}") for t in range(NT)]
        vbias_in = sem("vbias_in")
        stored = sem("stored")
        w_rounded = sem("w_rounded")
        w_split = sem("w_split")
        consts = sem("consts")
        ident_ok = sem("ident_ok")
        cond_ok = sem("cond_ok")
        tab_ready = sem("tab_ready")
        tab_abs = sem("tab_abs")
        tab_trig = sem("tab_trig")
        tab_sign = sem("tab_sign")
        dense_done = sem("dense_done")
        dense_free = sem("dense_free")
        ada_used = sem("ada_used")
        ada_fold = sem("ada_fold")
        mod_ok = sem("mod_ok")
        vec_ok = sem("vec_ok")
        sq_ok = sem("sq_ok")
        ss_ok = sem("ss_ok")
        stat_col = sem("stat_col")
        stat_std = sem("stat_std")
        stat_diag = sem("stat_diag")
        stat_row = sem("stat_row")
        lat_ok = sem("lat_ok")
        lat_rounded = sem("lat_rounded")
        lat_split = sem("lat_split")
        kr_ok = sem("kr_ok")
        kr_rounded = sem("kr_rounded")
        kr_split = sem("kr_split")
        hvec_ok = sem("hvec_ok")
        h32_in = sem("h32_in")
        h32_ok = sem("h32_ok")
        h_rounded = sem("h_rounded")
        h_split = sem("h_split")
        ln_sum = sem("ln_sum")
        ln_mean = sem("ln_mean")
        ln_cent = sem("ln_cent")
        ln_sqr = sem("ln_sqr")
        ln_sumsq_p = sem("ln_sumsq_p")
        ln_sumsq_v = sem("ln_sumsq_v")
        out_ok = sem("out_ok")
        ln_z = sem("ln_z")
        ln_res = sem("ln_res")
        res_scaled = sem("res_scaled")
        head_rounded = sem("head_rounded")
        rope_ok = sem("rope_ok")
        rope_rounded = sem("rope_rounded")
        s_done = sem("s_done")
        m_ok = sem("m_ok")
        e_done = sem("e_done")
        p_ok = sem("p_ok")
        t_done = sem("t_done")
        t_rounded = sem("t_rounded")
        t_split = sem("t_split")
        v_copied = sem("v_copied")
        v_split = sem("v_split")
        v_done = sem("v_done")
        o_rounded = sem("o_rounded")
        gate_done = sem("gate_done")
        up_done = sem("up_done")
        silu_ok = sem("silu_ok")
        f32_ok = sem("f32_ok")
        f_rounded = sem("f_rounded")
        f_split = sem("f_split")
        ada1_scaled = sem("ada1_scaled")
        ada1_used = sem("ada1_used")
        rot_ok = sem("rot_ok")
        rot_rounded = sem("rot_rounded")
        rot_split = sem("rot_split")
        k_stack = sem("k_stack")
        ss_done = sem("ss_done")
        sv_split = sem("sv_split")
        sm_ok = sem("sm_ok")
        se_done = sem("se_done")
        sp_ok = sem("sp_ok")
        sr_ok = sem("sr_ok")
        st_done = sem("st_done")
        sv_done = sem("sv_done")
        st_rounded = sem("st_rounded")
        st_split = sem("st_split")
        so_rounded = sem("so_rounded")
        dve_own = sem("dve_own")
        pool_own = sem("pool_own")

        DN = dense_numbers()
        block = ctx.enter_context(nc.Block())

        def halves(th):
            return slice(th * TH, th * TH + TH)

        def mean_row(L):
            return spad[:, 3, :] if L % 2 else tpad[:, 1, :]

        def res_floor(q):
            return 8 * 2 * q

        @block.sync
        def _(sp):
            ada0 = A["ada_w"][0]

            def load_ada(u):
                if u >= ADA_RING:
                    sp.wait_ge(ada_used, u - ADA_RING + 1)
                v, kc = u // KC, u % KC
                sp.dma_start(ada_raw[:, u % ADA_RING, :], ada0[kc * P:(kc + 1) * P, v * D:(v + 1) * D])\
                    .then_inc(ada_in[u % ADA_RING], 16)

            def load_w(T, src):
                if T >= RING:
                    sp.wait_ge(w_split, T - RING + 1)
                w = src.shape[-1]
                sp.dma_start(w_raw[:, T % RING, 0:w], src).then_inc(w_in[T % RING], 16)

            smalls = [(ada_b, A["ada_b"]), (ln_gb, A["ln_gb"]), (lat_g, A["lat_g"]),
                      (qk_b, A["qk_b"]), (wo_b, A["wo_b"]), (freq, A["freq"]),
                      (sinks, A["sinks"].partition_broadcast(P))]
            sp.dma_start(cond_in[:], A["cond"]).then_inc(c_in, 16)
            for u in range(2 * KC):
                load_ada(u)
                if u == 2:
                    for dst, src in smalls:
                        sp.dma_start(dst[:], src).then_inc(const_in, 16)
                    sp.dma_start(pos_i[:], A["pos"].partition_broadcast(P)).then_inc(pos_in, 16)
                if u == KC:
                    load_w(0, A["w_lat"][0])
            for th in range(NT):
                for part in range(2):
                    cs = slice(4 * part, 4 * part + 4)
                    sp.dma_start(x[:, cs, halves(th)], A["x"][:, cs, halves(th)])\
                        .then_inc(x_in[2 * th + part], 16)
                if th == 0:
                    for T in range(1, RING):
                        load_w(T, A["w_lat"][T % 6])
            for T in range(RING, T_HEAD + 3):
                load_w(T, A["w_lat"][T % 6] if T < T_HEAD else
                       [A["w_qr"], A["w_qn"], A["w_kv"]][T - T_HEAD][0])
            sp.wait_ge(tab_sign, 1)
            sp.wait_ge(dense_done, N_HEAD0)
            sp.dma_start(rcos[:], cos0[:]).then_inc(tab_in, 16)
            sp.dma_start(rsin[:], sin0[:]).then_inc(tab_in, 16)
            for p in range(1, HEADS // 2):
                for k, src in enumerate((A["w_qr"], A["w_qn"], A["w_kv"])):
                    load_w(T_HEAD + 3 * p + k, src[p])

            def residual_back(src):
                for th in range(NT):
                    sp.dma_start(x[:, :, halves(th)], src[:, :, halves(th)]).then_inc(res_in[th], 16)

            for layer in range(DEPTH):
                for s in range(NT * KC):
                    T = T_WO[layer] + s
                    if s == 0 and layer == 0:
                        sp.wait_ge(v_split, HEADS)
                    if s == 3:
                        if layer == 0:
                            sp.wait_ge(dense_done, DN["K", 1, 1, HEADS - 1] + 1)
                            residual_back(A["x"])
                        else:
                            sp.wait_ge(ss_done, NB * WKV)
                            residual_back(spill)
                    load_w(T, A["w_o"][layer, s % KC])

                def turn(i, ks=range(6)):
                    for k in ks:
                        T = T_FFN[layer] + 6 * i + k
                        T0 = T_FFN[layer] + k
                        f = 2 * i + (k % 4) // 2 if k < 4 else 2 * i + k - 4
                        src = A["w_dn"] if k >= 4 else (A["w_gt"], A["w_up"])[k % 2]
                        src = src[layer]
                        sp.wait_ge(w_split, T - RING + 1)
                        src = src[f] if isinstance(f, int) else src[ds(f, 1)].rearrange("a p n -> (a p) n")
                        sp.dma_start(w_raw[:, T0 % RING, :], src).then_inc(w_in[T0 % RING], 16)

                with sp.Fori(0, ITERS) as i:
                    turn(i)
                if layer == 0:
                    for T in range(T_QKV, T_QKV + RING):
                        load_w(T, A["w_qkv"][T - T_QKV])
                    for th in range(NT):
                        sp.wait_ge(ln_res, res_floor(1) + KC * (th + 1))
                        sp.dma_start(spill[:, :, halves(th)], x[:, :, halves(th)]).then_inc(spilled, 16)
                    for th in range(NT):
                        for k in range(12):
                            if k == RING:
                                if th:
                                    sp.wait_ge(dense_free, swa_number(15) + 1)
                                else:
                                    sp.wait_ge(tab_ready, 2)
                                sp.dma_start(sv_b[:], A["v_b"].partition_broadcast(P)).then_inc(vbias_in, 16)
                            T = T_QKV + 12 * th + k
                            if T >= T_QKV + RING:
                                load_w(T, A["w_qkv"][k])
            sp.wait_ge(spilled, 16 * NT)
            for th in range(NT):
                for c in range(KC):
                    if th == 0:
                        sp.wait_ge(out_ok, c + 1)
                    else:
                        sp.wait_ge(ln_res, res_floor(3) + c + 1)
                    sp.dma_start(A["out"][:, c, halves(th)], x[:, c, halves(th)]).then_inc(stored, 16)
            sp.wait_ge(stored, 16 * NT * KC)

        @block.tensor
        def _(pe):
            def three(out, w, x_, first, last, skip=False):
                pe.matmul(out, w[0], x_[0], start=first, stop=False, skip_group_check=skip)
                pe.matmul(out, w[0], x_[1], start=False, stop=False, skip_group_check=skip)
                return pe.matmul(out, w[1], x_[0], start=False, stop=last, skip_group_check=skip)

            def wt(T, lo, hi):
                return w_hi[:, T % RING, lo:hi], w_lo[:, T % RING, lo:hi]

            def bank(n_static):
                return dpad[:, n_static % 2, :]

            def claim(n):
                if not isinstance(n, int) or n >= 2:
                    pe.wait_ge(dense_free, n - 1)

            def dense(n, T, chunks, src, inputs=None):
                pe.wait_ge(w_split, T + 1)
                claim(n)
                for k in range(chunks):
                    if inputs is not None:
                        pe.wait_ge(h_split, inputs + k + 1)
                    mm = three(bank(n), wt(T, k * P, k * P + P), src(k), k == 0, k == chunks - 1)
                mm.then_inc(dense_done, 1)

            def h_of(th):
                return lambda k: (h_hi[:, k, halves(th)], h_lo[:, k, halves(th)])

            def stat_column(src):
                for t in range(4):
                    mm = pe.matmul(tpad[:, 0, t:t + 1], src[:, t * P:t * P + P], ones[:, 0:1],
                                   start=True, stop=True, skip_group_check=True)
                mm.then_inc(stat_col, 1)

            def stat_spread(z, diag):
                pe.wait_ge(stat_diag, z + 1)
                if 0 < z < 4:
                    pe.wait_ge(lat_ok, (0, 2, 5, 7)[z])
                elif z > 4:
                    pe.wait_ge(ln_z, KC * (z - 4))
                for t in range(4):
                    mm = pe.matmul(tpad[:, 1, t * P:t * P + P], ones[:], diag[:, t, :],
                                   start=True, stop=True, skip_group_check=True)
                mm.then_inc(stat_row, 1)

            def fold(v, acc, psum, before):
                if before:
                    pe.wait_ge(mod_ok, before)
                for c in range(KC):
                    mm = pe.matmul(psum[:, v * KC + c:v * KC + c + 1], acc[:, c * P:c * P + P], ones[:, 0:1],
                                   start=True, stop=True, skip_group_check=True)
                mm.then_inc(ada_fold, 1)

            pe.wait_ge(consts, 3)
            pe.wait_ge(ident_ok, 2)
            for v in range(2):
                pe.wait_ge(ada_used, KC * (v + 1))
                fold(v, ada_acc[:, v % 2, :], spad[:, 3, :], v)

            for step in lat_steps():
                if step[0] == "E":
                    _, th, m = step
                    dense(N_LAT + 6 * th + m, T_LAT + 6 * th + m, KC, h_of(th), KC * th if m == 0 else None)
                elif step[0] == "C":
                    z = step[1]
                    pe.wait_ge(ss_ok, 5 * (z // 2) + (2, 5)[z % 2])
                    stat_column(lat_ss)
                else:
                    stat_spread(step[1], diag0)

            def lat(lo, c):
                return lambda k: (lat_hi[:, lo + k, c], lat_lo[:, lo + k, c])

            for kind, a, b, h in head_work(PE_ORDER):
                if h == 0 and kind in "QRKW":
                    pe.wait_ge(lat_split, (2, 5, 7, 10)[2 * a + (kind in "QR")])
                p, hp = divmod(h, 2)
                T = T_HEAD + 3 * p
                e0 = 8 * h
                u0 = T_GROUPS * h
                if kind == "S":
                    i = a
                    if not (h == 0 and i < 4):
                        pe.wait_ge(e_done, e0 + i - SPREV[i][1] + 1)
                    th = i // 4
                    pe.wait_ge(dense_free, DN["K", th, th, h] + 1)
                    pe.wait_ge(rope_ok, 4 * p + 3 + th)
                    if h == 0:
                        pe.wait_ge(kr_split, NT)
                    for c0 in range(0, i + 1, 4):
                        c1 = min(c0 + 4, i + 1)
                        out = spad[:, SBANK[i] + c0 // 4, 0:(c1 - c0) * P]
                        q = slice(i * P, i * P + P)
                        keys = slice(c0 * P, c1 * P)
                        three(out, (q_hi[:, q], q_lo[:, q]), (k_hi[:, keys], k_lo[:, keys]), True, False)
                        pe.matmul(out, qr[:, hp, q], kr_hi[:, keys], start=False, stop=False)
                        mm = pe.matmul(out, qr[:, hp, q], kr_lo[:, keys], start=False, stop=c1 <= i)
                        if c1 > i:
                            mm = pe.matmul(out[:, (i - c0) * P:(i - c0) * P + P], ident[:], band[:, 1, :],
                                           start=False, stop=True)
                    mm.then_inc(s_done, 1)
                elif kind == "T":
                    g, cc = a, b
                    u = t_index(g, cc)
                    pe.wait_ge(p_ok, e0 + 2 * g + 2)
                    if u0 + u >= 2:
                        pe.wait_ge(t_split, u0 + u - 1)
                    for c in (2 * cc, 2 * cc + 1):
                        for i in (2 * g, 2 * g + 1):
                            if c <= i:
                                col = 256 if c == 2 * g + 1 else (c % 2) * 256 + (i % 2) * P
                                mm = pe.transpose(tpad[:, u % 2, col:col + P], prob[:, i % 4, c * P:c * P + P], ident32)
                    mm.then_inc(t_done, 1)
                elif kind == "V":
                    g, cc = a, b
                    u = t_index(g, cc)
                    n = DN["V", g, g, h]
                    pe.wait_ge(t_split, u0 + u + 1)
                    if cc == 0:
                        if hp:
                            pe.wait_ge(v_split, 2 * p + g // 2 + 1)
                        else:
                            pe.wait_ge(dense_free, DN["W", g // 2, 1, h] + 1)
                        claim(n)
                    for c in (2 * cc, 2 * cc + 1):
                        part = slice(P, 2 * P) if c == 2 * g + 1 else slice(0, 2 * P)
                        src = slice(256, 256 + P) if c == 2 * g + 1 else slice((c % 2) * 256, (c % 2) * 256 + 2 * P)
                        mm = three(bank(n)[:, part], (v_hi[:, c, :], v_lo[:, c, :]),
                                   (pt_hi[:, u % 2, src], pt_lo[:, u % 2, src]), c == 0, c == 2 * g + 1)
                    mm.then_inc(dense_done if cc == g else v_done, 1)
                elif kind == "A":
                    n = DN[kind, a, b, h]
                    pe.wait_ge(ada1_used, 2 * KC * (h - 1))
                    claim(n)
                    for v in range(2):
                        for c in range(KC):
                            mm = pe.matmul(bank(n)[:, v * KC + c:v * KC + c + 1],
                                           ada0_acc[2 * (h - 2) + v][:, c * P:c * P + P], ones[:, 0:1],
                                           start=True, stop=True, skip_group_check=True)
                    mm.then_inc(dense_done, 1)
                elif kind == "W":
                    if hp:
                        continue
                    n = DN[kind, a, b, h]
                    pe.wait_ge(w_split, T + 3)
                    claim(n)
                    for t in range(2):
                        tok = slice((4 * a + 2 * b + t) * P, (4 * a + 2 * b + t) * P + P)
                        out = bank(n)[:, t * 2 * P:(t + 1) * 2 * P].rearrange("p (h v) -> p h v", h=2)
                        for k in range(KVC):
                            v_cols = [w.rearrange("p (h s v) -> p h s v", h=2, s=2)[:, :, 1, :]
                                      for w in wt(T_HEAD + 2, k * 4 * P, (k + 1) * 4 * P)]
                            mm = three(out, lat(0, tok)(k), v_cols, k == 0, k == KVC - 1)
                    mm.then_inc(dense_done, 1)
                else:
                    n = DN[kind, a, b, h]
                    tile, chunks, src, step, first = {"R": (0, QC, KVC, P, 0), "Q": (1, QC, KVC, 2 * P, hp * P),
                                                      "K": (2, KVC, 0, 4 * P, 2 * hp * P)}[kind]
                    pe.wait_ge(w_split, T + tile + 1)
                    claim(n)
                    for k in range(chunks):
                        lo = k * step + first
                        mm = three(bank(n), wt(T_HEAD + tile, lo, lo + P), lat(src, halves(a))(k),
                                   k == 0, k == chunks - 1)
                    mm.then_inc(dense_done, 1)

            def ln_mean_mm(L):
                pe.wait_ge(ln_sum, L + 1)
                if L and L % 2 == 0:
                    pe.wait_ge(ln_z, KC * L)
                pe.matmul(mean_row(L), ones[:], ln_tot[:], start=True, stop=True).then_inc(ln_mean, 1)

            def ln_var_mm(L):
                pe.wait_ge(stat_std, 4 + L)
                for c, done in ((0, ln_sumsq_p), (SQ_POOL, ln_sumsq_v)):
                    pe.wait_ge(done, L + 1)
                    for t in range(4):
                        mm = pe.matmul(tpad[:, 0, t:t + 1], ln_sq8[:, c, t * P:t * P + P], ones[:, 0:1],
                                       start=c == 0 and t == 0, stop=c > 0, skip_group_check=True)
                mm.then_inc(stat_col, 1)

            def ln_spread(L):
                stat_spread(4 + L, ln_sq[:, 0, :].rearrange("p (t c) -> p t c", t=4))

            def out_proj(layer):
                for th in range(NT):
                    for c in range(KC):
                        s = KC * th + c
                        if layer == 0 and s == 0:
                            pe.wait_ge(o_rounded, 4 * HEADS)
                        if layer == 1 and s == 0:
                            pe.wait_ge(so_rounded, 2 * NB * WKV)
                        dense(N_WO[layer] + s, T_WO[layer] + s, KC, h_of(th))
                        if th == 1:
                            L = 4 * layer
                            if c == 0:
                                ln_mean_mm(L)
                            elif c == 2:
                                ln_var_mm(L)
                            elif c == 3:
                                ln_spread(L)

            def feed_forward(layer):
                jb = 44 * layer

                def turn(i, first, last):
                    T = T_FFN[layer] + 6 * i
                    T0 = T_FFN[layer]
                    for f in range(2):
                        for th in range(NT):
                            j = jb + 4 * i + 2 * f + th
                            for which, s in ((0, gate_done), (1, up_done)):
                                k = 2 * f + which
                                pe.wait_ge(w_split, T + k + 1)
                                if not (first and f == 0):
                                    pe.wait_ge((silu_ok, f32_ok)[which], j - 1)
                                for c in range(KC):
                                    if first and f == 0 and which == 0:
                                        pe.wait_ge(h_split, 16 * (2 * layer + 1) + KC * th + c + 1)
                                    mm = three(spad[:, 2 * which + th, :], wt(T0 + k, c * P, c * P + P), h_of(th)(c),
                                               c == 0, c == KC - 1)
                                mm.then_inc(s, 1)
                                if first and f == 0 and th == 0:
                                    (ln_var_mm, ln_spread)[which](4 * layer + 1)
                    for th in range(NT):
                        pe.wait_ge(f_split, jb + 4 * i + 3 + th)
                        pe.wait_ge(w_split, T + 6)
                        for c in range(KC):
                            n = N_FFN[layer] + 16 * i + KC * th + c
                            claim(n)
                            for f in range(2):
                                mm = three(bank(N_FFN[layer] + c), wt(T0 + 4 + f, c * P, c * P + P),
                                           (f_hi[:, f, halves(th)], f_lo[:, f, halves(th)]), f == 0, f == 1)
                            mm.then_inc(dense_done, 1)
                            if last and th == 1 and c == 1:
                                ln_mean_mm(4 * layer + 2)

                turn(0, True, False)
                with pe.Fori(1, ITERS - 1) as i:
                    turn(i, False, False)
                if layer == 0:
                    for v in range(6):
                        pe.wait_ge(ada1_used, 4 * KC + KC * (v + 1))
                        fold(v, ada1_acc[:, v, :], tpad[:, 0, :], None)
                turn(ITERS - 1, False, True)
                L = 4 * layer + 2
                ln_mean_mm(L + 1)
                ln_var_mm(L)
                ln_spread(L)
                ln_var_mm(L + 1)

            out_proj(0)
            ln_mean_mm(1)
            feed_forward(0)

            def qkv(th):
                for k in range(12):
                    T = T_QKV + 12 * th + k
                    n = N_QKV + 28 * th + k
                    if k == 1 and th == 0:
                        ln_spread(3)
                    if k in (2, 3):
                        pe.wait_ge(w_split, T + 1)
                        claim(n)
                        for t in range(4):
                            tok = slice(th * TH + t * P, th * TH + t * P + P)
                            for c in range(KC):
                                mm = three(bank(n)[:, t * P:t * P + P], (h_hi[:, c, tok], h_lo[:, c, tok]),
                                           wt(T, c * P, c * P + P), c == 0, c == KC - 1)
                        mm.then_inc(dense_done, 1)
                    else:
                        dense(n, T, KC, h_of(th), 16 * 2 + KC * th if k == 0 else None)

            def s_scores(r):
                b, j = divmod(r, WKV)
                lo = 0 if b else P
                sl = 2 * (r % 2)
                if r % 16 < WKV:
                    pe.wait_ge(rot_split, 16 * (b // 4) + 4 * (j + 1))
                if r >= 2:
                    pe.wait_ge(se_done, r - 1)
                q = slice((b % 4) * P, (b % 4) * P + P)
                keys = slice((b - 1) * P + lo, b * P + P)
                for half in range(2):
                    out2 = spad[:, sl + half, :].rearrange("p (g k) -> p g k", g=2)[:, :, lo:2 * P]
                    mask = band[:].rearrange("p a k -> p (a k)")[:, lo:2 * P].unsqueeze(1).to_broadcast([P, 2, 2 * P - lo])
                    pe.matmul(out2, ident[:], mask, start=True, stop=False, skip_group_check=True)
                    for g in range(2):
                        qs = sq_st[:, GRP * j + 2 * half + g, q]
                        pe.matmul(out2[:, g, :], qs, sk_hi[:, j, keys], start=False, stop=False, skip_group_check=True)
                        mm = pe.matmul(out2[:, g, :], qs, sk_lo[:, j, keys], start=False, stop=True,
                                       skip_group_check=True)
                mm.then_inc(ss_done, 1)

            def s_transpose(r, a):
                if r // WKV or a:
                    pe.wait_ge(sp_ok, r + 1)
                    if r > (0 if a else WKV):
                        pe.wait_ge(st_split, part_number(r - 1, a))
                    for g in range(GRP):
                        mm = pe.transpose(tpad[:, a, g * P:g * P + P], sprob[:, r % 2, g, a * P:a * P + P], ident32)
                    mm.then_inc(st_done, 1)

            def s_product(r, a):
                b, j = divmod(r, WKV)
                if b or a:
                    n = swa_number(r)
                    pe.wait_ge(st_split, part_number(r, a))
                    if a:
                        claim(n)
                    last = a == 0 or b == 0
                    blk = b - 1 + a
                    mm = three(bank(n)[0:WD, :], (sv_hi[:, blk, j * WD:j * WD + WD], sv_lo[:, blk, j * WD:j * WD + WD]),
                               (spt_hi[:, a, :], spt_lo[:, a, :]), a == 1, last)
                    mm.then_inc(dense_done if last else sv_done, 1)

            for th in range(NT):
                qkv(th)
                pe.wait_ge(k_stack, 8 * (th + 1))
                pe.wait_ge(sv_split, 2 * (th + 1))
                units = range(16 * th, 16 * th + 16)
                for r in range(16 * th - 2, 16 * th + 17):
                    if r + 2 in units:
                        s_scores(r + 2)
                    if r - 1 in units:
                        s_product(r - 1, 1)
                    if r in units:
                        s_transpose(r, 1)
                        s_transpose(r, 0)
                    if r - 1 in units:
                        s_product(r - 1, 0)

            out_proj(1)
            ln_mean_mm(5)
            feed_forward(1)
            ln_spread(7)

        @block.scalar
        def _(act):
            def split(T, width=D, turn=0):
                sl = T % RING
                act.wait_ge(w_in[sl], 16 * (T // RING + 1) + 32 * turn)
                act.activation(w_hi[:, sl, 0:width], w_raw[:, sl, 0:width], ACT.Copy).then_inc(w_rounded, 1)

            def split_after(T, done, value):
                if T < T_END:
                    act.wait_ge(done, value)
                    split(T, tile_width(T))

            act.wait_ge(c_in, 16)
            act.activation(cond[:], cond_in[:], ACT.Silu).then_inc(cond_ok, 1)
            act.wait_ge(consts, 5)
            act.activation(ident[:], tab_t[:, 0:P], ACT.Copy).then_inc(ident_ok, 1)
            act.activation(band[:].rearrange("p a k -> p (a k)"), tab_t[:, P:3 * P], ACT.Copy).then_inc(ident_ok, 1)

            split(0)

            def tables(t, ang, cos, sin, before=None):
                act.wait_ge(tab_ready, t + 1)
                act.activation(cos[:], ang[:], ACT.Abs).then_inc(tab_abs, 1)
                act.wait_ge(tab_abs, t + 1)
                act.activation(sin[:], ang[:], ACT.Sin).then_inc(tab_trig, 1)
                act.activation(cos[:], cos[:], ACT.Sin, scale=-1.0, bias=freq[:, 2:3]).then_inc(tab_trig, 1)

            tables(0, tab_ang, cos0, sin0)

            for th in range(NT):
                for c in range(KC):
                    act.wait_ge(h32_in, KC * th + c + 1)
                    act.activation(h_hi[:, c, halves(th)], h0[:, c % 4, :], ACT.Copy).then_inc(h_rounded, 1)
                if th == 0:
                    for T in range(1, RING):
                        split(T)

            rounded = 0
            for step in lat_steps():
                if step[0] == "E":
                    _, th, m = step
                    n = N_LAT + 6 * th + m
                    if m:
                        j = 5 * th + m - 1
                        act.wait_ge(dense_done, n + 1)
                        if j >= 2:
                            act.wait_ge(ss_ok, j - 1)
                        act.activation(lat_sq[:, j % 2, :], dpad[:, n % 2, :], ACT.Square).then_inc(sq_ok, 1)
                    else:
                        act.wait_ge(kr_ok, th + 1)
                        act.activation(kr_hi[:, halves(th)], ln_sq[:, 0, :], ACT.Copy).then_inc(kr_rounded, 1)
                    split_after(T_LAT + n + RING, dense_done, n + 1)
                elif step[0] == "C":
                    z = step[1]
                    act.wait_ge(stat_col, z + 1)
                    rank = (KVRANK, QRANK)[z % 2]
                    act.activation(stds[:, 0, :], tpad[:, 0, 0:4], ACT.Sqrt, scale=1.0 / rank, bias=freq[:, 4:5])\
                        .then_inc(stat_std, 1)
                else:
                    z = step[1]
                    th = z // 2
                    for m in ((0, 1), (2, 3, 4))[z % 2]:
                        rounded += 1
                        act.wait_ge(lat_ok, rounded)
                        act.activation(lat_hi[:, m, halves(th)], lat32[:, m, :], ACT.Copy).then_inc(lat_rounded, 1)

            def product_done(h, g, cc):
                if g == cc:
                    act.wait_ge(dense_done, DN["V", g, g, h] + 1)
                else:
                    act.wait_ge(v_done, 6 * h + g * (g - 1) // 2 + cc + 1)

            for kind, a, b, h in head_work(ACT_ORDER):
                p = h // 2
                u0 = T_GROUPS * h
                if kind == "S":
                    i = a
                    act.wait_ge(m_ok, 8 * h + i + 1)
                    if i >= 4:
                        act.wait_ge(t_done, u0 + t_index(i // 2 - 2, i // 2 - 2) + 1)
                    elif h:
                        act.wait_ge(t_done, u0 - T_GROUPS + t_index(i // 2 + 2, i // 2 + 2) + 1)
                    act.activation(prob[:, i % 4, 0:(i + 1) * P],
                                   spad_flat[:, SBANK[i] * 512:SBANK[i] * 512 + (i + 1) * P], ACT.Exp,
                                   bias=neg_max[:, i:i + 1], scale=MLA_SCALE, accum_out=row_sum[:, i:i + 1])\
                        .then_inc(e_done, 1)
                elif kind == "T":
                    g, cc = a, b
                    u = t_index(g, cc)
                    w = 384 if cc == g else 512
                    act.wait_ge(t_done, u0 + u + 1)
                    if u >= 2:
                        product_done(h, *((0, 0), (1, 0), (1, 1), (2, 0), (2, 1), (2, 2), (3, 0), (3, 1))[u - 2])
                    elif h:
                        product_done(h - 1, 3, 2 + u)
                    act.activation(pt_hi[:, u % 2, 0:w], tpad[:, u % 2, 0:w], ACT.Copy).then_inc(t_rounded, 1)
                elif kind == "R":
                    act.wait_ge(rope_ok, 4 * p + a + 1)
                    act.activation(qr[0:64, 0, halves(a)], rt_out[0:64, a, :], ACT.Copy).then_inc(rope_rounded, 1)
                    act.activation(qr[64:P, 1, halves(a)], rt_out[64:P, a, :], ACT.Copy).then_inc(rope_rounded, 1)
                elif kind == "X":
                    last = ("Q", "Q", "K")[a]
                    split_after(T_HEAD + 3 * p + 3 + a, dense_done, DN[last, 1, 1, h] + 1)
                elif kind == "W":
                    if h % 2:
                        dst, src = v_hi[:, 4 * a:4 * a + 4, :], v32[a][:]
                        act.wait_ge(v_copied, 4 * p + 2 * a + 2)
                    else:
                        n = DN[kind, a, b, h]
                        toks = slice(4 * a + 2 * b, 4 * a + 2 * b + 2)
                        both = dpad[:, n % 2, :].rearrange("p (t h v) -> p t h v", t=2, h=2)
                        act.wait_ge(dense_done, n + 1)
                        if p:
                            act.wait_ge(v_split, 2 * p)
                        act.activation(v32[a][:, 2 * b:2 * b + 2, :], both[:, :, 1, :], ACT.Copy).then_inc(v_copied, 1)
                        dst, src = v_hi[:, toks, :], both[:, :, 0, :]
                    if h:
                        product_done(h - 1, 3, 2 * a + 1)
                    act.activation(dst, src, ACT.Copy).then_inc(head_rounded, 1)
                else:
                    n = DN[kind, a, b, h]
                    act.wait_ge(dense_done, n + 1)
                    if kind == "V":
                        act.activation(h_hi[:, h, a * 256:a * 256 + 256], dpad[:, n % 2, 0:256], ACT.Copy)\
                            .then_inc(o_rounded, 1)
                        continue
                    dst = (q_hi if kind == "Q" else k_hi)[:, halves(a)]
                    act.activation(dst, dpad[:, n % 2, :], ACT.Copy).then_inc(head_rounded, 1)

            def ln_squares(L, cs=range(KC)):
                th = L % 2
                for c in cs:
                    act.wait_ge(ln_cent, KC * L + c + 1)
                    if c == 0:
                        act.wait_ge(stat_col, 4 + L)
                    act.activation(ln_sq8[:, c, :], x[:, c, halves(th)], ACT.Square).then_inc(ln_sqr, 1)

            def ln_root(L):
                act.wait_ge(stat_col, 4 + L + 1)
                act.activation(stds[:, 0, :], tpad[:, 0, 0:4], ACT.Sqrt, scale=1.0 / D, bias=freq[:, 3:4])\
                    .then_inc(stat_std, 1)

            def ln_outputs(L, last, cs=range(KC)):
                th = L % 2
                for c in cs:
                    xc = x[:, c, halves(th)]
                    if not last:
                        act.wait_ge(h32_ok, KC * L + c + 1)
                        act.activation(h_hi[:, c, halves(th)], h32[:, c % 2, :], ACT.Copy).then_inc(h_rounded, 1)
                    else:
                        act.wait_ge(ln_z, KC * L + c + 1)
                    act.activation(xc, xc, ACT.Identity, scale=vecs[:, 2, c:c + 1], bias=vecs[:, 3, c:c + 1])\
                        .then_inc(ln_res, 1)

            def out_proj(layer):
                for th in range(NT):
                    for c in range(KC):
                        s = KC * th + c
                        split_after(T_WO[layer] + s + RING, dense_done, N_WO[layer] + s + 1)
                        if th == 1:
                            L = 4 * layer
                            if c < 2:
                                ln_squares(L, range(4 * c, 4 * c + 4))
                            elif c == 2:
                                ln_root(L)
                            elif c >= 3:
                                ln_outputs(L, False, ((0, 1), (2, 3), (4, 5), (6, 7), ())[c - 3])
                ln_squares(4 * layer + 1)
                ln_root(4 * layer + 1)

            def feed_forward(layer):
                jb = 44 * layer

                def turn(i, first, last):
                    T = T_FFN[layer] + 6 * i
                    T0 = T_FFN[layer]
                    j0 = jb + 4 * i

                    def next_split(k, done, value):
                        if last and layer == DEPTH - 1 and k >= 6:
                            return
                        act.wait_ge(done, value)
                        split(T0 + k, D, i)

                    def silu(s):
                        act.wait_ge(gate_done, j0 + s + 1)
                        if not (first and s < 2):
                            act.wait_ge(f32_ok, j0 + s - 1)
                        act.activation(gate_s[:, s % 2, :], spad[:, s % 2, :], ACT.Silu).then_inc(silu_ok, 1)

                    def hi(s):
                        act.wait_ge(f32_ok, j0 + s + 1)
                        act.activation(f_hi[:, s // 2, halves(s % 2)], f32[:, s % 2, :], ACT.Copy)\
                            .then_inc(f_rounded, 1)

                    if last and layer == 0:
                        tables(1, ssin, scos, ssin)
                    silu(0)
                    if first:
                        ln_outputs(4 * layer + 1, False)
                    hi(0)
                    silu(1)
                    next_split(3, gate_done, j0 + 2)
                    hi(1)
                    next_split(4, up_done, j0 + 2)
                    silu(2)
                    hi(2)
                    silu(3)
                    next_split(5, gate_done, j0 + 4)
                    hi(3)
                    next_split(6, up_done, j0 + 4)
                    if last:
                        ln_squares(4 * layer + 2)
                    next_split(7, dense_done, N_FFN[layer] + 16 * i + 16)
                    next_split(8, dense_done, N_FFN[layer] + 16 * i + 16)

                turn(0, True, False)
                with act.Fori(1, ITERS - 1) as i:
                    turn(i, False, False)
                turn(ITERS - 1, False, True)
                L, end = 4 * layer + 2, layer == DEPTH - 1
                ln_root(L)
                ln_squares(L + 1)
                ln_root(L + 1)
                if not end:
                    ln_outputs(L, end)
                ln_outputs(L + 1, end)

            out_proj(0)
            feed_forward(0)

            def qkv(th):
                for k in range(12):
                    n = N_QKV + 28 * th + k
                    m = 12 * th + k
                    split_after(T_QKV + 12 * th + k + RING, dense_done, n + 1)
                    if k in (2, 3):
                        act.wait_ge(dense_free, n + 1)
                    else:
                        act.wait_ge(rot_ok, 10 * th + (k if k < 2 else k - 2) + 1)
                    if k < 2:
                        for part in range(2):
                            rows = slice(64 * part, 64 * part + 64)
                            for dst in range(2):
                                act.activation(sk_hi[64 * dst:64 * dst + 64, 2 * k + part, halves(th)],
                                               sr_out[rows, m % 2, :], ACT.Copy).then_inc(rot_rounded, 1)
                    elif k < 4:
                        act.activation(sv_hi[:, 4 * th:4 * th + 4, (k - 2) * P:(k - 1) * P],
                                       sr_out[:, m % 2, :].rearrange("p (t v) -> p t v", t=4), ACT.Copy)\
                            .then_inc(rot_rounded, 1)
                    else:
                        c = k - 4
                        if k == 4 and th == 0:
                            act.wait_ge(spilled, 16 * NT)
                        act.activation(sq_st[0:64, 2 * c, :], sr_out[0:64, m % 2, :], ACT.Copy).then_inc(rot_rounded, 1)
                        act.activation(sq_st[64:P, 2 * c + 1, :], sr_out[64:P, m % 2, :], ACT.Copy)\
                            .then_inc(rot_rounded, 1)

            def s_exp(r):
                b = r // WKV
                lo = 0 if b else P
                act.wait_ge(sm_ok, r + 1)
                if r >= 2:
                    act.wait_ge(st_done, parts_before(r - 1))
                sl = 4 * (r % 2)
                act.activation(sink_e[:, sl:sl + GRP], sink_e[:, sl:sl + GRP], ACT.Exp)
                for g in range(GRP):
                    mm = act.activation(sprob[:, r % 2, g, lo:2 * P],
                                        spad[:, 2 * (r % 2) + g // 2, (g % 2) * 256 + lo:(g % 2) * 256 + 256], ACT.Exp,
                                        bias=neg_max[:, sl + g:sl + g + 1], scale=SWA_SCALE,
                                        accum_out=row_sum[:, sl + g:sl + g + 1])
                mm.then_inc(se_done, 1)

            def s_round(r, a):
                if r // WKV or a:
                    act.wait_ge(st_done, part_number(r, a))
                    if r % 16 == 0 and a:
                        act.wait_ge(rot_split, r + 16)
                    if r > WKV and a:
                        act.wait_ge(sv_done, r - WKV)
                    elif r:
                        act.wait_ge(dense_done, swa_number(r - 1) + 1)
                    act.activation(spt_hi[:, a, :], tpad[:, a, :], ACT.Copy).then_inc(st_rounded, 1)

            def s_out(r):
                b, j = divmod(r, WKV)
                n = swa_number(r)
                act.wait_ge(dense_done, n + 1)
                src = dpad[0:WD, n % 2, :].rearrange("p (c e q) -> p c e q", c=2, e=2)
                for e in range(2):
                    act.activation(h_hi[64 * e:64 * e + 64, 2 * j:2 * j + 2, b * P:b * P + P], src[:, :, e, :], ACT.Copy)\
                        .then_inc(so_rounded, 1)

            for th in range(NT):
                qkv(th)
                units = range(16 * th, 16 * th + 16)
                for r in range(16 * th - 2, 16 * th + 17):
                    if r in units:
                        s_round(r, 1)
                        s_round(r, 0)
                    if r + 2 in units:
                        s_exp(r + 2)
                    if r - 1 in units:
                        s_out(r - 1)

            out_proj(1)
            feed_forward(1)

        @block.vector
        def _(dve):
            own = Chain(dve, dve_own)

            def split(T, width=D, turn=0):
                sl = T % RING
                dve.wait_ge(w_rounded, T + 1 + 6 * turn)
                dve.tensor_tensor(w_lo[:, sl, 0:width], w_raw[:, sl, 0:width], w_hi[:, sl, 0:width].bitcast(F32),
                                  ALU.subtract).then_inc(w_split, 1)

            def split_if(T):
                if T < T_END:
                    split(T, tile_width(T))

            def add_ada(u):
                v, kc = u // KC, u % KC
                dve.wait_ge(ada_in[u % ADA_RING], 16 * (u // ADA_RING + 1))
                acc = ada_acc[:, v % 2, :]
                if kc == 0:
                    if v >= 2:
                        dve.wait_ge(ada_fold, v - 1)
                    dve.tensor_scalar(acc, ada_raw[:, u % ADA_RING, :], cond[:, 0:1], None, ALU.mult).then_inc(ada_used, 1)
                else:
                    dve.wait_ge(ada_used, u)
                    dve.scalar_tensor_tensor(acc, ada_raw[:, u % ADA_RING, :], cond[:, kc:kc + 1], acc, ALU.mult, ALU.add)\
                        .then_inc(ada_used, 1)

            def finish_mod(layer, v, psum):
                dve.wait_ge(ada_fold, 6 * layer + v + 1)
                dve.tensor_tensor(mod[:, layer, v, :], psum[:, v * KC:v * KC + KC], ada_b[:, layer, v, :], ALU.add)\
                    .then_inc(mod_ok, 1)

            def split_h(idx, c, src, th):
                dve.wait_ge(h_rounded, idx + 1)
                dve.tensor_tensor(h_lo[:, c, halves(th)], src, h_hi[:, c, halves(th)].bitcast(F32), ALU.subtract)\
                    .then_inc(h_split, 1)

            dve.wait_ge(cond_ok, 1)
            for u in range(2 * KC):
                add_ada(u)
            split(0)
            finish_mod(0, 0, spad[:, 3, :])
            finish_mod(0, 1, spad[:, 3, :])
            dve.wait_ge(mod_ok, 2)
            dve.tensor_scalar(vecs[:, 0, :], mod[:, 0, 1, :], 1.0, None, ALU.add).then_inc(hvec_ok, 1)
            for th in range(NT):
                for c in range(KC if th == 0 else 4):
                    split_h(KC * th + c, c, h0[:, c % 4, :], th)
                if th == 0:
                    for T in range(1, RING):
                        split(T)

            def inverse_diag(z, diag):
                dve.wait_ge(stat_std, z + 1)
                own(dve.reciprocal(stds[:, 1, :], stds[:, 0, :]))
                for t in range(4):
                    ins = dve.tensor_scalar(diag[:, t, :], ident32, stds[:, 1, t:t + 1], None, ALU.mult)
                ins.then_inc(stat_diag, 1)

            def rotate(n, n0, cos, sin, out, tmp, bias=None):
                ps = dpad[:, n0 % 2, :]
                dve.wait_ge(dense_done, n + 1)
                for qd in range(4):
                    a = slice(32 * qd, 32 * qd + 32)
                    b = slice(32 * (qd ^ 1), 32 * (qd ^ 1) + 32)
                    if bias is None:
                        own.tick(dve.tensor_tensor(tmp[a, :], ps[b, :], sin[b, :], ALU.mult))
                    else:
                        own.tick(dve.scalar_tensor_tensor(tmp[a, :], ps[b, :], bias[b, :], sin[b, :], ALU.add, ALU.mult))
                if bias is None:
                    dve.tensor_tensor(out, ps, cos, ALU.mult).then_inc(dense_free, 1)
                else:
                    dve.scalar_tensor_tensor(out, ps, bias, cos, ALU.add, ALU.mult).then_inc(dense_free, 1)
                own.wait()
                dve.wait_ge(dense_free, n + 1)
                return dve.tensor_tensor(out, out, tmp, ALU.add)

            normed = 0
            for step in lat_steps():
                if step[0] == "E":
                    _, th, m = step
                    n = N_LAT + 6 * th + m
                    if m:
                        j = 5 * th + m - 1
                        dve.wait_ge(sq_ok, j + 1)
                        if th:
                            dve.wait_ge(lat_split, 2 if m <= KVC else 5)
                        dve.tensor_copy(lat32[:, m - 1, :], dpad[:, n % 2, :]).then_inc(dense_free, 1)
                        if m in (1, 3):
                            if j:
                                dve.wait_ge(stat_col, 2 * th + (m == 3))
                            dve.tensor_copy(lat_ss[:], lat_sq[:, j % 2, :]).then_inc(ss_ok, 1)
                        else:
                            dve.wait_ge(ss_ok, j)
                            dve.tensor_tensor(lat_ss[:], lat_ss[:], lat_sq[:, j % 2, :], ALU.add).then_inc(ss_ok, 1)
                    else:
                        if th == 0:
                            dve.wait_ge(tab_trig, 2)
                            dve.wait_ge(tab_sign, 1)
                        rotate(n, n, cos0[:, halves(th)], sin0[:, halves(th)], ln_sq[:, 0, :], ln_sq[:, 1, :])\
                            .then_inc(kr_ok, 1)
                        if th == 0:
                            for c in range(4, KC):
                                split_h(KC + c, c, h0[:, c % 4, :], 1)
                        dve.wait_ge(kr_rounded, th + 1)
                        dve.tensor_tensor(kr_lo[:, halves(th)], ln_sq[:, 0, :], kr_hi[:, halves(th)].bitcast(F32),
                                          ALU.subtract).then_inc(kr_split, 1)
                    split_if(T_LAT + n + RING)
                elif step[0] == "C":
                    inverse_diag(step[1], diag0)
                else:
                    z = step[1]
                    dve.wait_ge(stat_row, z + 1)
                    ms = ((0, 1), (2, 3, 4))[z % 2]
                    dve.wait_ge(dense_free, N_LAT + 6 * (z // 2) + (3, 6)[z % 2])
                    for m in ms:
                        dve.scalar_tensor_tensor(lat32[:, m, :], lat32[:, m, :], lat_g[:, m:m + 1], tpad[:, 1, :],
                                                 ALU.mult, ALU.mult).then_inc(lat_ok, 1)
                    for m in ms:
                        normed += 1
                        dve.wait_ge(lat_rounded, normed)
                        dve.tensor_tensor(lat_lo[:, m, halves(z // 2)], lat32[:, m, :],
                                          lat_hi[:, m, halves(z // 2)].bitcast(F32), ALU.subtract).then_inc(lat_split, 1)

            dve.wait_ge(tab_in, 32)
            for kind, a, b, h in head_work(DVE_ORDER):
                p = h // 2
                if kind == "S":
                    i = a
                    dve.wait_ge(s_done, 8 * h + i + 1)
                    own(dve.tensor_reduce(row_max[:, i:i + 1], spad_flat[:, SBANK[i] * 512:SBANK[i] * 512 + (i + 1) * P],
                                          AX, ALU.max))
                    dve.tensor_scalar(neg_max[:, i:i + 1], row_max[:, i:i + 1], -MLA_SCALE, None, ALU.mult)\
                        .then_inc(m_ok, 1)
                elif kind == "N":
                    i = a
                    dve.wait_ge(e_done, 8 * h + i + 1)
                    own(dve.reciprocal(row_inv[:, i:i + 1], row_sum[:, i:i + 1]))
                    dve.tensor_scalar(prob[:, i % 4, 0:(i + 1) * P], prob[:, i % 4, 0:(i + 1) * P],
                                      row_inv[:, i:i + 1], None, ALU.mult).then_inc(p_ok, 1)
                elif kind == "T":
                    u = t_index(a, b)
                    w = 384 if a == b else 512
                    dve.wait_ge(t_rounded, T_GROUPS * h + u + 1)
                    dve.tensor_tensor(pt_lo[:, u % 2, 0:w], tpad[:, u % 2, 0:w], pt_hi[:, u % 2, 0:w].bitcast(F32),
                                      ALU.subtract).then_inc(t_split, 1)
                elif kind == "R":
                    if a:
                        dve.wait_ge(rope_ok, 4 * p + 1)
                    n = DN[kind, a, b, h]
                    rotate(n, n, rcos[:, halves(a)], rsin[:, halves(a)], rt_out[:, a, :], rt_tmp[:]).then_inc(rope_ok, 1)
                elif kind == "L":
                    dve.wait_ge(rope_rounded, 4 * p + 2 * a + 2)
                    dve.tensor_tensor(qr[64:P, 0, halves(a)], rt_out[0:64, a, :],
                                      qr[0:64, 0, halves(a)].bitcast(F32), ALU.subtract)
                    dve.tensor_tensor(qr[0:64, 1, halves(a)], rt_out[64:P, a, :],
                                      qr[64:P, 1, halves(a)].bitcast(F32), ALU.subtract).then_inc(rope_ok, 1)
                elif kind == "X":
                    split_if(T_HEAD + 3 * p + 3 + a)
                elif kind == "A":
                    n = DN[kind, a, b, h]
                    v = 2 * (h - 1)
                    dve.wait_ge(dense_done, n + 1)
                    dve.tensor_tensor(mod[:, 0, v:v + 2].rearrange("p v c -> p (v c)"), dpad[:, n % 2, 0:2 * KC],
                                      ada_b[:, 0, v:v + 2].rearrange("p v c -> p (v c)"), ALU.add)\
                        .then_inc(dense_free, 1)
                elif kind == "W":
                    if h % 2:
                        dve.wait_ge(head_rounded, 14 * p + 8 + 4 + a + 1)
                        dve.tensor_tensor(v_lo[:, 4 * a:4 * a + 4, :], v32[a][:], v_hi[:, 4 * a:4 * a + 4, :].bitcast(F32),
                                          ALU.subtract).then_inc(v_split, 1)
                    else:
                        n = DN[kind, a, b, h]
                        toks = slice(4 * a + 2 * b, 4 * a + 2 * b + 2)
                        dve.wait_ge(head_rounded, 14 * p + 4 + 2 * a + b + 1)
                        dve.tensor_tensor(v_lo[:, toks, :],
                                          dpad[:, n % 2, :].rearrange("p (t h v) -> p t h v", t=2, h=2)[:, :, 0, :],
                                          v_hi[:, toks, :].bitcast(F32), ALU.subtract).then_inc(dense_free, 1)
                else:
                    n = DN[kind, a, b, h]
                    if kind == "V":
                        dve.wait_ge(o_rounded, 4 * h + a + 1)
                        cols = slice(a * 256, a * 256 + 256)
                        lo, hi, ps = h_lo[:, h, cols], h_hi[:, h, cols], dpad[:, n % 2, 0:256]
                    else:
                        dve.wait_ge(head_rounded, 14 * p + 8 * (h % 2) + 2 * (kind == "K") + a + 1)
                        ps = dpad[:, n % 2, :]
                        lo, hi = (v[:, halves(a)] for v in ((q_lo, q_hi) if kind == "Q" else (k_lo, k_hi)))
                    dve.tensor_tensor(lo, ps, hi.bitcast(F32), ALU.subtract).then_inc(dense_free, 1)

            def norm_vectors(q):
                g, b = ln_gb[:, q, 0, :], ln_gb[:, q, 1, :]
                if q:
                    dve.wait_ge(ln_res, res_floor(q))
                    dve.wait_ge(vec_ok, q)
                if q == 3:
                    own(dve.tensor_copy(vecs[:, 2, :], g))
                    dve.tensor_copy(vecs[:, 3, :], b).then_inc(vec_ok, 1)
                    return
                layer, sh = ((0, 3), (1, 0), (1, 3))[q]
                dve.wait_ge(mod_ok, 2 + 6 * layer)
                own(dve.tensor_scalar(vtmp[:, 0, :], mod[:, layer, sh + 1, :], 1.0, None, ALU.add))
                own(dve.tensor_tensor(vecs[:, 0, :], g, vtmp[:, 0, :], ALU.mult))
                own(dve.tensor_tensor(vtmp[:, 1, :], b, vtmp[:, 0, :], ALU.mult))
                own(dve.tensor_tensor(vecs[:, 1, :], vtmp[:, 1, :], mod[:, layer, sh, :], ALU.add))
                own(dve.tensor_scalar(vecs[:, 2, :], g, ALPHA, None, ALU.mult))
                if q == 1:
                    own(dve.tensor_tensor(vtmp[:, 0, :], wo_b[:], mod[:, 1, 2, :], ALU.mult))
                    dve.scalar_tensor_tensor(vecs[:, 3, :], b, ALPHA, vtmp[:, 0, :], ALU.mult, ALU.add)\
                        .then_inc(vec_ok, 1)
                else:
                    dve.tensor_scalar(vecs[:, 3, :], b, ALPHA, None, ALU.mult).then_inc(vec_ok, 1)

            def ln_total(L, c, n):
                c0 = halves(L % 2)
                dve.wait_ge(dense_free, n)
                if c == 2:
                    if L:
                        dve.wait_ge(ln_mean, L)
                    own.tick(dve.tensor_tensor(ln_tot[:], x[:, 0, c0], x[:, 1, c0], ALU.add))
                elif c > 2:
                    own.wait()
                    own.tick(dve.tensor_tensor(ln_tot[:], ln_tot[:], x[:, c - 1, c0], ALU.add))

            def ln_total_last(L, n):
                own.wait()
                dve.wait_ge(dense_free, n + 1)
                dve.tensor_tensor(ln_tot[:], ln_tot[:], x[:, KC - 1, halves(L % 2)], ALU.add).then_inc(ln_sum, 1)

            def ln_center(L, cs=range(KC)):
                c0 = halves(L % 2)
                for c in cs:
                    if c == 0:
                        dve.wait_ge(ln_mean, L + 1)
                    dve.scalar_tensor_tensor(x[:, c, c0], mean_row(L), -1.0 / D, x[:, c, c0], ALU.mult, ALU.add)\
                        .then_inc(ln_cent, 1)

            def ln_squares_sum(L):
                acc = ln_sq8[:, SQ_POOL, :]
                for c in range(SQ_POOL + 1, KC):
                    dve.wait_ge(ln_sqr, KC * L + c + 1)
                    ins = dve.tensor_tensor(acc, acc, ln_sq8[:, c, :], ALU.add)
                    if c < KC - 1:
                        own(ins)
                    else:
                        ins.then_inc(ln_sumsq_v, 1)

            def ln_inverse(L):
                inverse_diag(4 + L, ln_sq[:, 0, :].rearrange("p (t c) -> p t c", t=4))

            def ln_scale(L, last, cs=range(KC + 2)):
                c0 = halves(L % 2)
                for c in cs:
                    if c == 0:
                        dve.wait_ge(stat_row, 4 + L + 1)
                        dve.wait_ge(ln_cent, KC * (L + 1))
                    if c < KC:
                        dve.tensor_tensor(x[:, c, c0], x[:, c, c0], tpad[:, 1, :], ALU.mult).then_inc(ln_z, 1)
                    if c >= 2 and not last:
                        split_h(16 + KC * L + c - 2, c - 2, h32[:, c % 2, :], L % 2)

            def add_out(layer, n, n0, c, th, which):
                dve.wait_ge(dense_done, n + 1)
                dve.scalar_tensor_tensor(x[:, c, halves(th)], dpad[:, n0 % 2, :], mod[:, layer, which, c:c + 1],
                                         x[:, c, halves(th)], ALU.mult, ALU.add).then_inc(dense_free, 1)

            def out_proj(layer):
                for th in range(NT):
                    for c in range(KC):
                        s = KC * th + c
                        n = N_WO[layer] + s
                        if layer == 0:
                            dve.wait_ge(res_scaled, s + 1)
                        else:
                            dve.wait_ge(res_in[th], 32)
                        add_out(layer, n, n, c, th, 2)
                        split_if(T_WO[layer] + s + RING)
                        ln_total(4 * layer + th, c, n)
                        if s == KC - 1:
                            ln_total_last(4 * layer, n)
                            norm_vectors(2 * layer)
                        if th == 1:
                            L = 4 * layer
                            if c < 2:
                                ln_center(L, range(4 * c, 4 * c + 4))
                                if c == 1:
                                    ln_squares_sum(L)
                            elif c == 2:
                                ln_inverse(L)
                            else:
                                ln_scale(L, False, ((0, 1, 2, 3), (4, 5), (6, 7), (8, 9), ())[c - 3])
                L = 4 * layer + 1
                ln_total_last(L, N_WO[layer] + NT * KC - 1)
                ln_center(L)
                ln_squares_sum(L)
                ln_inverse(L)

            def feed_forward(layer):
                jb = 44 * layer

                def turn(i, first, last):
                    T = T_FFN[layer] + 6 * i
                    T0 = T_FFN[layer]
                    j0 = jb + 4 * i

                    def next_split(k):
                        if last and layer == DEPTH - 1 and k >= 6:
                            return
                        split(T0 + k, D, i)

                    def product(s):
                        dve.wait_ge(up_done, j0 + s + 1)
                        dve.wait_ge(silu_ok, j0 + s + 1)
                        if not (first and s < 2):
                            dve.wait_ge(f_split, j0 + s - 1)
                        dve.tensor_tensor(f32[:, s % 2, :], spad[:, 2 + s % 2, :], gate_s[:, s % 2, :], ALU.mult)\
                            .then_inc(f32_ok, 1)

                    def lo(s):
                        dve.wait_ge(f_rounded, j0 + s + 1)
                        part = halves(s % 2)
                        dve.tensor_tensor(f_lo[:, s // 2, part], f32[:, s % 2, :], f_hi[:, s // 2, part].bitcast(F32),
                                          ALU.subtract).then_inc(f_split, 1)

                    product(0)
                    if first:
                        ln_scale(4 * layer + 1, False)
                    lo(0)
                    next_split(3)
                    product(1)
                    lo(1)
                    next_split(4)
                    product(2)
                    lo(2)
                    next_split(5)
                    product(3)
                    lo(3)
                    L = 4 * layer + 2
                    for th in range(NT):
                        for c in range(KC):
                            k = KC * th + c
                            n = N_FFN[layer] + 16 * i + k
                            if first:
                                dve.wait_ge(ln_res, 16 * (2 * layer) + k + 1)
                            else:
                                dve.wait_ge(dense_free, n - 15)
                            add_out(layer, n, N_FFN[layer] + k, c, th, 5)
                            if k == 1:
                                next_split(6)
                            if last:
                                ln_total(L + th, c, n)
                                if c == KC - 1:
                                    ln_total_last(L + th, n)
                                    if th == 0:
                                        norm_vectors(L // 2)
                                if th == 1 and c >= 2:
                                    ln_center(L, [c - 2])
                    if last:
                        ln_center(L, [KC - 2, KC - 1])
                        ln_squares_sum(L)
                    next_split(7)
                    next_split(8)

                turn(0, True, False)
                with dve.Fori(1, ITERS - 1) as i:
                    turn(i, False, False)
                if layer == 0:
                    dve.wait_ge(ada_fold, 2 + 6)
                    dve.tensor_tensor(mod[:, 1].rearrange("p v c -> p (v c)"), tpad[:, 0, 0:6 * KC],
                                      ada_b[:, 1].rearrange("p v c -> p (v c)"), ALU.add).then_inc(mod_ok, 6)
                turn(ITERS - 1, False, True)
                L, end = 4 * layer + 2, layer == DEPTH - 1
                if end:
                    ln_center(L + 1, range(0, 3))
                    ln_inverse(L)
                    ln_center(L + 1, range(3, KC))
                else:
                    ln_center(L + 1)
                    ln_inverse(L)
                ln_squares_sum(L + 1)
                ln_scale(L, end)
                ln_inverse(L + 1)
                ln_scale(L + 1, end)

            out_proj(0)
            feed_forward(0)

            def qkv(th):
                for k in range(12):
                    n = N_QKV + 28 * th + k
                    m = 12 * th + k
                    out = sr_out[:, m % 2, :]
                    if m >= 2 and k >= 6:
                        dve.wait_ge(rot_split, 16 * th + 2 * (k - 5))
                    if k < 2 or k >= 4:
                        if k == 0:
                            dve.wait_ge(tab_trig, 4)
                            dve.wait_ge(tab_sign, 2)
                            if th == 0:
                                dve.wait_ge(h_split, 48)
                            else:
                                dve.wait_ge(st_done, parts_before(16 * th))
                        bcol = k if k < 2 else k - 2
                        if k in (4, 5):
                            dve.wait_ge(sv_split, 2 * th + k - 3)
                        if bcol or th:
                            dve.wait_ge(rot_ok, 10 * th + bcol)
                        rotate(n, n, scos[:, halves(th)], ssin[:, halves(th)], out, sr_tmp[:], qk_b[:, bcol:bcol + 1])\
                            .then_inc(rot_ok, 1)
                    else:
                        dve.wait_ge(vbias_in, 16 * (th + 1))
                        dve.wait_ge(k_stack, 8 * th + 4 * (k - 1))
                        dve.wait_ge(dense_done, n + 1)
                        bias = sv_b[:, (k - 2) * P:(k - 1) * P].unsqueeze(1).to_broadcast([P, 4, P])
                        dve.tensor_tensor(out.rearrange("p (t v) -> p t v", t=4),
                                          dpad[:, n % 2, :].rearrange("p (t v) -> p t v", t=4), bias, ALU.add)\
                            .then_inc(dense_free, 1)
                        dve.wait_ge(rot_rounded, 26 * th + 8 + (k - 1))
                        dve.tensor_tensor(sv_lo[:, 4 * th:4 * th + 4, (k - 2) * P:(k - 1) * P],
                                          out.rearrange("p (t v) -> p t v", t=4),
                                          sv_hi[:, 4 * th:4 * th + 4, (k - 2) * P:(k - 1) * P].bitcast(F32),
                                          ALU.subtract).then_inc(sv_split, 1)
                    split_if(T_QKV + 12 * th + k + RING)

            def s_max(r):
                b, j = divmod(r, WKV)
                lo = 0 if b else P
                sl = 4 * (r % 2)
                cols = slice(sl, sl + GRP)
                dve.wait_ge(ss_done, r + 1)
                src = spad[:, 2 * (r % 2):2 * (r % 2) + 2, :].rearrange("p b (g k) -> p (b g) k", g=2)[:, :, lo:2 * P]
                own(dve.tensor_reduce(row_max[:, cols], src, AX, ALU.max))
                own(dve.scalar_tensor_tensor(neg_max[:, cols], row_max[:, cols], -SWA_SCALE,
                                             neg_sinks[:, GRP * j:GRP * j + GRP], ALU.mult, ALU.min))
                dve.tensor_tensor(sink_e[:, cols], sinks[:, GRP * j:GRP * j + GRP], neg_max[:, cols], ALU.add)\
                    .then_inc(sm_ok, 1)

            def s_inverse(r):
                cols = slice(4 * (r % 2), 4 * (r % 2) + GRP)
                dve.wait_ge(se_done, r + 1)
                own(dve.tensor_tensor(row_sum[:, cols], row_sum[:, cols], sink_e[:, cols], ALU.add))
                dve.reciprocal(row_inv[:, cols], row_sum[:, cols]).then_inc(sr_ok, 1)

            def s_low(r, a):
                if r // WKV or a:
                    dve.wait_ge(st_rounded, part_number(r, a))
                    dve.tensor_tensor(spt_lo[:, a, :], tpad[:, a, :], spt_hi[:, a, :].bitcast(F32), ALU.subtract)\
                        .then_inc(st_split, 1)

            def s_out(r):
                b, j = divmod(r, WKV)
                n = swa_number(r)
                src = dpad[0:WD, n % 2, :].rearrange("p (c e q) -> p c e q", c=2, e=2)
                dve.wait_ge(so_rounded, 2 * r + 2)
                for e in range(2):
                    rows, cs, cols = slice(64 * e, 64 * e + 64), slice(2 * j, 2 * j + 2), slice(b * P, b * P + P)
                    ins = dve.tensor_tensor(h_lo[rows, cs, cols], src[:, :, e, :], h_hi[rows, cs, cols].bitcast(F32),
                                            ALU.subtract)
                ins.then_inc(dense_free, 1)

            own(dve.tensor_scalar(neg_sinks[:], sinks[:], -1.0, None, ALU.mult))
            for th in range(NT):
                qkv(th)
                units = range(16 * th, 16 * th + 16)
                for r in range(16 * th - 2, 16 * th + 18):
                    if r + 2 in units:
                        s_max(r + 2)
                    if r + 1 in units:
                        s_inverse(r + 1)
                    if r - 2 in units:
                        s_out(r - 2)
                    if r in units:
                        s_low(r, 1)
                        s_low(r, 0)

            out_proj(1)
            feed_forward(1)

        @block.gpsimd
        def _(pool):
            own = Chain(pool, pool_own)
            pool.memset(ones[:], 1.0).then_inc(consts, 1)
            pool.memset(tab_t[:, 0:3 * P], 0.0).then_inc(consts, 1)
            pool.wait_ge(consts, 2)
            pool.affine_select(out=tab_t[:, 0:P], in_=tab_t[:, 0:P], compare_op=ALU.not_equal, fill=1.0, base=0,
                               pattern=[[-1, P]], channel_multiplier=1).then_inc(consts, 1)
            pool.affine_select(out=tab_t[:, P:2 * P], in_=tab_t[:, P:2 * P], compare_op=ALU.is_gt, fill=MASKED, base=0,
                               pattern=[[1, P]], channel_multiplier=-1).then_inc(consts, 1)
            pool.affine_select(out=tab_t[:, 2 * P:3 * P], in_=tab_t[:, 2 * P:3 * P], compare_op=ALU.is_ge, fill=MASKED,
                               base=0, pattern=[[-1, P]], channel_multiplier=1).then_inc(consts, 1)
            pool.wait_ge(ident_ok, 2)
            pool.wait_ge(pos_in, 16)
            TWO_PI_PARTS = (6.28125, 0.0019350051879882812, 3.0199159819591595e-07)
            NEAREST = 1.5 * 2.0 ** 23
            PI_BELOW = 3.1415925

            def angles(t, pos, ang, k, tmp):
                own(pool.tensor_copy(tmp, pos))
                own(pool.tensor_scalar(ang, tmp, freq[:, t:t + 1], 1.0, ALU.mult, ALU.mult))
                own(pool.tensor_scalar(k, ang, 1.0 / (2.0 * np.pi), NEAREST, ALU.mult, ALU.add))
                own(pool.tensor_scalar(k, k, -NEAREST, -1.0, ALU.add, ALU.mult))
                for part in TWO_PI_PARTS:
                    own(pool.tensor_scalar(tmp, k, part, 1.0, ALU.mult, ALU.mult))
                    own(pool.tensor_tensor(ang, ang, tmp, ALU.add))
                return pool.tensor_scalar(ang, ang, PI_BELOW, -PI_BELOW, ALU.min, ALU.max)

            def sine_sign(t, sin):
                pool.wait_ge(tab_trig, 2 * t + 1)
                pool.tensor_scalar(sin[:], sin[:], freq[:, 5:6], 1.0, ALU.mult, ALU.mult).then_inc(tab_sign, 1)

            pool.wait_ge(const_in, 16 * 7)
            angles(1, pos_i[:], tab_ang[:], tab_k[:], tab_t[:]).then_inc(tab_ready, 1)
            sine_sign(0, sin0)

            pool.wait_ge(hvec_ok, 1)
            for th in range(NT):
                for c in range(KC):
                    pool.wait_ge(x_in[2 * th + c // 4], 16)
                    if KC * th + c >= 4:
                        pool.wait_ge(h_split, KC * th + c - 3)
                    pool.tensor_scalar(h0[:, c % 4, :], x[:, c, halves(th)], vecs[:, 0, c:c + 1], mod[:, 0, 0, c:c + 1],
                                       ALU.mult, ALU.add).then_inc(h32_in, 1)

            def load_ada(u, raw):
                layer, v, kc = (0, 2 + u // KC, u % KC) if u < 4 * KC else (1, u // KC - 4, u % KC)
                pool.dma_start(raw[u % 2], A["ada_w"][layer][kc * P:(kc + 1) * P, v * D:(v + 1) * D])\
                    .then_inc(ada1_in[u % 2], 16)

            def ada_vectors(lo, hi, raw, acc):
                for u in (lo, lo + 1):
                    load_ada(u, raw)
                for u in range(lo, hi):
                    kc, sum_ = u % KC, acc[(u - lo) // KC]
                    pool.wait_ge(ada1_in[u % 2], 16 * (u // 2 + 1))
                    pool.tensor_scalar(raw[u % 2] if kc else sum_, raw[u % 2], cond[:, kc:kc + 1], 1.0, ALU.mult, ALU.mult)\
                        .then_inc(ada1_scaled if kc else ada1_used, 1)
                    if kc:
                        pool.wait_ge(ada1_scaled, u - u // KC)
                        pool.wait_ge(ada1_used, u)
                        pool.tensor_tensor(sum_, sum_, raw[u % 2], ALU.add).then_inc(ada1_used, 1)
                    if u + 2 < hi:
                        pool.wait_ge(ada1_used, u + 1)
                        load_ada(u + 2, raw)

            pool.wait_ge(cond_ok, 1)
            pool.wait_ge(dense_done, N_HEAD0)
            ada_vectors(0, 4 * KC, [t[:] for t in ada0_raw], [t[:] for t in ada0_acc])

            for th in range(NT):
                pool.wait_ge(res_in[th], 16)
                for c in range(KC):
                    xc = x[:, c, halves(th)]
                    pool.tensor_scalar(xc, xc, ALPHA, 1.0, ALU.mult, ALU.mult).then_inc(res_scaled, 1)

            def squares_sum(L):
                acc = ln_sq8[:, 0, :]
                for c in range(1, SQ_POOL):
                    pool.wait_ge(ln_sqr, KC * L + c + 1)
                    ins = pool.tensor_tensor(acc, acc, ln_sq8[:, c, :], ALU.add)
                    if c < SQ_POOL - 1:
                        own(ins)
                    else:
                        ins.then_inc(ln_sumsq_p, 1)

            def modulate(L):
                pool.wait_ge(vec_ok, L // 2 + 1)
                for c in range(KC):
                    pool.wait_ge(ln_z, KC * L + c + 1)
                    pool.wait_ge(h_split, 16 + KC * L + c - 1)
                    pool.tensor_scalar(h32[:, c % 2, :], x[:, c, halves(L % 2)], vecs[:, 0, c:c + 1], vecs[:, 1, c:c + 1],
                                       ALU.mult, ALU.add).then_inc(h32_ok, 1)

            squares_sum(0)
            modulate(0)
            squares_sum(1)
            modulate(1)

            pool.wait_ge(f_split, 1)
            ada_vectors(4 * KC, 10 * KC, [ada1_raw[:, t, :] for t in range(2)], [ada1_acc[:, v, :] for v in range(6)])
            pool.wait_ge(ada1_used, 10 * KC)
            pool.dma_start(spos_i[:], A["pos"].partition_broadcast(P)).then_inc(spos_in, 16)
            pool.wait_ge(spos_in, 16)
            for th in range(NT):
                ins = angles(0, spos_i[:, halves(th)], ssin[:, halves(th)], stab_k[:], scos[:, halves(th)])
                if th == 0:
                    own(ins)
                else:
                    ins.then_inc(tab_ready, 1)
            sine_sign(1, ssin)
            squares_sum(2)
            squares_sum(3)
            modulate(2)
            modulate(3)

            for th in range(NT):
                for k in range(2):
                    pool.wait_ge(rot_rounded, 26 * th + 4 * k + 4)
                    for part in range(2):
                        rows = slice(64 * part, 64 * part + 64)
                        for dst in (rows, slice(64 - 64 * part, P - 64 * part)):
                            pool.tensor_tensor(sk_lo[dst, 2 * k + part, halves(th)], sr_out[rows, k, :],
                                               sk_hi[rows, 2 * k + part, halves(th)].bitcast(F32), ALU.subtract)\
                                .then_inc(k_stack, 1)
                for c in range(8):
                    m = 12 * th + 4 + c
                    pool.wait_ge(rot_rounded, 26 * th + 10 + 2 * c + 2)
                    pool.tensor_tensor(sq_st[64:P, 2 * c, :], sr_out[0:64, m % 2, :], sq_st[0:64, 2 * c, :].bitcast(F32),
                                       ALU.subtract).then_inc(rot_split, 1)
                    pool.tensor_tensor(sq_st[0:64, 2 * c + 1, :], sr_out[64:P, m % 2, :],
                                       sq_st[64:P, 2 * c + 1, :].bitcast(F32), ALU.subtract).then_inc(rot_split, 1)
                pool.wait_ge(rot_split, 16 * (th + 1))
                for r in range(16 * th, 16 * th + 16):
                    lo = 0 if r // WKV else P
                    pool.wait_ge(sr_ok, r + 1)
                    for g in range(GRP):
                        pr = sprob[:, r % 2, g, lo:2 * P]
                        col = 4 * (r % 2) + g
                        ins = pool.tensor_scalar(pr, pr, row_inv[:, col:col + 1], 1.0, ALU.mult, ALU.mult)
                    ins.then_inc(sp_ok, 1)
            squares_sum(4)
            modulate(4)
            squares_sum(5)
            modulate(5)
            squares_sum(6)
            squares_sum(7)
            pool.wait_ge(vec_ok, 4)
            for c in range(KC):
                xc = x[:, c, halves(0)]
                pool.wait_ge(ln_z, KC * 6 + c + 1)
                pool.tensor_scalar(xc, xc, vecs[:, 2, c:c + 1], vecs[:, 3, c:c + 1], ALU.mult, ALU.add).then_inc(out_ok, 1)



def _tiles(w):
    k, n = w.shape
    return np.ascontiguousarray(w.reshape(k // P, P, n // P, P).transpose(2, 1, 0, 3)).reshape(n // P, P, k)


def _rotary_order(w):
    w = w.reshape(w.shape[0], -1, WD)
    half = WROT // 2
    return np.concatenate([w[:, :, 0:half], w[:, :, WROT:WROT + 24], w[:, :, half:WROT], w[:, :, WROT + 24:]],
                          axis=2).reshape(w.shape[0], -1)


def _columns(v):
    v = v.reshape(v.shape[:-1] + (-1, P))
    return np.ascontiguousarray(np.moveaxis(v, -1, 0))


def kernel(**inputs):
    import concourse.bacc as bacc
    from concourse.bass_utils import run_bass_kernel_spmd

    i = {k: np.asarray(v) for k, v in inputs.items()}
    q_cols = WH * WD
    w_in = i["mla_w_in"][0]
    rope_in = w_in[:, QRANK + KVRANK:]
    w_q = i["mla_w_q_b"][0].reshape(QC, P, HEADS // 2, 2, NOPE + ROT)
    w_kv = i["mla_w_kv_b"][0].reshape(KVC, P, HEADS // 2, 2 * (NOPE + VDIM))
    w_qkv, b_qkv = i["swa_w_qkv"][0], i["swa_b_qkv"]
    k_end = q_cols + WKV * WD
    inv = np.zeros((P, 8), np.float32)
    for p in range(P):
        r = p % 32
        if r < WROT // 2:
            inv[p, 0] = np.float32(THETA) ** np.float32(-2 * r / WROT)
        inv[p, 1] = np.float32(THETA) ** np.float32(-2 * r / ROT)
        inv[p, 5] = 1.0 if (p // 32) % 2 == 0 else -1.0
    inv[:, 2], inv[:, 3], inv[:, 4] = np.pi / 2, LN_EPS, RMS_EPS
    arrays = {
        "x": np.ascontiguousarray(i["x"][0].T.reshape(KC, P, SEQ).transpose(1, 0, 2)),
        "cond": _columns(i["c"][0]),
        "pos": np.ascontiguousarray(i["positions"][0]),
        "ada_w": i["ada_w"],
        "ada_b": _columns(i["ada_b"].reshape(DEPTH, 6, D)),
        "ln_gb": _columns(np.stack([np.stack([i["ln_mix_g"], i["ln_ffn_g"]], 1), np.stack([i["ln_mix_b"], i["ln_ffn_b"]], 1)],
                                   2).reshape(4, 2, D)),
        "lat_g": np.concatenate([_columns(i["mla_kv_norm"][0]), _columns(i["mla_q_norm"][0])], 1),
        "qk_b": np.concatenate([_columns(_rotary_order(b_qkv[:, q_cols:k_end])[0]),
                                _columns(_rotary_order(b_qkv[:, :q_cols])[0])], 1),
        "v_b": np.ascontiguousarray(b_qkv[0, k_end:]),
        "wo_b": _columns(i["swa_b_o"][0]),
        "sinks": np.ascontiguousarray(i["swa_sinks"][0]),
        "freq": inv,
        "w_lat": _tiles(np.concatenate([rope_in, rope_in, w_in[:, QRANK:QRANK + KVRANK], w_in[:, :QRANK]], 1)),
        "w_qr": np.ascontiguousarray(w_q[..., NOPE:].transpose(2, 1, 0, 3, 4)).reshape(HEADS // 2, P, -1),
        "w_qn": np.ascontiguousarray(w_q[..., :NOPE].transpose(2, 1, 0, 3, 4)).reshape(HEADS // 2, P, -1),
        "w_kv": np.ascontiguousarray(w_kv.transpose(2, 1, 0, 3)).reshape(HEADS // 2, P, -1),
        "w_qkv": np.concatenate([_tiles(_rotary_order(w_qkv[:, q_cols:k_end])), _tiles(w_qkv[:, k_end:]),
                                 _tiles(_rotary_order(w_qkv[:, :q_cols]))], 0),
        "w_o": np.stack([_tiles(i["mla_w_o"][0]), _tiles(i["swa_w_o"][0])]),
        "w_gt": np.stack([_tiles(w) for w in i["ffn_w_gate"]]),
        "w_up": np.stack([_tiles(w) for w in i["ffn_w_up"]]),
        "w_dn": i["ffn_w_down"].reshape(DEPTH, FC, P, D),
    }
    nc = bacc.Bacc("TRN2", target_bir_lowering=False, num_devices=1)
    A = {k: nc.dram_tensor("in_" + k, a.shape, I32 if k == "pos" else F32, kind="ExternalInput").ap() for k, a in arrays.items()}
    A["out"] = nc.dram_tensor("out", (P, KC, SEQ), F32, kind="ExternalOutput").ap()
    build(nc, A)
    got = run_bass_kernel_spmd(nc, [{"in_" + k: a for k, a in arrays.items()}], core_ids=[0]).results[0]["out"]
    return np.ascontiguousarray(got.transpose(2, 1, 0)).reshape(1, SEQ, D)
```
